# Optimizing a Trainium2 kernel written in Bass

```python
import jax, jax.numpy as jnp
from jax import lax
import numpy as np

D_MODEL = 1024
BATCH = 1
SEQ = 512
DEPTH = 1

CTX_LEN = 256
GRID_W = 64
HEAD_DIM = 128
N_Q_HEADS = D_MODEL // HEAD_DIM
N_KV_HEADS = N_Q_HEADS // 4
GQA_GROUP = N_Q_HEADS // N_KV_HEADS
ROPE_AXIS_DIM = HEAD_DIM // 2
ROPE_THETA = 10000.0
Q_BLOCK = 128
CONV_DIM = D_MODEL
CONV_WIDTH = 31
PEER_HEADS = 8
PEER_N_KEYS = 128
PEER_EXPERTS = PEER_N_KEYS * PEER_N_KEYS
PEER_TOPK = 16
PEER_KEY_DIM = 256
PEER_HALF = PEER_KEY_DIM // 2
PEER_CHUNK = 128
N_MOD = 6
EPS = 1e-6
Q_W = N_Q_HEADS * HEAD_DIM
KV_W = N_KV_HEADS * HEAD_DIM
IN_SPLITS = (Q_W, Q_W + KV_W, Q_W + 2 * KV_W, Q_W + 2 * KV_W + 2 * CONV_DIM, Q_W + 2 * KV_W + 2 * CONV_DIM + D_MODEL)
IN_W = IN_SPLITS[-1] + D_MODEL


def rmsnorm(x, g):
    xf = x.astype(jnp.float32)
    y = xf * lax.rsqrt(jnp.mean(xf * xf, axis=-1, keepdims=True) + EPS)
    return (y * g.astype(jnp.float32)).astype(x.dtype)

def layernorm(x, g, b):
    xf = x.astype(jnp.float32)
    mu = jnp.mean(xf, axis=-1, keepdims=True)
    var = jnp.mean(jnp.square(xf - mu), axis=-1, keepdims=True)
    y = (xf - mu) * lax.rsqrt(var + EPS) * g.astype(jnp.float32) + b.astype(jnp.float32)
    return y.astype(x.dtype)

def modulate(h, shift, scale):
    return h * (1 + scale) + shift

def axial_rope_tables(n_tokens, dtype):
    rows = n_tokens // GRID_W
    row = jnp.repeat(jnp.arange(rows, dtype=jnp.float32), GRID_W)
    col = jnp.tile(jnp.arange(GRID_W, dtype=jnp.float32), rows)
    inv = ROPE_THETA ** (-jnp.arange(0, ROPE_AXIS_DIM, 2, dtype=jnp.float32) / ROPE_AXIS_DIM)
    ang_r = row[:, None] * inv
    ang_c = col[:, None] * inv
    return (jnp.cos(ang_r)[:, None, :].astype(dtype), jnp.sin(ang_r)[:, None, :].astype(dtype),
            jnp.cos(ang_c)[:, None, :].astype(dtype), jnp.sin(ang_c)[:, None, :].astype(dtype))

def rotate(xa, cos, sin):
    x1, x2 = jnp.split(xa, 2, axis=-1)
    return jnp.concatenate([x1 * cos - x2 * sin, x1 * sin + x2 * cos], axis=-1)

def apply_rope(x, rope):
    cos_r, sin_r, cos_c, sin_c = rope
    xr, xc = jnp.split(x, 2, axis=-1)
    return jnp.concatenate([rotate(xr, cos_r, sin_r), rotate(xc, cos_c, sin_c)], axis=-1)

def attend(q, k, v):
    B, T = q.shape[0], q.shape[1]
    nb = T // Q_BLOCK
    scale = HEAD_DIM ** -0.5
    qb = q.reshape(B, nb, Q_BLOCK, N_KV_HEADS, GQA_GROUP, HEAD_DIM).transpose(1, 0, 2, 3, 4, 5)

    def block(qi):
        s = jnp.einsum('bqkgd,bskd->bkgqs', qi, k).astype(jnp.float32) * scale
        p = jax.nn.softmax(s, axis=-1).astype(v.dtype)
        return jnp.einsum('bkgqs,bskd->bqkgd', p, v)

    o = lax.map(block, qb)
    return o.transpose(1, 0, 2, 3, 4, 5).reshape(B, T, Q_W)

def conformer_conv(u, lw):
    a, b = jnp.split(u, 2, axis=-1)
    g = a * jax.nn.sigmoid(b)
    pad = CONV_WIDTH // 2
    g = lax.conv_general_dilated(g, lw['conv_dw'][:, None, :], window_strides=(1,), padding=[(pad, pad)],
                                 dimension_numbers=('NWC', 'WIO', 'NWC'), feature_group_count=CONV_DIM)
    g = layernorm(g + lw['conv_b'], lw['conv_ln_g'], lw['conv_ln_b'])
    return jax.nn.silu(g) @ lw['w_conv_o']

def context_kv(h, lw):
    B, T, _ = h.shape
    kv = h @ lw['w_in'][:, Q_W:Q_W + 2 * KV_W]
    k, v = jnp.split(kv, 2, axis=-1)
    k = rmsnorm(k.reshape(B, T, N_KV_HEADS, HEAD_DIM), lw['k_norm_g'])
    return k, v.reshape(B, T, N_KV_HEADS, HEAD_DIM)

def token_mixer(h, lw, rope, k_ctx, v_ctx):
    B, T, _ = h.shape
    q, k, v, u, ga, gc = jnp.split(h @ lw['w_in'], IN_SPLITS, axis=-1)
    q = rmsnorm(q.reshape(B, T, N_Q_HEADS, HEAD_DIM), lw['q_norm_g'])
    k = rmsnorm(k.reshape(B, T, N_KV_HEADS, HEAD_DIM), lw['k_norm_g'])
    v = v.reshape(B, T, N_KV_HEADS, HEAD_DIM)
    if rope is not None:
        q = apply_rope(q, rope)
        k = jnp.concatenate([apply_rope(k, rope), k_ctx], axis=1)
        v = jnp.concatenate([v, v_ctx], axis=1)
    y_att = attend(q, k, v) @ lw['w_attn_o']
    y_conv = conformer_conv(u, lw)
    merged = jax.nn.sigmoid(ga) * y_att + jax.nn.sigmoid(gc) * y_conv
    return merged @ lw['w_out']

def peer_ffn(h, lw):
    B, T, D = h.shape
    wq, keys, u_tab, v_tab = lw['peer_wq'], lw['peer_keys'], lw['peer_u'], lw['peer_v']

    def chunk(xc):
        q = (xc @ wq).reshape(PEER_CHUNK, PEER_HEADS, 2, PEER_HALF)
        s = jnp.einsum('thpd,hpnd->thpn', q, keys)
        s_top, i_top = lax.top_k(s, PEER_TOPK)
        n_cand = PEER_TOPK * PEER_TOPK
        cand_s = (s_top[:, :, 0, :, None] + s_top[:, :, 1, None, :]).reshape(PEER_CHUNK, PEER_HEADS, n_cand)
        cand_i = (i_top[:, :, 0, :, None] * PEER_N_KEYS + i_top[:, :, 1, None, :]).reshape(PEER_CHUNK, PEER_HEADS, n_cand)
        best_s, best_pos = lax.top_k(cand_s, PEER_TOPK)
        eid = jnp.take_along_axis(cand_i, best_pos, axis=-1)
        w = jax.nn.softmax(best_s.astype(jnp.float32), axis=-1).astype(xc.dtype)
        act = jax.nn.gelu(jnp.einsum('thkd,td->thk', jnp.take(u_tab, eid, axis=0), xc), approximate=False)
        return jnp.einsum('thk,thkd->td', w * act, jnp.take(v_tab, eid, axis=0))

    y = lax.map(chunk, h.reshape(-1, PEER_CHUNK, D))
    return y.reshape(B, T, D)

def first_inputs(seed: int = 0) -> dict:
    key = jax.random.key(seed)
    ks = jax.random.split(key, 24)
    L, D = DEPTH, D_MODEL

    def nrm(k, shape, scale):
        return jax.random.normal(k, shape, jnp.float32) * scale

    return {
        'x': nrm(ks[0], (BATCH, SEQ, D), 1.0),
        'c': nrm(ks[1], (BATCH, D), 1.0),
        'ctx': nrm(ks[2], (BATCH, CTX_LEN, D), 1.0),
        'c_ctx': nrm(ks[3], (D,), 1.0),
        'w_mod': nrm(ks[4], (L, D, N_MOD * D), 0.5 * D ** -0.5),
        'b_mod': nrm(ks[5], (L, N_MOD * D), 0.01),
        'norm1_g': 1.0 + nrm(ks[6], (L, D), 0.1),
        'norm2_g': 1.0 + nrm(ks[7], (L, D), 0.1),
        'w_in': nrm(ks[8], (L, D, IN_W), D ** -0.5),
        'q_norm_g': 1.0 + nrm(ks[9], (L, HEAD_DIM), 0.1),
        'k_norm_g': 1.0 + nrm(ks[10], (L, HEAD_DIM), 0.1),
        'w_attn_o': nrm(ks[11], (L, Q_W, D), Q_W ** -0.5),
        'conv_dw': nrm(ks[12], (L, CONV_WIDTH, CONV_DIM), CONV_WIDTH ** -0.5),
        'conv_b': nrm(ks[13], (L, CONV_DIM), 0.01),
        'conv_ln_g': 1.0 + nrm(ks[14], (L, CONV_DIM), 0.1),
        'conv_ln_b': nrm(ks[15], (L, CONV_DIM), 0.01),
        'w_conv_o': nrm(ks[16], (L, CONV_DIM, D), CONV_DIM ** -0.5),
        'w_out': nrm(ks[17], (L, D, D), D ** -0.5),
        'peer_wq': nrm(ks[18], (L, D, PEER_HEADS * PEER_KEY_DIM), D ** -0.5),
        'peer_keys': nrm(ks[19], (L, PEER_HEADS, 2, PEER_N_KEYS, PEER_HALF), PEER_HALF ** -0.5),
        'peer_u': nrm(ks[20], (L, PEER_EXPERTS, D), D ** -0.5),
        'peer_v': nrm(ks[21], (L, PEER_EXPERTS, D), 0.5),
        'final_norm_g': 1.0 + nrm(ks[22], (D,), 0.1),
    }

def first_block(x, c, ctx, c_ctx, w_mod, b_mod, norm1_g, norm2_g, w_in, q_norm_g, k_norm_g,
              w_attn_o, conv_dw, conv_b, conv_ln_g, conv_ln_b, w_conv_o, w_out,
              peer_wq, peer_keys, peer_u, peer_v, final_norm_g):
    S = x.shape[1]
    rope = axial_rope_tables(S, x.dtype)
    xs, cs = x, ctx
    for l in range(DEPTH):
        lw = {'w_in': w_in[l], 'q_norm_g': q_norm_g[l], 'k_norm_g': k_norm_g[l], 'w_attn_o': w_attn_o[l],
              'conv_dw': conv_dw[l], 'conv_b': conv_b[l], 'conv_ln_g': conv_ln_g[l], 'conv_ln_b': conv_ln_b[l],
              'w_conv_o': w_conv_o[l], 'w_out': w_out[l], 'peer_wq': peer_wq[l], 'peer_keys': peer_keys[l],
              'peer_u': peer_u[l], 'peer_v': peer_v[l]}
        last = l == DEPTH - 1
        sh1, sc1, g1, sh2, sc2, g2 = [m[:, None, :] for m in
                                      jnp.split(jax.nn.silu(c) @ w_mod[l] + b_mod[l], N_MOD, axis=-1)]
        csh1, csc1, cg1, csh2, csc2, cg2 = jnp.split(jax.nn.silu(c_ctx) @ w_mod[l] + b_mod[l], N_MOD, axis=-1)
        hc = modulate(rmsnorm(cs, norm1_g[l]), csh1, csc1)
        k_c, v_c = context_kv(hc, lw)
        hx = modulate(rmsnorm(xs, norm1_g[l]), sh1, sc1)
        xs = xs + g1 * token_mixer(hx, lw, rope, k_c, v_c)
        if not last:
            cs = cs + cg1 * token_mixer(hc, lw, None, None, None)
        hx = modulate(rmsnorm(xs, norm2_g[l]), sh2, sc2)
        xs = xs + g2 * peer_ffn(hx, lw)
        if not last:
            hc = modulate(rmsnorm(cs, norm2_g[l]), csh2, csc2)
            cs = cs + cg2 * peer_ffn(hc, lw)
    return rmsnorm(xs, final_norm_g)


DEPTH_2 = 2

CHUNK = 64
CONV_CH = 512
CONV_WIDTH_2 = 3
GLA_HEADS = 4
GLA_DK = 64
GLA_DV = 128
GLA_KW = GLA_HEADS * GLA_DK
GLA_VW = GLA_HEADS * GLA_DV
GATE_RANK = 16
GATE_NORMALIZER = 16.0
GATE_LOG_MIN = -1.0
MIX_WIDTH = CONV_CH + GLA_VW
IN_WIDTH = 3 * CONV_CH + 2 * GLA_KW + 2 * GLA_VW + GATE_RANK
IN_SPLITS_2 = (
    CONV_CH,
    2 * CONV_CH,
    3 * CONV_CH,
    3 * CONV_CH + GLA_KW,
    3 * CONV_CH + 2 * GLA_KW,
    3 * CONV_CH + 2 * GLA_KW + GLA_VW,
    3 * CONV_CH + 2 * GLA_KW + 2 * GLA_VW,
)
D_FF = 2816
N_EXPERTS = 8
TOP_K = 2
D_FF_EXPERT = 2816
N_DENSE = (DEPTH_2 + 1) // 2
N_MOE = DEPTH_2 // 2
DEEPNORM_ALPHA = (2.0 * DEPTH_2) ** 0.25
DEEPNORM_BETA = (8.0 * DEPTH_2) ** -0.25
LN_EPS = 1e-5
RMS_EPS = 1e-6


def _layernorm(x, g, b):
    xf = x.astype(jnp.float32)
    mu = jnp.mean(xf, axis=-1, keepdims=True)
    var = jnp.mean(jnp.square(xf - mu), axis=-1, keepdims=True)
    return ((xf - mu) * lax.rsqrt(var + LN_EPS) * g.astype(jnp.float32)
            + b.astype(jnp.float32)).astype(x.dtype)

def _causal_depthwise_conv(z, w):
    return lax.conv_general_dilated(
        z, w[:, None, :].astype(z.dtype), window_strides=(1,),
        padding=[(CONV_WIDTH_2 - 1, 0)],
        dimension_numbers=("NWC", "WIO", "NWC"),
        feature_group_count=z.shape[-1])

def _gla_chunked(q, k, v, gk):
    bsz, seq = q.shape[0], q.shape[1]
    n_chunks = seq // CHUNK
    shp_k = (bsz, n_chunks, CHUNK, GLA_HEADS, GLA_DK)
    shp_v = (bsz, n_chunks, CHUNK, GLA_HEADS, GLA_DV)
    q = q.astype(jnp.float32).reshape(shp_k) * (GLA_DK ** -0.5)
    k = k.astype(jnp.float32).reshape(shp_k)
    v = v.astype(jnp.float32).reshape(shp_v)
    b = jnp.cumsum(gk.astype(jnp.float32).reshape(shp_k), axis=2)
    b_last = b[:, :, -1:]
    q_in = q * jnp.exp(b)
    k_in = k * jnp.exp(-b)
    k_out = k * jnp.exp(b_last - b)
    causal = jnp.tril(jnp.ones((CHUNK, CHUNK), dtype=bool))
    scores = jnp.einsum("bnihd,bnjhd->bnhij", q_in, k_in)
    scores = jnp.where(causal, scores, 0.0)
    o_intra = jnp.einsum("bnhij,bnjhv->bnihv", scores, v)
    kv_chunk = jnp.einsum("bnjhd,bnjhv->bnhdv", k_out, v)
    decay_chunk = jnp.exp(b_last[:, :, 0])

    def step(state, inp):
        kv_n, dec_n = inp
        return dec_n[..., None] * state + kv_n, state

    init = jnp.zeros((bsz, GLA_HEADS, GLA_DK, GLA_DV), jnp.float32)
    _, states = lax.scan(step, init, (jnp.swapaxes(kv_chunk, 0, 1), jnp.swapaxes(decay_chunk, 0, 1)))
    states = jnp.swapaxes(states, 0, 1)
    o_inter = jnp.einsum("bnihd,bnhdv->bnihv", q_in, states)
    return (o_intra + o_inter).reshape(bsz, seq, GLA_HEADS, GLA_DV)

def _mixer(u, w_in, conv_w, gk_w2, gk_b, gla_norm_w, w_out):
    bsz, seq, _ = u.shape
    proj = jnp.einsum("bsd,de->bse", u, w_in)
    c_b, c_c, c_h, q, k, v, g, g_low = jnp.split(proj, IN_SPLITS_2, axis=-1)
    y_conv = c_b * _causal_depthwise_conv(c_c * c_h, conv_w)
    gk = jax.nn.log_sigmoid((jnp.einsum("bsr,rk->bsk", g_low, gk_w2) + gk_b).astype(jnp.float32))
    gk = jnp.maximum(gk / GATE_NORMALIZER, GATE_LOG_MIN)
    o = _gla_chunked(q.reshape(bsz, seq, GLA_HEADS, GLA_DK),
                     k.reshape(bsz, seq, GLA_HEADS, GLA_DK),
                     v.reshape(bsz, seq, GLA_HEADS, GLA_DV),
                     gk.reshape(bsz, seq, GLA_HEADS, GLA_DK))
    o = o * lax.rsqrt(jnp.mean(jnp.square(o), axis=-1, keepdims=True) + RMS_EPS)
    o = o * gla_norm_w.astype(jnp.float32) * jax.nn.silu(
        g.astype(jnp.float32).reshape(bsz, seq, GLA_HEADS, GLA_DV))
    y_gla = o.reshape(bsz, seq, GLA_VW).astype(u.dtype)
    y = jnp.concatenate([y_conv, y_gla], axis=-1)
    return jnp.einsum("bse,ed->bsd", y, w_out)

def _dense_swiglu(u, w_gate, w_up, w_down):
    h = jax.nn.silu(jnp.einsum("bsd,df->bsf", u, w_gate)) * jnp.einsum("bsd,df->bsf", u, w_up)
    return jnp.einsum("bsf,fd->bsd", h, w_down)

def _moe_swiglu(u, w_router, w_gate, w_up, w_down):
    bsz, seq, dm = u.shape
    n_tok = bsz * seq
    xt = u.reshape(n_tok, dm)
    logits = jnp.dot(xt, w_router).astype(jnp.float32)
    top_logits, top_idx = lax.top_k(logits, TOP_K)
    top_w = jax.nn.softmax(top_logits, axis=-1).astype(u.dtype)
    flat_e = top_idx.reshape(-1)
    order = jnp.argsort(flat_e)
    tok = order // TOP_K
    group_sizes = jnp.bincount(flat_e, length=N_EXPERTS).astype(jnp.int32)
    xs = xt[tok]
    h = jax.nn.silu(lax.ragged_dot(xs, w_gate, group_sizes)) * lax.ragged_dot(xs, w_up, group_sizes)
    ys = lax.ragged_dot(h, w_down, group_sizes) * top_w.reshape(-1)[order][:, None]
    out = jax.ops.segment_sum(ys, tok, num_segments=n_tok)
    return out.reshape(bsz, seq, dm)

def second_inputs(seed: int = 0) -> dict:
    key = jax.random.key(seed)
    ks = jax.random.split(key, 24)
    nrm = jax.random.normal
    f32 = jnp.float32
    x = nrm(ks[0], (BATCH, SEQ, D_MODEL), f32)
    c = nrm(ks[1], (BATCH, D_MODEL), f32)
    ada_w = nrm(ks[2], (DEPTH_2, D_MODEL, 6 * D_MODEL), f32) * (0.1 * D_MODEL ** -0.5)
    ada_b = nrm(ks[3], (DEPTH_2, 6 * D_MODEL), f32) * 0.02
    w_in = nrm(ks[4], (DEPTH_2, D_MODEL, IN_WIDTH), f32) * D_MODEL ** -0.5
    conv_w = nrm(ks[5], (DEPTH_2, CONV_WIDTH_2, CONV_CH), f32) * CONV_WIDTH_2 ** -0.5
    gk_w2 = nrm(ks[6], (DEPTH_2, GATE_RANK, GLA_KW), f32) * GATE_RANK ** -0.5
    gk_b = nrm(ks[7], (DEPTH_2, GLA_KW), f32) * 0.02
    gla_norm_w = 1.0 + 0.02 * nrm(ks[8], (DEPTH_2, GLA_DV), f32)
    w_out = nrm(ks[9], (DEPTH_2, MIX_WIDTH, D_MODEL), f32) * (DEEPNORM_BETA * MIX_WIDTH ** -0.5)
    ln1_g = 1.0 + 0.02 * nrm(ks[10], (DEPTH_2, D_MODEL), f32)
    ln1_b = 0.02 * nrm(ks[11], (DEPTH_2, D_MODEL), f32)
    ln2_g = 1.0 + 0.02 * nrm(ks[12], (DEPTH_2, D_MODEL), f32)
    ln2_b = 0.02 * nrm(ks[13], (DEPTH_2, D_MODEL), f32)
    ffn_w_gate = nrm(ks[14], (N_DENSE, D_MODEL, D_FF), f32) * D_MODEL ** -0.5
    ffn_w_up = nrm(ks[15], (N_DENSE, D_MODEL, D_FF), f32) * D_MODEL ** -0.5
    ffn_w_down = nrm(ks[16], (N_DENSE, D_FF, D_MODEL), f32) * (DEEPNORM_BETA * D_FF ** -0.5)
    router_w = nrm(ks[17], (N_MOE, D_MODEL, N_EXPERTS), f32) * D_MODEL ** -0.5
    moe_w_gate = nrm(ks[18], (N_MOE, N_EXPERTS, D_MODEL, D_FF_EXPERT), f32) * D_MODEL ** -0.5
    moe_w_up = nrm(ks[19], (N_MOE, N_EXPERTS, D_MODEL, D_FF_EXPERT), f32) * D_MODEL ** -0.5
    moe_w_down = nrm(ks[20], (N_MOE, N_EXPERTS, D_FF_EXPERT, D_MODEL), f32) * (DEEPNORM_BETA * D_FF_EXPERT ** -0.5)
    return {"x": x, "c": c, "ada_w": ada_w, "ada_b": ada_b, "w_in": w_in, "conv_w": conv_w,
            "gk_w2": gk_w2, "gk_b": gk_b, "gla_norm_w": gla_norm_w, "w_out": w_out,
            "ln1_g": ln1_g, "ln1_b": ln1_b, "ln2_g": ln2_g, "ln2_b": ln2_b,
            "ffn_w_gate": ffn_w_gate, "ffn_w_up": ffn_w_up, "ffn_w_down": ffn_w_down,
            "router_w": router_w, "moe_w_gate": moe_w_gate, "moe_w_up": moe_w_up,
            "moe_w_down": moe_w_down}

def second_block(x, c, ada_w, ada_b, w_in, conv_w, gk_w2, gk_b, gla_norm_w, w_out,
              ln1_g, ln1_b, ln2_g, ln2_b, ffn_w_gate, ffn_w_up, ffn_w_down,
              router_w, moe_w_gate, moe_w_up, moe_w_down):
    cond = jax.nn.silu(c)
    for layer in range(DEPTH_2):
        mod = (jnp.dot(cond, ada_w[layer]) + ada_b[layer])[:, None, :]
        sh1, sc1, g1, sh2, sc2, g2 = jnp.split(mod, 6, axis=-1)
        u = x * (1.0 + sc1) + sh1
        mix = _mixer(u, w_in[layer], conv_w[layer], gk_w2[layer], gk_b[layer],
                     gla_norm_w[layer], w_out[layer])
        x = _layernorm(DEEPNORM_ALPHA * x + (1.0 + g1) * mix, ln1_g[layer], ln1_b[layer])
        u = x * (1.0 + sc2) + sh2
        j = layer // 2
        if layer % 2 == 0:
            ff = _dense_swiglu(u, ffn_w_gate[j], ffn_w_up[j], ffn_w_down[j])
        else:
            ff = _moe_swiglu(u, router_w[j], moe_w_gate[j], moe_w_up[j], moe_w_down[j])
        x = _layernorm(DEEPNORM_ALPHA * x + (1.0 + g2) * ff, ln2_g[layer], ln2_b[layer])
    return x


def setup_inputs(seed=0):
    out = dict(first_inputs(seed))
    for name, value in second_inputs(seed + 1).items():
        if name != "x":
            out[name + "_2"] = value
    return out


def reference(
    x, c, ctx, c_ctx, w_mod, b_mod, norm1_g, norm2_g, w_in, q_norm_g, k_norm_g, w_attn_o,
    conv_dw, conv_b, conv_ln_g, conv_ln_b, w_conv_o, w_out, peer_wq, peer_keys, peer_u, peer_v,
    final_norm_g, c_2, ada_w_2, ada_b_2, w_in_2, conv_w_2, gk_w2_2, gk_b_2, gla_norm_w_2,
    w_out_2, ln1_g_2, ln1_b_2, ln2_g_2, ln2_b_2, ffn_w_gate_2, ffn_w_up_2, ffn_w_down_2,
    router_w_2, moe_w_gate_2, moe_w_up_2, moe_w_down_2,
):
    x = first_block(
        x, c, ctx, c_ctx, w_mod, b_mod, norm1_g, norm2_g, w_in, q_norm_g, k_norm_g, w_attn_o,
        conv_dw, conv_b, conv_ln_g, conv_ln_b, w_conv_o, w_out, peer_wq, peer_keys, peer_u,
        peer_v, final_norm_g,
    )
    return second_block(
        x, c_2, ada_w_2, ada_b_2, w_in_2, conv_w_2, gk_w2_2, gk_b_2, gla_norm_w_2, w_out_2,
        ln1_g_2, ln1_b_2, ln2_g_2, ln2_b_2, ffn_w_gate_2, ffn_w_up_2, ffn_w_down_2, router_w_2,
        moe_w_gate_2, moe_w_up_2, moe_w_down_2,
    )


_drawn_inputs = setup_inputs


def setup_inputs(seed=0):
    import zlib

    import numpy as np

    out = dict(_drawn_inputs(seed))
    spreads = {}
    factors = {'ctx': 3.351,
     'b_mod': 2.731,
     'q_norm_g': 8.0,
     'k_norm_g': 8.0,
     'conv_b': 7.305,
     'conv_ln_b': 8.0,
     'gk_b_2': 8.0,
     'gla_norm_w_2': 8.0}
    for name, (base, spread) in spreads.items():
        noise = np.random.default_rng([zlib.crc32(name.encode()), seed]).standard_normal(out[name].shape)
        drawn = base * np.exp(spread * noise) if base else spread * noise
        out[name] = __import__('jax').numpy.asarray(drawn.astype(out[name].dtype))
    for name, factor in factors.items():
        out[name] = (out[name] * factor).astype(out[name].dtype)
    return out
```

```python
from contextlib import ExitStack, contextmanager

import numpy as np

import concourse.bass as bass
from concourse import mybir

F32 = mybir.dt.float32
U32 = mybir.dt.uint32
I32 = mybir.dt.int32
ACT = mybir.ActivationFunctionType
ALU = mybir.AluOpType
AX = mybir.AxisListType
ds = bass.ds

P = 128
D = 1024
KT = D // P
T = 512
TT = T // P
CTX = 256
SKV = T + CTX
ST = SKV // P
HEADS, KV_HEADS = 8, 2
GROUP = HEADS // KV_HEADS
NMOD = 6 * KT
TAPS = 31
PAD = TAPS // 2
PH, PTOP, PKEYS = 8, 16, 128
NCAND = PTOP * PTOP
PSEL = PH * PTOP
GH, GDK, GDV, GCH = 4, 64, 128, 64
NCH = T // GCH
CONV2 = 4
TAPS2 = 3
FF = 2816
FT = FF // P
NE = 8
EPS, LN_EPS = 1e-6, 1e-5
ALPHA = 4.0 ** 0.25
SLOTS = 4
TOP2 = 2
BLOCKS = (TOP2 * T) // P + NE - 1
FC = 2 * P
STEPS = FF // FC
HALF_FT = FT // 2
LOW = -3.0e38

W_IN_ORDER = [8, 9, 10, 11] + [t for c in range(8) for t in (20 + c, 12 + c)] + list(range(8)) + list(range(28, 44))
W_IN2_ORDER = [t for c in range(4) for t in (4 + c, 8 + c)] + list(range(4)) + list(range(12, 24))
MOE_ORDER = [(0, 0), (1, 0)] + [x for c in range(1, STEPS) for x in ((0, c), (1, c), (2, c - 1))] + [(2, STEPS - 1)]
MOE_SLABS = len(MOE_ORDER)
MOE_SLOTS = STEPS

VECTORS = {}


def _vector_columns():
    at = 0
    for name, width in (
        ("b_mod", NMOD), ("norm1", KT), ("norm2", KT), ("final", KT), ("qk_gain", HEADS + KV_HEADS),
        ("k_gain", 1), ("conv_w", KT * TAPS), ("conv_b", KT), ("cln_g", KT), ("cln_b", KT),
        ("ada_b", 2 * NMOD), ("ln1_g", 2 * KT), ("ln1_b", 2 * KT), ("ln2_g", 2 * KT), ("ln2_b", 2 * KT),
        ("gk_b", 2 * 2), ("gla_g", 2), ("conv2_w", 2 * CONV2 * TAPS2),
    ):
        VECTORS[name] = (at, width)
        at += width
    return at


NVEC = _vector_columns()

CONSTS = {}


def _const_columns():
    at = 0
    for name, width in (("ident", P), ("ones", P), ("perm", P), ("causal", P), ("before", P),
                        ("pair", 2 * P), ("iota", P), ("cos", T), ("sin", T), ("carry", T), ("half", 2)):
        CONSTS[name] = (at, width)
        at += width
    return at


NCONST = _const_columns()


class Signal:

    def __init__(self, sem):
        self.sem, self.base = sem, 0

    def at(self, n):
        return self.base + n

    def close(self, n):
        self.base += n


@contextmanager
def repeat(eng, n):
    if n == 1:
        yield 0
    else:
        with eng.Fori(0, n) as i:
            yield i


class Program:
    def __init__(self, nc, d, stop=None):
        self.nc, self.d, self.stop = nc, d, stop
        self.ctx = ExitStack()
        self.signals = {}
        self.issued = 0
        self.used = 0

    def sb(self, name, shape, dt=F32, scope=None):
        return (scope or self.ctx).enter_context(self.nc.sbuf_tensor(name, shape, dt))

    def ps(self, name, shape, dt=F32):
        return self.ctx.enter_context(self.nc.psum_tensor(name, shape, dt))

    def sig(self, name):
        if name not in self.signals:
            self.signals[name] = Signal(self.ctx.enter_context(self.nc.semaphore(name)))
        return self.signals[name]

    def vec(self, name, i=0, n=1):
        at, _ = VECTORS[name]
        return self.vectors[:, ds(at + i, n)]

    def const(self, name, rows=P, a=0, b=None):
        at, w = CONSTS[name]
        return self.consts[0:rows, at + a:at + (w if b is None else b)]

    def issue(self, sp, upto):
        upto = min(upto, sum(ap.shape[0] for ap in self.stream))
        while self.issued < upto:
            at = 0
            for ap in self.stream:
                if self.issued < at + ap.shape[0]:
                    break
                at += ap.shape[0]
            n = min(upto, at + ap.shape[0]) - self.issued
            first, index = self.issued, self.issued - at
            width = ap.shape[2]

            def group(turn):
                for j in range(SLOTS):
                    free = first + SLOTS * turn + j - SLOTS + 1
                    if not (isinstance(free, int) and free <= 0):
                        sp.wait_ge(self.slab_used, free)
                    sp.dma_start(self.ring[j][:, 0:width], ap[ds(index + SLOTS * turn + j, 1)].rearrange("a p n -> (a p) n")
                                 ).then_inc(self.landed[j], 16)

            turns = n // SLOTS
            assert turns * SLOTS == n
            done = 0
            if first == 0:
                group(0)
                done = 1
            if turns - done > 1:
                with sp.Fori(done, turns) as turn:
                    group(turn)
            elif turns - done == 1:
                group(done)
            self.issued += n

    def slabs(self, pe, first, n, product, every=1):
        first += self.used

        def group(turn):
            for j in range(SLOTS):
                pe.wait_ge(self.landed[j], 16 * (first // SLOTS + 1) + 16 * turn)
                taken = first + SLOTS * turn + j - SLOTS + 1
                if not (isinstance(taken, int) and taken <= 0):
                    pe.wait_ge(self.taken, taken)
                product(j, SLOTS * turn + j).then_inc(self.slab_used, 1)

        turns = n // SLOTS
        assert first % SLOTS == 0 and turns * SLOTS == n
        done = 0
        if first == 0:
            group(0)
            done = 1
        if turns - done > 1:
            with pe.Fori(done, turns) as turn:
                group(turn)
        elif turns - done == 1:
            group(done)

    def take(self, eng, first, n, out_of_bank, width=SLOTS):
        first += self.used
        with repeat(eng, n // width) as turn:
            for j in range(width):
                eng.wait_ge(self.slab_used, first + width * turn + j + 1)
                out_of_bank(self.bank[:, (first + j) % SLOTS, :], width * turn + j).then_inc(self.taken, 1)

    def wslab(self, slot, k):
        return self.ring[slot][:, k * P:(k + 1) * P]

    def linear(self, pe, src):
        def product(slot, index):
            for k in range(KT):
                mm = pe.matmul(self.bank[:, slot, :], self.wslab(slot, k), src[:, k, :], start=k == 0, stop=k == KT - 1)
            return mm
        return product

    def natural(self, pe, src, slot, out, tiles):
        for t in range(tiles):
            for k in range(KT):
                mm = pe.matmul(out[:, t * P:(t + 1) * P], src[:, k, t * P:(t + 1) * P], self.wslab(slot, k),
                               start=k == 0, stop=k == KT - 1)
        return mm

    def normalise(self, src, width, eps, outs, centre=False, also=None):
        nc, squares = self.nc, self.squares
        squared, summed, rooted, inverted = (self.sig(n) for n in ("squared", "summed", "rooted", "inverted"))
        centred, averaged, scaled, normed = (self.sig(n) for n in ("centred", "averaged", "scaled", "normed"))
        total = self.side[:, 0, 0:width]
        mean = self.side[:, 1, 0:width]
        root, inv = self.stat[:, 0, 0:width], self.stat[:, 1, 0:width]
        ones = self.const("ones")
        with nc.Block() as block:
            if also is not None:
                block.sync(also)

            @block.scalar
            def _(act):
                for k in range(KT):
                    if centre:
                        act.wait_ge(centred.sem, centred.at(k + 1))
                    act.activation(squares[:, k, 0:width], src[:, k, 0:width], ACT.Square).then_inc(squared.sem, 1)
                act.wait_ge(summed.sem, summed.at(1))
                act.activation(root, total, ACT.Sqrt, bias=self.eps[eps], scale=1.0 / D).then_inc(rooted.sem, 1)
                for k in range(KT):
                    act.wait_ge(scaled.sem, scaled.at(k + 1))
                    for n, (dst, func, scale, bias) in enumerate(outs):
                        at = squares[:, k, 0:width]
                        if n == 1:
                            act.wait_ge(normed.sem, normed.at(2 * k + 1))
                            at = outs[0][0][:, k, 0:width]
                        if bias is None:
                            act.activation(dst[:, k, 0:width], at, ACT.Copy, scale=scale(k)).then_inc(normed.sem, 1)
                        else:
                            act.activation(dst[:, k, 0:width], at, func, scale=scale(k), bias=bias(k)).then_inc(normed.sem, 1)

            @block.vector
            def _(dve):
                if centre:
                    dve.wait_ge(averaged.sem, averaged.at(1))
                    for k in range(KT):
                        dve.scalar_tensor_tensor(src[:, k, 0:width], mean, -1.0 / D, src[:, k, 0:width],
                                                            ALU.mult, ALU.add).then_inc(centred.sem, 1)
                dve.wait_ge(rooted.sem, rooted.at(1))
                dve.reciprocal(inv, root).then_inc(inverted.sem, 1)
                dve.wait_ge(inverted.sem, inverted.at(1))
                for k in range(KT):
                    dve.tensor_tensor(squares[:, k, 0:width], src[:, k, 0:width], inv, ALU.mult).then_inc(scaled.sem, 1)

            @block.tensor
            def _(pe):
                if centre:
                    for k in range(KT):
                        mm = pe.matmul(mean, ones, src[:, k, 0:width], start=k == 0, stop=k == KT - 1)
                    mm.then_inc(averaged.sem, 1)
                for k in range(KT):
                    pe.wait_ge(squared.sem, squared.at(k + 1))
                    mm = pe.matmul(total, ones, squares[:, k, 0:width], start=k == 0, stop=k == KT - 1)
                mm.then_inc(summed.sem, 1)
        squared.close(KT)
        summed.close(1)
        rooted.close(1)
        inverted.close(1)
        scaled.close(KT)
        normed.close(KT * len(outs))
        if centre:
            centred.close(KT)
            averaged.close(1)

    def prefetch(self, upto):
        return lambda sp: self.issue(sp, upto)

    def load_and_modulate(self):
        nc, d = self.nc, self.d
        loaded, ready, cooked = self.sig("loaded"), self.sig("cond_ready"), self.sig("cooked")
        with nc.Block() as block:
            @block.sync
            def _(sp):
                for dst, src in ((self.cond, d["cond"]), (self.consts, d["consts"]), (self.vectors, d["vectors"]),
                                 (self.small, d["small"])):
                    sp.dma_start(dst[:], src).then_inc(loaded.sem, 16)
                sp.dma_start(self.x[:], d["x"]).then_inc(self.sig("x_loaded").sem, 16)
                sp.dma_start(self.ctx_in[:], d["ctx"]).then_inc(self.sig("x_loaded").sem, 16)
                self.issue(sp, 3 * NMOD + SLOTS)
                sp.wait_ge(self.sig("x_loaded").sem, self.sig("x_loaded").at(32))

            @block.scalar
            def _(act):
                act.wait_ge(loaded.sem, loaded.at(64))
                act.activation(self.cond_s[:], self.cond[:], ACT.Silu).then_inc(ready.sem, 1)

            @block.tensor
            def _(pe):
                pe.wait_ge(ready.sem, ready.at(1))
                for layer, (a, b) in enumerate(((0, 2), (2, 3), (2, 3))):
                    def product(slot, index, a=a, b=b):
                        for k in range(KT):
                            mm = pe.matmul(self.bank[:, slot, 0:b - a], self.wslab(slot, k), self.cond_s[:, k, a:b],
                                           start=k == 0, stop=k == KT - 1)
                        return mm
                    self.slabs(pe, layer * NMOD, NMOD, product)

            @block.vector
            def _(dve):
                dve.wait_ge(loaded.sem, loaded.at(64))
                self.take(dve, 0, NMOD, lambda bank, i: dve.tensor_scalar(
                    self.mod[:, ds(i, 1), :].rearrange("p a c -> p (a c)"), bank[:, 0:2], self.vec("b_mod", i), None, ALU.add))
                self.take(dve, NMOD, 2 * NMOD, lambda bank, i: dve.tensor_scalar(
                    self.mod2[:, ds(i, 1)], bank[:, 0:1], self.vec("ada_b", i), None, ALU.add))
                dve.wait_ge(self.taken, 3 * NMOD)
                v = lambda name, i=0: self.vec(name, i, KT)
                one_plus = lambda out, at, gain: dve.scalar_tensor_tensor(out, at, 1.0, gain, ALU.add, ALU.mult).then_inc(cooked.sem, 1)
                one_plus(self.cooked[:, 0, :], self.mod[:, KT:2 * KT, 0], v("norm1"))
                one_plus(self.cooked[:, 1, :], self.mod[:, KT:2 * KT, 1], v("norm1"))
                one_plus(self.cooked[:, 2, :], self.mod[:, 4 * KT:5 * KT, 0], v("norm2"))
                for layer in range(2):
                    for n, at in enumerate((1, 2, 4, 5)):
                        dve.tensor_scalar(self.cooked[:, 3 + 4 * layer + n, :],
                                                    self.mod2[:, layer * NMOD + at * KT:layer * NMOD + (at + 1) * KT],
                                                    1.0, None, ALU.add).then_inc(cooked.sem, 1)
        cooked.close(11)
        self.used += 3 * NMOD

    def project(self, s):
        nc = self.nc
        free, tapped = self.sig("gate_slot_free"), self.sig("tapped")
        side_ready, side_taken = self.sig("side_ready"), self.sig("side_taken")
        base = self.used
        with nc.Block() as block:
            @block.sync
            def _(sp):
                self.issue(sp, base + 44 + SLOTS)

            @block.tensor
            def _(pe):
                def kv(slot, index):
                    side = self.side[:, slot, :]
                    if slot < 2:
                        for k in range(KT):
                            mm = pe.matmul(side[:, 0:CTX], self.wslab(slot, k), self.hc[:, k, :], start=k == 0, stop=k == KT - 1)
                        mm.then_inc(side_ready.sem, 1)
                        return self.linear(pe, self.h)(slot, index)
                    self.natural(pe, self.hc, slot, side, CTX // P).then_inc(side_ready.sem, 1)
                    return self.natural(pe, self.h, slot, self.bank[:, slot, :], TT)
                self.slabs(pe, 0, 4, kv)
                self.slabs(pe, 4, 40, self.linear(pe, self.h))

            @block.scalar
            def _(act):
                def kv(bank, i):
                    act.wait_ge(side_ready.sem, side_ready.at(i + 1))
                    if i < 2:
                        act.activation(s.kc[:, i, :], self.side[:, i, 0:CTX], ACT.Copy)
                        return act.activation(s.qk[:, HEADS + i, :], bank, ACT.Copy)
                    g = slice((i - 2) * P, (i - 1) * P)
                    act.activation(s.v[:, TT:ST, g], self.side[:, i, 0:CTX].rearrange("p (a c) -> p a c", c=P), ACT.Copy)
                    return act.activation(s.v[:, 0:TT, g], bank.rearrange("p (a c) -> p a c", c=P), ACT.Copy)
                self.take(act, 0, 4, kv)
                with act.Fori(0, KT // 2) as turn:
                    for j in range(2):
                        for half in range(2):
                            act.wait_ge(self.slab_used, base + 5 + 4 * turn + 2 * j + half)
                            n = 2 * j + half
                            if half == 0:
                                act.wait_ge(free.sem, free.at(2 * turn + j + 1))
                            act.activation(s.ab[:, n, :], self.bank[:, n, :], ACT.Sigmoid if half == 0 else ACT.Copy
                                           ).then_inc(self.taken, 1)
                self.take(act, 20, HEADS, lambda bank, i: act.activation(s.qk[:, ds(i, 1), :].rearrange("p a t -> p (a t)"), bank, ACT.Copy))
                self.take(act, 28, 16, lambda bank, i: act.activation(s.gates[:, ds(i, 1), :].rearrange("p a t -> p (a t)"), bank, ACT.Sigmoid))

            @block.vector
            def _(dve):
                dve.memset(s.gpad[:], 0.0).then_inc(free.sem, 2)
                dve.wait_ge(free.sem, free.at(2))
                with dve.Fori(0, KT // 2) as turn:
                    for j in range(2):
                        c = 2 * turn + j
                        dve.wait_ge(self.taken, base + 4 + 2 * c + 2)
                        gp = s.gpad[:, j, :]
                        dve.tensor_tensor(gp[:, PAD:PAD + T], s.ab[:, 2 * j, :], s.ab[:, 2 * j + 1, :], ALU.mult).then_inc(free.sem, 1)
                        dve.wait_ge(free.sem, free.at(c + 3))
                        out = s.conv[:, ds(c, 1), :].rearrange("p a t -> p (a t)")
                        dve.tensor_scalar(out, gp[:, 0:T], self.vec("conv_w", TAPS * c), self.vec("conv_b", c), ALU.mult, ALU.add).then_inc(tapped.sem, 1)
                        for tap in range(1, TAPS):
                            dve.wait_ge(tapped.sem, tapped.at(TAPS * c + tap))
                            dve.scalar_tensor_tensor(out, gp[:, tap:tap + T], self.vec("conv_w", TAPS * c + tap), out,
                                                               ALU.mult, ALU.add).then_inc(tapped.sem, 1)
        side_ready.close(4)
        free.close(KT + 2)
        tapped.close(TAPS * KT)
        self.used += 44

    def conv_out(self, s):
        base = self.used
        with self.nc.Block() as block:
            @block.sync
            def _(sp):
                self.issue(sp, base + KT + SLOTS)

            @block.tensor
            def _(pe):
                self.slabs(pe, 0, KT, self.linear(pe, self.h))

            @block.vector
            def _(dve):
                def gate(bank, i):
                    at = s.gates[:, ds(KT + i, 1), :].rearrange("p a t -> p (a t)")
                    return dve.tensor_tensor(at, bank, at, ALU.mult)
                self.take(dve, 0, KT, gate)
        self.used += KT

    def rotate(self, s):
        sig = self.sig
        squared, summed, rooted, inverted = sig("h_squared"), sig("h_summed"), sig("h_rooted"), sig("h_inverted")
        normed, turned, products, rotated = sig("h_normed"), sig("h_turned"), sig("h_products"), sig("h_rotated")
        units = HEADS + KV_HEADS

        def unit_src(u):
            return s.kc[:].rearrange("p a t -> p (a t)") if u is None else s.qk[:, ds(u, 1), :].rearrange("p a t -> p (a t)")

        with self.nc.Block() as block:
            @block.scalar
            def _(act):
                def unit(u, j, n):
                    act.activation(s.sq[:, j, :], unit_src(u), ACT.Square).then_inc(squared.sem, 1)
                    act.wait_ge(summed.sem, summed.at(n + 1))
                    act.activation(s.root[:, j, :], self.bank[:, j, :], ACT.Sqrt, bias=self.eps[EPS], scale=1.0 / P).then_inc(rooted.sem, 1)
                with act.Fori(0, units // 2) as turn:
                    for j in range(2):
                        unit(2 * turn + j, j, 2 * turn + j)
                unit(None, 0, units)

            @block.tensor
            def _(pe):
                def total(j, n):
                    pe.wait_ge(squared.sem, squared.at(n + 1))
                    pe.matmul(self.bank[:, j, :], self.const("ones"), s.sq[:, j, :], start=True, stop=True).then_inc(summed.sem, 1)
                with pe.Fori(0, units // 2) as turn:
                    for j in range(2):
                        n = 2 * turn + j
                        total(j, n)
                        pe.wait_ge(normed.sem, normed.at(n + 1))
                        pe.matmul(self.side[:, j, :], self.const("perm"), s.nrm[:, j, :], start=True, stop=True).then_inc(turned.sem, 1)
                total(0, units)

            @block.vector
            def _(dve):
                def unit(u, j, n, gain, out):
                    dve.wait_ge(rooted.sem, rooted.at(n + 1))
                    dve.reciprocal(s.inv[:, j, :], s.root[:, j, :]).then_inc(inverted.sem, 1)
                    dve.wait_ge(inverted.sem, inverted.at(n + 1))
                    dve.scalar_tensor_tensor(out, unit_src(u), gain, s.inv[:, j, :], ALU.mult, ALU.mult).then_inc(normed.sem, 1)
                with dve.Fori(0, units // 2) as turn:
                    for j in range(2):
                        n = 2 * turn + j
                        unit(n, j, n, self.vec("qk_gain", n), s.nrm[:, j, :])
                        dve.wait_ge(normed.sem, normed.at(n + 1))
                        dve.tensor_tensor(s.cosx[:, j, :], s.nrm[:, j, :], self.const("cos"), ALU.mult).then_inc(products.sem, 1)
                        dve.wait_ge(turned.sem, turned.at(n + 1))
                        dve.tensor_tensor(s.sinx[:, j, :], self.side[:, j, :], self.const("sin"), ALU.mult).then_inc(products.sem, 1)
                        dve.wait_ge(products.sem, products.at(2 * n + 2))
                        dve.tensor_tensor(unit_src(n), s.cosx[:, j, :], s.sinx[:, j, :], ALU.add).then_inc(rotated.sem, 1)
                unit(None, 0, units, self.vec("k_gain"), unit_src(None))
        squared.close(units + 1)
        summed.close(units + 1)
        rooted.close(units + 1)
        inverted.close(units + 1)
        normed.close(units + 1)
        turned.close(units)
        products.close(2 * units)
        rotated.close(units)

    def attend(self, s):
        sig = self.sig
        staged, scored, topped, biased = sig("q_staged"), sig("scored"), sig("topped"), sig("biased")
        powered, inverse, probable = sig("powered"), sig("inverse"), sig("probable")
        flipped, moved_a, moved_b = sig("flipped"), sig("moved_a"), sig("moved_b")
        weighted, kept = sig("weighted"), sig("kept")
        scale = float(P) ** -0.5
        PAIRS = HEADS // 2
        TILES = 2 * TT

        def scores(i):
            return self.bank[:, 2 * (i % 2):2 * (i % 2) + 2, :].rearrange("p a n -> p (a n)")[:, 0:SKV]

        def flips(half):
            return self.side[:, half, :].rearrange("p (a n) -> p a n", n=P)

        with self.nc.Block() as block:
            @block.gpsimd
            def _(pool):
                def stage(pair, j):
                    pool.tensor_copy(s.q[:, j, :], s.qk[:, ds(2 * pair + j, 1), :].rearrange("p a t -> p (a t)")).then_inc(staged.sem, 1)
                for j in range(2):
                    stage(0, j)
                with pool.Fori(1, PAIRS) as pair:
                    for j in range(2):
                        pool.wait_ge(scored.sem, scored.at(TT * (2 * pair + j - 1)))
                        stage(pair, j)

            @block.tensor
            def _(pe):
                for g in range(KV_HEADS):
                    with pe.Fori(0, PAIRS // KV_HEADS) as p:
                        pair = p + g * (PAIRS // KV_HEADS)

                        def score(i):
                            j, qt = divmod(i, TT)
                            if qt == 0:
                                pe.wait_ge(staged.sem, staged.at(2 * pair + j + 1))
                            if i >= 2:
                                pe.wait_ge(powered.sem, powered.at(TILES * pair + i - 1))
                            at, q = scores(i), s.q[:, j, qt * P:(qt + 1) * P]
                            pe.matmul(at[:, 0:T], q, s.qk[:, HEADS + g, :], start=True, stop=True)
                            pe.matmul(at[:, T:SKV], q, s.kc[:, g, :], start=True, stop=True).then_inc(scored.sem, 1)

                        def flip(i):
                            pe.wait_ge(probable.sem, probable.at(TILES * pair + i + 1))
                            if i >= 1:
                                pe.wait_ge(moved_a.sem, moved_a.at(TILES * pair + i))
                                pe.wait_ge(moved_b.sem, moved_b.at(TILES * pair + i))
                            for st in range(ST):
                                mm = pe.transpose(flips(st // 4)[:, st % 4, :], s.p[:, i % 2, st * P:(st + 1) * P], self.const("ident"))
                            mm.then_inc(flipped.sem, 1)

                        def weigh(j):
                            pe.wait_ge(moved_a.sem, moved_a.at(TILES * pair + TT * (j + 1)))
                            pe.wait_ge(moved_b.sem, moved_b.at(TILES * pair + TT * (j + 1)))
                            for st in range(ST):
                                mm = pe.matmul(self.side[:, 2 + j, :], s.v[:, st, g * P:(g + 1) * P], s.pt[:, j, st, :],
                                               start=st == 0, stop=st == ST - 1)
                            mm.then_inc(weighted.sem, 1)
                        score(0)
                        for i in range(TILES):
                            if i + 1 < TILES:
                                score(i + 1)
                            flip(i)
                            if i == TT:
                                weigh(0)
                        weigh(1)
                        pe.wait_ge(kept.sem, kept.at(2 * pair + 2))

            @block.scalar
            def _(act):
                with act.Fori(0, PAIRS) as pair:
                    def exponentials(i):
                        act.wait_ge(biased.sem, biased.at(TILES * pair + i + 1))
                        act.activation(s.p[:, i % 2, :], scores(i), ACT.Exp, bias=s.bias[:, i:i + 1], scale=scale,
                                                  accum_out=s.total[:, i:i + 1]).then_inc(powered.sem, 1)

                    def move(i):
                        act.wait_ge(flipped.sem, flipped.at(TILES * pair + i + 1))
                        j, qt = divmod(i, TT)
                        act.activation(s.pt[:, j, 0:4, qt * P:(qt + 1) * P], flips(0), ACT.Copy).then_inc(moved_a.sem, 1)
                    for i in range(TILES):
                        exponentials(i)
                        if i >= 1:
                            move(i - 1)
                        if i == TT + 2:
                            act.wait_ge(weighted.sem, weighted.at(2 * pair + 1))
                            act.activation(s.o[:, ds(2 * pair, 1), :].rearrange("p a t -> p (a t)"), self.side[:, 2, :], ACT.Copy).then_inc(kept.sem, 1)
                    move(TILES - 1)
                    act.wait_ge(weighted.sem, weighted.at(2 * pair + 2))
                    act.activation(s.o[:, ds(2 * pair + 1, 1), :].rearrange("p a t -> p (a t)"), self.side[:, 3, :], ACT.Copy).then_inc(kept.sem, 1)

            @block.vector
            def _(dve):
                with dve.Fori(0, PAIRS) as pair:
                    def top(i):
                        dve.wait_ge(scored.sem, scored.at(TILES * pair + i + 1))
                        instruction = dve.tensor_reduce(s.top[:, i:i + 1], scores(i), AX.X, ALU.max)
                        instruction.then_inc(topped.sem, 1)
                        dve.wait_ge(topped.sem, topped.at(TILES * pair + i + 1))
                        dve.tensor_scalar(s.bias[:, i:i + 1], s.top[:, i:i + 1], -scale, None, ALU.mult).then_inc(biased.sem, 1)

                    def normal(i):
                        dve.wait_ge(powered.sem, powered.at(TILES * pair + i + 1))
                        dve.reciprocal(s.recip[:, i:i + 1], s.total[:, i:i + 1]).then_inc(inverse.sem, 1)
                        dve.wait_ge(inverse.sem, inverse.at(TILES * pair + i + 1))
                        dve.tensor_scalar(s.p[:, i % 2, :], s.p[:, i % 2, :], s.recip[:, i:i + 1], None, ALU.mult).then_inc(probable.sem, 1)

                    def move(i):
                        dve.wait_ge(flipped.sem, flipped.at(TILES * pair + i + 1))
                        j, qt = divmod(i, TT)
                        dve.tensor_copy(s.pt[:, j, 4:ST, qt * P:(qt + 1) * P], flips(1)[:, 0:ST - 4, :]).then_inc(moved_b.sem, 1)
                    top(0)
                    for i in range(TILES):
                        if i + 1 < TILES:
                            top(i + 1)
                        normal(i)
                        if i >= 1:
                            move(i - 1)
                    move(TILES - 1)
        n = HEADS * TT
        for signal in (scored, topped, biased, powered, inverse, probable, flipped, moved_a, moved_b):
            signal.close(n)
        staged.close(HEADS)
        weighted.close(HEADS)
        kept.close(HEADS)

    def mix_out(self, s):
        base = self.used
        part, merged = self.sig("part"), self.sig("merged")
        with self.nc.Block() as block:
            @block.sync
            def _(sp):
                self.issue(sp, base + 2 * KT + SLOTS)

            @block.tensor
            def _(pe):
                self.slabs(pe, 0, KT, self.linear(pe, s.o))
                pe.wait_ge(merged.sem, merged.at(KT))
                self.slabs(pe, KT, KT, self.linear(pe, s.gates[:, KT:2 * KT, :]))

            @block.vector
            def _(dve):
                def flat(tile, i):
                    return tile[:, ds(i, 1), :].rearrange("p a t -> p (a t)")
                with dve.Fori(0, KT // SLOTS) as turn:
                    for j in range(SLOTS):
                        i = SLOTS * turn + j
                        dve.wait_ge(self.slab_used, base + i + 1)
                        dve.tensor_tensor(flat(s.gates, i), self.bank[:, j, :], flat(s.gates, i), ALU.mult).then_inc(self.taken, 1)
                        dve.wait_ge(self.taken, base + i + 1)
                        dve.tensor_tensor(flat(s.gates, KT + i), flat(s.gates, i), flat(s.gates, KT + i), ALU.add).then_inc(merged.sem, 1)
                self.take(dve, KT, KT, lambda bank, i: dve.scalar_tensor_tensor(
                    flat(self.x, i), bank, self.mod[:, ds(2 * KT + i, 1), 0], flat(self.x, i), ALU.mult, ALU.add))
        merged.close(KT)
        self.used += 2 * KT

    def flip_tiles(self, src, dst, to_natural, after=None):
        flipped, copied = self.sig("tiles_flipped"), self.sig("tiles_copied")
        n = TT * KT // 4

        def where(i):
            t, quarter = divmod(i, KT // 4)
            return t, quarter * 4
        with self.nc.Block() as block:
            @block.tensor
            def _(pe):
                for i in range(n):
                    t, k0 = where(i)
                    if i >= 4:
                        pe.wait_ge(copied.sem, copied.at(i - 3))
                    for j in range(4):
                        at = self.side[:, i % 4, j * P:(j + 1) * P]
                        k = k0 + j
                        tile = src[:, k, t * P:(t + 1) * P] if to_natural else src[:, t, k * P:(k + 1) * P]
                        mm = pe.transpose(at, tile, self.const("ident"))
                    mm.then_inc(flipped.sem, 1)

            @block.vector
            def _(dve):
                for i in range(n):
                    t, k0 = where(i)
                    dve.wait_ge(flipped.sem, flipped.at(i + 1))
                    if to_natural:
                        last = dve.tensor_copy(dst[:, t, k0 * P:(k0 + 4) * P], self.side[:, i % 4, :])
                    elif after is None:
                        last = dve.tensor_copy(dst[:, k0:k0 + 4, t * P:(t + 1) * P],
                                               self.side[:, i % 4, :].rearrange("p (a c) -> p a c", c=P))
                    else:
                        for j in range(4):
                            last = after(dve, k0 + j, t, self.side[:, i % 4, j * P:(j + 1) * P])
                    last.then_inc(copied.sem, 1)
        flipped.close(n)
        copied.close(n)

    def top16(self, dve, chain, n, source, spare, values, places):
        dve.max(values[:, 0:8], source).then_inc(chain.sem, 1)
        dve.wait_ge(chain.sem, chain.at(n + 1))
        dve.nop(nofuse=True)
        dve.max_index(places[:, 0:8], values[:, 0:8], source).then_inc(chain.sem, 1)
        dve.match_replace(spare, values[:, 0:8], source, LOW).then_inc(chain.sem, 1)
        dve.wait_ge(chain.sem, chain.at(n + 3))
        dve.nop(nofuse=True)
        dve.max(values[:, 8:16], spare).then_inc(chain.sem, 1)
        dve.wait_ge(chain.sem, chain.at(n + 4))
        dve.nop(nofuse=True)
        dve.max_index(places[:, 8:16], values[:, 8:16], spare).then_inc(chain.sem, 1)
        return n + 5

    def score_keys(self, s):
        base, n = self.used, 2 * PH
        sig = self.sig
        keyed, copied, scored, staged = sig("keys_loaded"), sig("pq_copied"), sig("key_scored"), sig("key_staged")
        chain, picked = sig("pick_chain"), sig("picked")
        with self.nc.Block() as block:
            @block.sync
            def _(sp):
                sp.dma_start(s.keys[:], self.d["keys"]).then_inc(keyed.sem, 16)
                self.issue(sp, base + n + SLOTS)

            @block.tensor
            def _(pe):
                pe.wait_ge(keyed.sem, keyed.at(16))

                def against_keys(i, j):
                    pe.wait_ge(copied.sem, copied.at(i + 1))
                    for t in range(TT):
                        mm = pe.matmul(self.side[:, j, t * P:(t + 1) * P], s.pq[:, j, t * P:(t + 1) * P],
                                       s.keys[:, ds(i, 1), :].rearrange("p a n -> p (a n)"), start=True, stop=True)
                    mm.then_inc(scored.sem, 1)
                for i in range(n):
                    pos = base + i
                    pe.wait_ge(self.landed[i % SLOTS], 16 * (pos // SLOTS + 1))
                    pe.wait_ge(self.taken, pos - SLOTS + 1)
                    self.linear(pe, self.h)(i % SLOTS, i).then_inc(self.slab_used, 1)
                    if i:
                        against_keys(i - 1, (i - 1) % 2)
                against_keys(n - 1, (n - 1) % 2)

            @block.scalar
            def _(act):
                def turn(i, j, bank):
                    act.wait_ge(self.slab_used, base + i + 1)
                    act.activation(s.pq[:, j, :], self.bank[:, bank, :], ACT.Copy).then_inc(self.taken, 1)
                    act.wait_ge(self.taken, base + i + 1)
                    act.activation(s.mark[:], self.stat[:, 0, 0:1], ACT.Copy).then_inc(copied.sem, 1)
                for i in range(n):
                    if i >= 2:
                        act.wait_ge(scored.sem, scored.at(i - 1))
                    turn(i, i % 2, i % SLOTS)
                    if i:
                        act.wait_ge(scored.sem, scored.at(i))
                        if i > 2:
                            act.wait_ge(picked.sem, picked.at(i - 2))
                        act.activation(s.sk[:, (i - 1) % 2, :], self.side[:, (i - 1) % 2, :], ACT.Copy).then_inc(staged.sem, 1)
                act.wait_ge(scored.sem, scored.at(n))
                act.wait_ge(picked.sem, picked.at(n - 2))
                act.activation(s.sk[:, (n - 1) % 2, :], self.side[:, (n - 1) % 2, :], ACT.Copy).then_inc(staged.sem, 1)

            @block.vector
            def _(dve):
                with dve.Fori(0, n // 2) as turn:
                    for j in range(2):
                        i = 2 * turn + j
                        dve.wait_ge(staged.sem, staged.at(i + 1))
                        dve.nop(nofuse=True)
                        c = 20 * i
                        for t in range(TT):
                            c = self.top16(dve, chain, c, s.sk[:, j, t * P:(t + 1) * P], s.spare[:, 0:P],
                                           s.val[:, t, :], s.pos[:, t, :])
                        dve.wait_ge(chain.sem, chain.at(c))
                        dve.nop(nofuse=True)
                        dve.tensor_copy(s.best[:, :, ds(i, 1), :].rearrange("p t a k -> p t (a k)"), s.val[:])
                        dve.tensor_copy(s.at[:, :, ds(i, 1), :].rearrange("p t a k -> p t (a k)"), s.pos[:]).then_inc(picked.sem, 1)
                        dve.wait_ge(picked.sem, picked.at(i + 1))
        copied.close(n)
        scored.close(n)
        staged.close(n)
        picked.close(n)
        chain.close(20 * n)
        keyed.close(16)
        self.used += n

    def combine(self, s):
        chain = self.sig("pick_chain")
        powered, summed = self.sig("w_powered"), self.sig("w_summed")
        PER = 5 * PH + 19

        def grid(tile, n=PTOP):
            return tile.rearrange("p (a b c) -> p a b c", b=PTOP, c=PTOP)

        def bc_last(ap):
            return ap.unsqueeze(3).to_broadcast([P, PH, PTOP, PTOP])

        def bc_mid(ap):
            return ap.unsqueeze(2).to_broadcast([P, PH, PTOP, PTOP])

        with self.nc.Block() as block:
            @block.vector
            def _(dve):
                with dve.Fori(0, TT) as t:
                    n = [PER * t]

                    def step(instruction):
                        instruction.then_inc(chain.sem, 1)
                        n[0] = n[0] + 1
                        dve.wait_ge(chain.sem, chain.at(n[0]))
                        dve.nop(nofuse=True)
                    best = s.best[:, ds(t, 1), :, :].rearrange("p t (h two) k -> p (t h) two k", two=2)
                    at = s.at[:, ds(t, 1), :, :].rearrange("p t (h two) k -> p (t h) two k", two=2)
                    step(dve.tensor_tensor(grid(s.cand[:]), bc_last(best[:, :, 0, :]), bc_mid(best[:, :, 1, :]), ALU.add))
                    for h in range(PH):
                        n[0] = self.top16(dve, chain, n[0], s.cand[:, h * NCAND:(h + 1) * NCAND], s.spare[:],
                                          s.top[:, h, :], s.place[:, h, :])
                    dve.wait_ge(chain.sem, chain.at(n[0]))
                    for half in range(2):
                        if half == 0:
                            step(dve.tensor_scalar(s.which[:], s.place[:].rearrange("p h k -> p (h k)"), 4, None, ALU.logical_shift_right))
                        else:
                            step(dve.tensor_scalar(s.which[:], s.place[:].rearrange("p h k -> p (h k)"), PTOP - 1, None, ALU.bitwise_and))
                        step(dve.tensor_copy(s.whichf[:], s.which[:]))
                        iota = self.const("iota", b=PTOP).unsqueeze(1).unsqueeze(1).to_broadcast([P, PH, PTOP, PTOP])
                        step(dve.tensor_tensor(grid(s.cand[:]), bc_last(s.whichf[:].rearrange("p (h k) -> p h k", k=PTOP)), iota, ALU.is_equal))
                        step(dve.tensor_copy(s.atf[:], at[:, :, half, :]))
                        step(dve.tensor_tensor(grid(s.cand[:]), grid(s.cand[:]), bc_mid(s.atf[:]), ALU.mult))
                        step(dve.tensor_reduce(s.key[:, half, :], grid(s.cand[:]), AX.X, ALU.add))
                    step(dve.scalar_tensor_tensor(s.key[:, 0, :], s.key[:, 0, :], float(PKEYS), s.key[:, 1, :], ALU.mult, ALU.add))
                    step(dve.tensor_copy(s.expert[:, ds(t, 1), :].rearrange("p a n -> p (a n)"), s.key[:, 0, :]))
                    step(dve.tensor_tensor(s.power[:], s.top[:], s.top[:, :, 0:1].to_broadcast([P, PH, PTOP]), ALU.subtract))
                    dve.wait_ge(powered.sem, powered.at(t + 1))
                    step(dve.tensor_reduce(s.wsum[:], s.power[:], AX.X, ALU.add))
                    step(dve.reciprocal(s.wsum[:], s.wsum[:]))
                    wt = s.weight[:, ds(t, 1), :].rearrange("p a (h k) -> p (a h) k", k=PTOP)
                    dve.tensor_tensor(wt, s.power[:], s.wsum[:].unsqueeze(2).to_broadcast([P, PH, PTOP]), ALU.mult).then_inc(chain.sem, 1)
                    n[0] = n[0] + 1
                    s.per = n[0]

            @block.scalar
            def _(act):
                with act.Fori(0, TT) as t:
                    act.wait_ge(chain.sem, chain.at(PER * t + 5 * PH + 1 + 12 + 3))
                    act.activation(s.power[:], s.power[:], ACT.Exp).then_inc(powered.sem, 1)
        powered.close(TT)
        chain.close(TT * (5 * PH + 1 + 12 + 3 + 3))

    def experts(self, s):
        sig, d = self.sig, self.d
        G = s.row.shape[1]
        GROUPS = PSEL // G
        indexed, dotted, row_used, coefficient = sig("indexed"), sig("dotted"), sig("row_used"), sig("coefficient")
        gelued, added, hready = sig("gelued"), sig("row_added"), sig("h_ready")
        landed = [sig(f"row_landed{j}") for j in range(G)]
        with self.nc.Block() as block:
            @block.gpsimd
            def _(pool):
                def gathers(table, t, group, number, first=False):
                    if not first:
                        pool.wait_ge(row_used.sem, row_used.at(G * number))
                        pool.nop(nofuse=True)
                    pool.tensor_copy(s.index[:], s.expert[:, ds(t, 1), ds(G * group, G)].rearrange("p a n -> p (a n)")).then_inc(indexed.sem, 1)
                    pool.wait_ge(indexed.sem, indexed.at(number + 1))
                    pool.nop(nofuse=True)
                    for j in range(G):
                        if not first:
                            pool.wait_ge(row_used.sem, row_used.at(G * (number - 1) + j + 1))
                            pool.nop(nofuse=True)
                        pool.indirect_dma_start(
                            out=s.row[:, j, :], out_offset=None, in_=table,
                            in_offset=bass.IndirectOffsetOnAxis(ap=s.index[:, j:j + 1], axis=0)).then_inc(landed[j].sem, 16)
                for table, half in ((d["peer_u"], 0),):
                    gathers(table, 0, 0, 0, first=True)
                    with pool.Fori(1, GROUPS) as group:
                        gathers(table, 0, group, group)
                with pool.Fori(0, GROUPS) as group:
                    gathers(d["peer_v"], 0, group, GROUPS + group)
                with pool.Fori(1, TT) as t:
                    with pool.Fori(0, GROUPS) as group:
                        gathers(d["peer_u"], t, group, 2 * GROUPS * t + group)
                    with pool.Fori(0, GROUPS) as group:
                        gathers(d["peer_v"], t, group, 2 * GROUPS * t + GROUPS + group)

            @block.vector
            def _(dve):
                with dve.Fori(0, TT) as t:
                    dve.tensor_copy(s.hcur[:], s.hn[:, ds(t, 1), :].rearrange("p a n -> p (a n)")).then_inc(hready.sem, 1)
                    dve.wait_ge(hready.sem, hready.at(t + 1))
                    dve.nop(nofuse=True)
                    with dve.Fori(0, GROUPS) as group:
                        number = 2 * GROUPS * t + group
                        for j in range(G):
                            dve.wait_ge(landed[j].sem, landed[j].at(16 * (number + 1)))
                            dve.tensor_tensor_reduce(s.row[:, j, :], s.row[:, j, :], s.hcur[:], 1.0, 0.0, ALU.mult, ALU.add,
                                                                 s.dot[:, j:j + 1]).then_inc(row_used.sem, 1)
                        dve.wait_ge(row_used.sem, row_used.at(G * (number + 1)))
                        dve.tensor_copy(s.act[:, ds(G * group, G)], s.dot[:]).then_inc(dotted.sem, 1)
                        dve.wait_ge(dotted.sem, dotted.at(GROUPS * t + group + 1))
                    dve.wait_ge(gelued.sem, gelued.at(t + 1))
                    dve.tensor_tensor(s.coef[:], s.gelu[:], s.weight[:, ds(t, 1), :].rearrange("p a n -> p (a n)"), ALU.mult).then_inc(coefficient.sem, 1)
                    dve.wait_ge(coefficient.sem, coefficient.at(2 * t + 1))
                    y = s.y[:, ds(t, 1), :].rearrange("p a n -> p (a n)")
                    dve.memset(s.acc[:], 0.0).then_inc(coefficient.sem, 1)
                    dve.wait_ge(coefficient.sem, coefficient.at(2 * t + 2))
                    dve.nop(nofuse=True)
                    with dve.Fori(0, GROUPS) as group:
                        number = 2 * GROUPS * t + GROUPS + group
                        for j in range(G):
                            dve.wait_ge(landed[j].sem, landed[j].at(16 * (number + 1)))
                            dve.wait_ge(row_used.sem, row_used.at(G * number + j - 1))
                            dve.scalar_tensor_tensor(s.acc[:, j % 2, :], s.row[:, j, :], s.coef[:, ds(G * group + j, 1)],
                                                                 s.acc[:, j % 2, :], ALU.mult, ALU.add).then_inc(row_used.sem, 1)
                        dve.wait_ge(row_used.sem, row_used.at(G * (number + 1)))
                    dve.tensor_tensor(y, s.acc[:, 0, :], s.acc[:, 1, :], ALU.add).then_inc(added.sem, 1)
                    dve.wait_ge(added.sem, added.at(t + 1))

            @block.scalar
            def _(act):
                with act.Fori(0, TT) as t:
                    act.wait_ge(dotted.sem, dotted.at(GROUPS * (t + 1)))
                    act.activation(s.gelu[:], s.act[:], ACT.Gelu).then_inc(gelued.sem, 1)
        groups = 2 * GROUPS * TT
        indexed.close(groups)
        for signal in landed:
            signal.close(16 * groups)
        row_used.close(G * groups)
        dotted.close(GROUPS * TT)
        gelued.close(TT)
        coefficient.close(2 * TT)
        added.close(TT)
        hready.close(TT)

    def mix_in(self, s, layer):
        base = self.used
        sig = self.sig
        chain, low, gate = sig("mix_chain"), sig("low"), sig("decay")
        with self.nc.Block() as block:
            @block.sync
            def _(sp):
                self.issue(sp, base + 24 + SLOTS)

            @block.tensor
            def _(pe):
                self.slabs(pe, 0, 16, self.linear(pe, self.h))
                self.slabs(pe, 16, 4, lambda slot, i: self.natural(pe, self.h, slot, self.bank[:, slot, :], TT))
                self.slabs(pe, 20, 4, self.linear(pe, self.h))
                for k in range(KT):
                    at = (layer * KT + k) * 16
                    mm = pe.matmul(self.side[0:16, 0, :], self.small[:, at:at + 16], self.h[:, k, :], start=k == 0, stop=k == KT - 1)
                mm.then_inc(low.sem, 1)
                pe.wait_ge(low.sem, low.at(2))
                for p in range(2):
                    at = 2 * KT * 16 + KT * NE + layer * 2 * P + p * P
                    mm = pe.matmul(self.side[:, 1 + p, :], self.small[0:16, at:at + P], s.low[0:16, :], start=True, stop=True)
                mm.then_inc(low.sem, 1)

            @block.scalar
            def _(act):
                def flat(tile):
                    return lambda bank, i: act.activation(tile[:, ds(i, 1), :].rearrange("p a t -> p (a t)"), bank, ACT.Copy)
                self.take(act, 0, 8, flat(s.cch))
                self.take(act, 8, 4, flat(s.cb))
                self.take(act, 12, 4, flat(s.qk))
                self.take(act, 16, 4, lambda bank, i: act.activation(
                    s.v[:, :, ds(i, 1), :].rearrange("p t a n -> p t (a n)"), bank.rearrange("p (t n) -> p t n", n=P), ACT.Copy))
                self.take(act, 20, 4, lambda bank, i: act.activation(
                    s.gate[:, ds(i, 1), :].rearrange("p a t -> p (a t)"), bank, ACT.Silu))
                act.wait_ge(low.sem, low.at(1))
                act.activation(s.low[0:16, :], self.side[0:16, 0, :], ACT.Copy).then_inc(low.sem, 1)
                act.wait_ge(low.sem, low.at(3))
                for p in range(2):
                    act.activation(s.z[:, p, :], self.side[:, 1 + p, :], ACT.Identity, bias=self.vectors[
                        :, VECTORS["gk_b"][0] + 2 * layer + p:VECTORS["gk_b"][0] + 2 * layer + p + 1]).then_inc(gate.sem, 1)
                act.wait_ge(gate.sem, gate.at(3))
                act.activation(s.b[:], s.b[:], ACT.Exp, scale=-1.0).then_inc(gate.sem, 1)
                act.wait_ge(gate.sem, gate.at(4))
                act.activation(s.b[:], s.b[:], ACT.Ln, bias=self.one).then_inc(gate.sem, 1)
                act.wait_ge(gate.sem, gate.at(6))
                act.activation(s.eb[:], s.b[:], ACT.Exp).then_inc(gate.sem, 1)
                act.activation(s.enb[:], s.b[:], ACT.Exp, scale=-1.0).then_inc(gate.sem, 1)
                act.activation(s.z[:], s.z[:], ACT.Exp).then_inc(gate.sem, 1)

            @block.vector
            def _(dve):
                n = [0]

                def step(instruction):
                    instruction.then_inc(chain.sem, 1)
                    n[0] += 1
                    dve.wait_ge(chain.sem, chain.at(n[0]))

                def tap(c, j):
                    at = VECTORS["conv2_w"][0] + (layer * CONV2 + c) * TAPS2 + j
                    return self.vectors[:, at:at + 1]
                step(dve.memset(s.zpad[:, :, 0:2], 0.0))
                for c in range(CONV2):
                    dve.wait_ge(self.taken, base + 2 * c + 2)
                    step(dve.tensor_tensor(s.zpad[:, c, 2:2 + T], s.cch[:, 2 * c, :], s.cch[:, 2 * c + 1, :], ALU.mult))
                    step(dve.tensor_scalar(s.y[:, c, :], s.zpad[:, c, 0:T], tap(c, 0), None, ALU.mult))
                    for j in range(1, TAPS2):
                        step(dve.scalar_tensor_tensor(s.y[:, c, :], s.zpad[:, c, j:j + T], tap(c, j), s.y[:, c, :], ALU.mult, ALU.add))
                for c in range(CONV2):
                    dve.wait_ge(self.taken, base + 9 + c)
                    step(dve.tensor_tensor(s.y[:, c, :], s.y[:, c, :], s.cb[:, c, :], ALU.mult))
                dve.wait_ge(gate.sem, gate.at(2))
                dve.scalar_tensor_tensor(s.b[:], s.z[:], -1.0, s.z[:], ALU.mult, ALU.max).then_inc(gate.sem, 1)
                dve.wait_ge(gate.sem, gate.at(5))
                step(dve.scalar_tensor_tensor(s.z[:], s.z[:], 0.0, s.b[:], ALU.min, ALU.subtract))
                step(dve.tensor_scalar(s.z[:], s.z[:], 1.0 / 16.0, -1.0, ALU.mult, ALU.max))
                for p in range(2):
                    step(dve.tensor_tensor_scan(s.b[:, p, :], self.const("carry"), s.z[:, p, :], 0.0, ALU.mult, ALU.add))
                chunks = s.b[:].rearrange("p a (n c) -> p (a n) c", c=GCH)
                dve.tensor_tensor(s.z[:].rearrange("p a (n c) -> p (a n) c", c=GCH),
                                          chunks[:, :, GCH - 1:GCH].to_broadcast([P, 2 * NCH, GCH]), chunks, ALU.subtract).then_inc(gate.sem, 1)
                dve.wait_ge(self.taken, base + 16)
                dve.wait_ge(gate.sem, gate.at(9))
                step(dve.scalar_tensor_tensor(s.qk[:, 0:2, :], s.qk[:, 0:2, :], float(GDK) ** -0.5, s.eb[:], ALU.mult, ALU.mult))
                step(dve.tensor_tensor(s.enb[:], s.enb[:], s.qk[:, 2:4, :], ALU.mult))
                step(dve.tensor_tensor(s.kout[:], s.z[:], s.qk[:, 2:4, :], ALU.mult))
                s.steps = n[0]
        chain.close(s.steps)
        low.close(3)
        gate.close(9)
        self.used += 24

    def linear_attention(self, s, layer):
        sig = self.sig
        masked, scored, weighed = sig("k_masked"), sig("gla_scored"), sig("gla_weighed")
        flipped, parted, added, chain = sig("kout_flipped"), sig("kout_parted"), sig("kv_made"), sig("state_chain")
        made, squared, summed, rooted = sig("o_made"), sig("o_squared"), sig("o_summed"), sig("o_rooted")
        oc = sig("o_chain")
        half = self.const("half")
        qin = s.qk[:, 0:2, :]
        PAIRS = GH // 2

        with self.nc.Block() as block:
            @block.tensor
            def _(pe):
                for p in range(PAIRS):
                    for t in range(TT):
                        mm = pe.transpose(self.side[:, p, t * P:(t + 1) * P], s.kout[:, p, t * P:(t + 1) * P], self.const("ident"))
                    mm.then_inc(flipped.sem, 1)
                for h in range(GH):
                    pe.wait_ge(masked.sem, masked.at(h + 1))
                    for t in range(TT):
                        at = slice(t * P, (t + 1) * P)
                        mm = pe.matmul(self.bank[:, h, at], s.kmask[:, h, at], qin[:, h // 2, at], start=True, stop=True)
                    mm.then_inc(scored.sem, 1)
                for p in range(PAIRS):
                    after = weighed if p == 0 else parted
                    pe.wait_ge(after.sem, after.at(GH))
                    if p == 0:
                        pe.wait_ge(parted.sem, parted.at(2))
                    for n in range(NCH):
                        place = (self.bank if p == 0 else self.side)[:, n // 2, (n % 2) * 2 * P:(n % 2 + 1) * 2 * P]
                        mm = pe.matmul(place, s.kon[:, n % 2, p, (n // 2) * P:(n // 2 + 1) * P],
                                       s.v[:, n // 2, 2 * p:2 * p + 2, :].rearrange("p a n -> p (a n)"), start=True, stop=True)
                        if n % 2:
                            mm.then_inc(added.sem, 1)
                for h in range(GH):
                    p = h // 2
                    pe.wait_ge(chain.sem, chain.at((p + 1) * (NCH // 2 + NCH - 2)))
                    if p == 0 and h == 0:
                        pass
                    for t in range(TT):
                        pe.matmul(self.bank[:, h, t * P:(t + 1) * P], s.v[:, t, h, :], s.a[:, h, t * P:(t + 1) * P],
                                  start=True, stop=False, skip_group_check=True)
                        for r in range(2):
                            n = 2 * t + r
                            if n:
                                mm = pe.matmul(self.bank[:, h, n * GCH:(n + 1) * GCH],
                                               s.state[:, p, n - 1, (h % 2) * P:(h % 2 + 1) * P],
                                               qin[:, p, n * GCH:(n + 1) * GCH], start=False, stop=r == 1, skip_group_check=True)
                    mm.then_inc(made.sem, 1)
                for h in range(GH):
                    pe.wait_ge(squared.sem, squared.at(h + 1))
                    if h == 0:
                        pe.wait_ge(chain.sem, chain.at(PAIRS * (NCH // 2 + NCH - 2)))
                    pe.matmul(self.side[:, h, :], self.const("ones"), s.sq[:, h, :], start=True, stop=True).then_inc(summed.sem, 1)

            @block.vector
            def _(dve):
                for h in range(GH):
                    dve.tensor_scalar(s.kmask[:, h, :], s.enb[:, h // 2, :], half[:, h % 2:h % 2 + 1], None, ALU.mult).then_inc(masked.sem, 1)
                for p in range(PAIRS):
                    dve.wait_ge(flipped.sem, flipped.at(p + 1))
                    for r in range(2):
                        dve.tensor_scalar(s.kon[:, r, p, :], self.side[:, p, :], half[:, r:r + 1], None, ALU.mult).then_inc(parted.sem, 1)
                for h in range(GH):
                    dve.wait_ge(scored.sem, scored.at(h + 1))
                    dve.tensor_tensor(s.a[:, h, :].rearrange("p (t n) -> p t n", n=P),
                                                 self.bank[:, h, :].rearrange("p (t n) -> p t n", n=P),
                                                 self.const("causal").unsqueeze(1).to_broadcast([P, TT, P]), ALU.mult).then_inc(weighed.sem, 1)
                k = 0
                for p in range(PAIRS):
                    source = self.bank if p == 0 else self.side
                    for n in range(NCH // 2):
                        dve.wait_ge(added.sem, added.at(p * (NCH // 2) + n + 1))
                        dve.tensor_tensor(s.state[:, p, 2 * n:2 * n + 2, :], source[:, n, :].rearrange("p (a m) -> p a m", a=2),
                                                   self.const("pair").unsqueeze(1).to_broadcast([P, 2, 2 * P]), ALU.mult).then_inc(chain.sem, 1)
                        k += 1
                    for n in range(1, NCH - 1):
                        dve.wait_ge(chain.sem, chain.at(k))
                        dve.scalar_tensor_tensor(s.state[:, p, n, :], s.state[:, p, n - 1, :],
                                                          s.eb[:, p, (n + 1) * GCH - 1:(n + 1) * GCH], s.state[:, p, n, :],
                                                          ALU.mult, ALU.add).then_inc(chain.sem, 1)
                        k += 1
                assert k == PAIRS * (NCH // 2 + NCH - 2)
                for h in range(GH):
                    dve.wait_ge(rooted.sem, rooted.at(h + 1))
                    dve.reciprocal(s.inv[:], s.root[:, h, :]).then_inc(oc.sem, 1)
                    dve.wait_ge(oc.sem, oc.at(3 * h + 1))
                    dve.tensor_tensor(s.inv[:], self.bank[:, h, :], s.inv[:], ALU.mult).then_inc(oc.sem, 1)
                    dve.wait_ge(oc.sem, oc.at(3 * h + 2))
                    dve.scalar_tensor_tensor(s.y[:, CONV2 + h, :], s.inv[:],
                                                   self.vectors[:, VECTORS["gla_g"][0] + layer:VECTORS["gla_g"][0] + layer + 1],
                                                   s.gate[:, h, :], ALU.mult, ALU.mult).then_inc(oc.sem, 1)
                    dve.wait_ge(oc.sem, oc.at(3 * h + 3))

            @block.scalar
            def _(act):
                for h in range(GH):
                    act.wait_ge(made.sem, made.at(h + 1))
                    act.activation(s.sq[:, h, :], self.bank[:, h, :], ACT.Square).then_inc(squared.sem, 1)
                for h in range(GH):
                    act.wait_ge(summed.sem, summed.at(h + 1))
                    act.activation(s.root[:, h, :], self.side[:, h, :], ACT.Sqrt, bias=self.eps[EPS], scale=1.0 / GDV).then_inc(rooted.sem, 1)
        for signal in (masked, scored, weighed, parted, made, squared, summed, rooted):
            signal.close(GH)
        flipped.close(2)
        added.close(NCH)
        chain.close(PAIRS * (NCH // 2 + NCH - 2))
        oc.close(3 * GH)

    def residual(self, src, gain):
        base = self.used
        chain = self.sig("residual_chain")
        with self.nc.Block() as block:
            @block.sync
            def _(sp):
                self.issue(sp, base + KT + SLOTS)

            @block.tensor
            def _(pe):
                self.slabs(pe, 0, KT, self.linear(pe, src))

            @block.vector
            def _(dve):
                with dve.Fori(0, KT // SLOTS) as turn:
                    for j in range(SLOTS):
                        i = SLOTS * turn + j
                        dve.wait_ge(self.slab_used, base + i + 1)
                        dve.tensor_scalar(self.stat[:, j % 2, :], self.bank[:, j, :], gain(i), None, ALU.mult).then_inc(self.taken, 1)
                        dve.wait_ge(self.taken, base + i + 1)
                        flat = self.x[:, ds(i, 1), :].rearrange("p a t -> p (a t)")
                        dve.scalar_tensor_tensor(flat, flat, ALPHA, self.stat[:, j % 2, :], ALU.mult, ALU.add).then_inc(chain.sem, 1)
                        dve.wait_ge(chain.sem, chain.at(i + 1))
        chain.close(KT)
        self.used += KT

    def dense_up(self, s):
        base = self.used
        made = self.sig("hidden_made")
        with self.nc.Block() as block:
            @block.sync
            def _(sp):
                self.issue(sp, base + 2 * FT + SLOTS)

            @block.tensor
            def _(pe):
                self.slabs(pe, 0, 2 * FT, self.linear(pe, self.h))

            @block.scalar
            def _(act):
                def turn(turn, first=False):
                    for j in range(SLOTS):
                        act.wait_ge(self.slab_used, base + SLOTS * turn + j + 1)
                        if j % 2 == 0 and not first:
                            act.wait_ge(made.sem, made.at(2 * turn + j // 2 - 1))
                        act.activation(s.ab[:, j, :], self.bank[:, j, :], ACT.Copy if j % 2 else ACT.Silu).then_inc(self.taken, 1)
                turn(0, first=True)
                with act.Fori(1, 2 * FT // SLOTS) as t:
                    turn(t)

            @block.vector
            def _(dve):
                with dve.Fori(0, FT // 2) as turn:
                    for j in range(2):
                        f = 2 * turn + j
                        dve.wait_ge(self.taken, base + 2 * f + 2)
                        dve.tensor_tensor(s.hidden[:, ds(f, 1), :].rearrange("p a t -> p (a t)"),
                                                  s.ab[:, 2 * j, :], s.ab[:, 2 * j + 1, :], ALU.mult).then_inc(made.sem, 1)
        made.close(FT)
        self.used += 2 * FT

    def dense_down(self, s, gain):
        base = self.used
        chain = self.sig("residual_chain")
        with self.nc.Block() as block:
            @block.sync
            def _(sp):
                self.issue(sp, base + 2 * KT + SLOTS)

            @block.tensor
            def _(pe):
                def product(slot, index):
                    half = slot % 2
                    for k in range(HALF_FT):
                        mm = pe.matmul(self.bank[:, slot - half, :], self.wslab(slot, k), s.hidden[:, half * HALF_FT + k, :],
                                       start=half == 0 and k == 0, stop=half == 1 and k == HALF_FT - 1)
                    return mm
                self.slabs(pe, 0, 2 * KT, product)

            @block.vector
            def _(dve):
                with dve.Fori(0, KT // 2) as turn:
                    for j in range(2):
                        i = 2 * turn + j
                        dve.wait_ge(self.slab_used, base + 2 * i + 2)
                        dve.tensor_scalar(self.stat[:, j, :], self.bank[:, 2 * j, :], gain(i), None, ALU.mult).then_inc(self.taken, 2)
                        dve.wait_ge(self.taken, base + 2 * i + 2)
                        flat = self.x[:, ds(i, 1), :].rearrange("p a t -> p (a t)")
                        dve.scalar_tensor_tensor(flat, flat, ALPHA, self.stat[:, j, :], ALU.mult, ALU.add).then_inc(chain.sem, 1)
                        dve.wait_ge(chain.sem, chain.at(i + 1))
        chain.close(KT)
        self.used += 2 * KT

    def route(self, s):
        sig, d = self.sig, self.d
        stored, routed, picked, member = sig("tokens_stored"), sig("routed"), sig("expert_picked"), sig("member")
        ranked, chain, weights = sig("ranked"), sig("route_chain"), sig("route_exp")
        cleared, spread, numbered, read = sig("table_cleared"), sig("table_filled"), sig("numbered"), sig("table_read")
        at = 2 * KT * 16
        with self.nc.Block() as block:
            @block.sync
            def _(sp):
                sp.dma_start(s.tokens.rearrange("(t p) n -> p t n", p=P), s.hn[:]).then_inc(stored.sem, 16)
                sp.wait_ge(stored.sem, stored.at(16))
                sp.wait_ge(spread.sem, spread.at(16 * 2 * TT))
                with self.nc.allow_non_contiguous_dma(reason="2048 slot numbers"):
                    sp.dma_start(s.slot_token[:], s.table.rearrange("(b p) o -> p (b o)", p=P)).then_inc(read.sem, 16)
                sp.wait_ge(read.sem, read.at(16))

            @block.tensor
            def _(pe):
                for t in range(TT):
                    for k in range(KT):
                        mm = pe.matmul(self.side[:, 0, t * NE:(t + 1) * NE], self.h[:, k, t * P:(t + 1) * P],
                                       self.small[:, at + k * NE:at + (k + 1) * NE], start=k == 0, stop=k == KT - 1)
                mm.then_inc(routed.sem, 1)
                pe.wait_ge(member.sem, member.at(1))
                for t in range(TT):
                    pe.matmul(self.side[:, 1, t * NE:(t + 1) * NE], self.const("before"), s.member[:, t, :], start=True, stop=t == 0)
                    for u in range(t):
                        pe.matmul(self.side[:, 1, t * NE:(t + 1) * NE], self.const("ones"), s.member[:, u, :], start=False, stop=u == t - 1)
                for t in range(TT):
                    mm = pe.matmul(self.side[:, 2, 0:NE], self.const("ones"), s.member[:, t, :], start=t == 0, stop=t == TT - 1)
                mm.then_inc(ranked.sem, 1)

            @block.scalar
            def _(act):
                act.wait_ge(weights.sem, weights.at(1))
                act.activation(s.w[:, 1, :], s.w[:, 1, :], ACT.Exp).then_inc(weights.sem, 1)
                act.wait_ge(chain.sem, chain.at(1))
                act.dma_start(s.table.rearrange("(p b) o -> p (b o)", p=P), s.zero[:]).then_inc(self.sig("act_stored").sem, 16)
                act.wait_ge(self.sig("act_stored").sem, self.sig("act_stored").at(16))
                act.activation(s.mark[:], self.eps[EPS], ACT.Copy).then_inc(cleared.sem, 1)

            @block.vector
            def _(dve):
                n = [0]

                def step(instruction):
                    instruction.then_inc(chain.sem, 1)
                    n[0] += 1
                    dve.wait_ge(chain.sem, chain.at(n[0]))
                step(dve.memset(s.zero[:], 0))
                dve.wait_ge(routed.sem, routed.at(1))
                step(dve.tensor_copy(s.logit[:].rearrange("p t e -> p (t e)"), self.side[:, 0, 0:TT * NE]))
                for t in range(TT):
                    step(dve.max(s.best[:, t, :], s.logit[:, t, :]))
                    step(dve.max_index(s.place[:, t, :], s.best[:, t, :], s.logit[:, t, :]))
                dve.tensor_tensor(s.w[:, 1, :], s.best[:, :, 1], s.best[:, :, 0], ALU.subtract).then_inc(weights.sem, 1)
                step(dve.tensor_copy(s.choice[:].rearrange("p c t -> p t c"), s.place[:, :, 0:2]))
                iota = self.const("iota", b=NE).unsqueeze(1).to_broadcast([P, TOP2 * TT, NE])
                step(dve.tensor_tensor(s.hot[:].rearrange("p c t e -> p (c t) e"),
                                       s.choice[:].rearrange("p c t -> p (c t)").unsqueeze(2).to_broadcast([P, TOP2 * TT, NE]), iota, ALU.is_equal))
                dve.tensor_tensor(s.member[:], s.hot[:, 0, :, :], s.hot[:, 1, :, :], ALU.add).then_inc(member.sem, 1)
                dve.wait_ge(weights.sem, weights.at(2))
                step(dve.tensor_scalar(s.w[:, 0, :], s.w[:, 1, :], 1.0, None, ALU.add))
                step(dve.reciprocal(s.w[:, 0, :], s.w[:, 0, :]))
                step(dve.tensor_tensor(s.w[:, 1, :], s.w[:, 1, :], s.w[:, 0, :], ALU.mult))
                dve.wait_ge(ranked.sem, ranked.at(1))
                total = self.side[:, 2, 0:NE]
                step(dve.tensor_scalar(s.blocks[:], total, 0.0, None, ALU.is_gt))
                for j in range(1, TT):
                    step(dve.scalar_tensor_tensor(s.blocks[:], total, float(j * P), s.blocks[:], ALU.is_gt, ALU.add))
                step(dve.tensor_tensor_scan(s.end[:], self.const("ones", b=NE), s.blocks[:], 0.0, ALU.mult, ALU.add))
                step(dve.tensor_tensor(s.start[:], s.end[:], s.blocks[:], ALU.subtract))
                step(dve.tensor_scalar(s.start[:], s.start[:], float(P), None, ALU.mult))
                step(dve.tensor_tensor(s.where[:], self.side[:, 1, 0:TT * NE].rearrange("p (t e) -> p t e", e=NE),
                                       s.start[:].unsqueeze(1).to_broadcast([P, TT, NE]), ALU.add))
                for c in range(TOP2):
                    step(dve.tensor_tensor(s.hot[:, c, :, :], s.hot[:, c, :, :], s.where[:], ALU.mult))
                step(dve.tensor_reduce(s.slotf[:], s.hot[:].rearrange("p c t e -> p (c t) e"), AX.X, ALU.add))
                step(dve.tensor_copy(s.slot[:], s.slotf[:]))
                step(dve.tensor_tensor(s.before[:], s.end[:].unsqueeze(1).to_broadcast([P, BLOCKS, NE]),
                                       self.const("iota", b=BLOCKS).unsqueeze(2).to_broadcast([P, BLOCKS, NE]), ALU.is_le))
                step(dve.tensor_reduce(s.ownerf[:], s.before[:], AX.X, ALU.add))
                step(dve.tensor_scalar(s.ownerf[:], s.ownerf[:], float(NE - 1), None, ALU.min))
                step(dve.tensor_copy(s.owner[:], s.ownerf[:]))
                dve.memset(s.mark2[:], 0.0).then_inc(picked.sem, 1)
                s.steps = n[0]

            @block.gpsimd
            def _(pool):
                pool.iota(s.token[:], pattern=[[P, TT]], base=0, channel_multiplier=1).then_inc(numbered.sem, 1)
                pool.wait_ge(numbered.sem, numbered.at(1))
                pool.wait_ge(cleared.sem, cleared.at(1))
                pool.wait_ge(picked.sem, picked.at(1))
                for c in range(TOP2):
                    for t in range(TT):
                        j = c * TT + t
                        pool.indirect_dma_start(
                            out=s.table, out_offset=bass.IndirectOffsetOnAxis(ap=s.slot[:, j:j + 1], axis=0),
                            in_=s.token[:, t:t + 1], in_offset=None).then_inc(spread.sem, 16)
                pool.wait_ge(spread.sem, spread.at(16 * TOP2 * TT))
        stored.close(16)
        routed.close(1)
        picked.close(1)
        member.close(1)
        ranked.close(1)
        chain.close(s.steps)
        weights.close(2)
        cleared.close(1)
        spread.close(16 * TOP2 * TT)
        numbered.close(1)
        read.close(16)
        self.sig("act_stored").close(16)

    def run_experts(self, s):
        sig, d = self.sig, self.d
        used, gathered, numbered = sig("moe_used"), sig("slots_gathered"), sig("slots_numbered")
        flipped, ready = sig("x_flipped"), sig("x_ready")
        lit, hidden, turned, moved = sig("pair_silu"), sig("pair_hidden"), sig("hidden_turned"), sig("hidden_moved")
        kept, stored = sig("kept"), sig("act_stored")
        landed = [sig(f"expert_slab_landed{j}") for j in range(MOE_SLOTS)]
        assert MOE_SLABS % MOE_SLOTS == 0
        weights = d["moe"].rearrange("e s p n -> (e s) p n")

        with self.nc.Block() as block:
            @block.sync
            def _(sp):
                def slab(b, e, i, first=False):
                    if not first:
                        sp.wait_ge(used.sem, used.at(MOE_SLABS * b + i - MOE_SLOTS + 1))
                    sp.dma_start(
                        s.wring[:, i % MOE_SLOTS, :], weights[ds(e * MOE_SLABS + i, 1)].rearrange("a p n -> (a p) n")).then_inc(landed[i % MOE_SLOTS].sem, 16)
                e = sp.value_load(s.owner[0:1, 0:1], min_val=0, max_val=NE - 1)
                for i in range(MOE_SLABS):
                    slab(0, e, i, first=i < MOE_SLOTS)
                with sp.Fori(1, BLOCKS) as b:
                    e = sp.value_load(s.owner[0:1, ds(b, 1)], min_val=0, max_val=NE - 1)
                    for i in range(MOE_SLABS):
                        slab(b, e, i)

            @block.gpsimd
            def _(pool):
                def gather(b):
                    pool.tensor_copy(s.number[:], s.slot_token[:, ds(b, 1)]).then_inc(numbered.sem, 1)
                    pool.wait_ge(numbered.sem, numbered.at(b + 1))
                    pool.nop(nofuse=True)
                    pool.indirect_dma_start(out=s.xs[:], out_offset=None, in_=s.tokens,
                                                        in_offset=bass.IndirectOffsetOnAxis(ap=s.number[:], axis=0)).then_inc(gathered.sem, 16)
                gather(0)
                with pool.Fori(1, BLOCKS + 1) as b:
                    pool.wait_ge(flipped.sem, flipped.at(b))
                    pool.nop(nofuse=True)
                    gather(b)

            @block.tensor
            def _(pe):
                def flip(b):
                    pe.wait_ge(gathered.sem, gathered.at(16 * (b + 1)))
                    for k in range(KT):
                        mm = pe.transpose(self.side[:, 2 + k // 4, (k % 4) * P:(k % 4 + 1) * P], s.xs[:, k * P:(k + 1) * P], self.const("ident"))
                    mm.then_inc(flipped.sem, 1)

                flip(0)
                with pe.Fori(0, BLOCKS) as b:
                    def slab(i):
                        pe.wait_ge(landed[i % MOE_SLOTS].sem, landed[i % MOE_SLOTS].at(16 * (MOE_SLABS // MOE_SLOTS) * b + 16 * (i // MOE_SLOTS + 1)))
                        return s.wring[:, i % MOE_SLOTS, :]

                    def down(c):
                        pe.wait_ge(hidden.sem, hidden.at(STEPS * b + c + 1))
                        for kk in range(2):
                            mm = pe.transpose(self.bank[:, 2 + c % 2, kk * P:(kk + 1) * P], s.hidden[:, c % 2, kk * P:(kk + 1) * P],
                                              self.const("ident"))
                        mm.then_inc(turned.sem, 1)
                        if c == STEPS - 1:
                            flip(b + 1)
                        w = slab(MOE_ORDER.index((2, c)))
                        pe.wait_ge(moved.sem, moved.at(STEPS * b + c + 1))
                        if c == 0:
                            pe.wait_ge(kept.sem, kept.at(b))
                        for kk in range(2):
                            for half in range(2):
                                mm = pe.matmul(self.side[:, half, :], s.ht[:, c % 2, kk * P:(kk + 1) * P],
                                               w[:, kk * D + half * T:kk * D + (half + 1) * T],
                                               start=c == 0 and kk == 0, stop=c == STEPS - 1 and kk == 1)
                        mm.then_inc(used.sem, 1)
                        return mm
                    pe.wait_ge(ready.sem, ready.at(b + 1))
                    for c in range(STEPS):
                        if c >= 2:
                            pe.wait_ge(hidden.sem, hidden.at(STEPS * b + c - 1))
                        for part in range(2):
                            w = slab(MOE_ORDER.index((part, c)))
                            for k in range(KT):
                                mm = pe.matmul(self.bank[:, c % 2, part * FC:(part + 1) * FC], s.xt[:, k, :], w[:, k * FC:(k + 1) * FC],
                                               start=k == 0, stop=k == KT - 1)
                            mm.then_inc(used.sem, 1)
                        if c:
                            down(c - 1)
                    down(STEPS - 1)

            @block.scalar
            def _(act):
                with act.Fori(0, BLOCKS) as b:
                    def move(c):
                        act.wait_ge(turned.sem, turned.at(STEPS * b + c + 1))
                        act.activation(s.ht[:, c % 2, :], self.bank[:, 2 + c % 2, 0:FC], ACT.Copy).then_inc(moved.sem, 1)
                    for c in range(STEPS):
                        act.wait_ge(used.sem, used.at(MOE_SLABS * b + MOE_ORDER.index((1, c)) + 1))
                        act.activation(s.sg[:, c % 2, :], self.bank[:, c % 2, 0:FC], ACT.Silu).then_inc(lit.sem, 1)
                        if c:
                            move(c - 1)
                    move(STEPS - 1)
                    act.wait_ge(used.sem, used.at(MOE_SLABS * (b + 1)))
                    act.wait_ge(stored.sem, stored.at(16 * b))
                    act.activation(s.ys[:, 0:T], self.side[:, 0, :], ACT.Copy)
                    act.activation(s.ys[:, T:D], self.side[:, 1, :], ACT.Copy).then_inc(kept.sem, 1)
                    act.wait_ge(kept.sem, kept.at(b + 1))
                    act.dma_start(s.slots_y.rearrange("(b p) n -> b p n", p=P)[ds(b, 1)].rearrange("a p n -> (a p) n"), s.ys[:]).then_inc(stored.sem, 16)
                act.wait_ge(stored.sem, stored.at(16 * BLOCKS))

            @block.vector
            def _(dve):
                def turn_in(b):
                    dve.wait_ge(flipped.sem, flipped.at(b + 1))
                    dve.tensor_copy(s.xt[:].rearrange("p k n -> p (k n)"), self.side[:, 2:4, :].rearrange("p a n -> p (a n)")).then_inc(ready.sem, 1)
                turn_in(0)
                with dve.Fori(0, BLOCKS) as b:
                    for c in range(STEPS):
                        dve.wait_ge(lit.sem, lit.at(STEPS * b + c + 1))
                        dve.tensor_tensor(s.hidden[:, c % 2, :], self.bank[:, c % 2, FC:2 * FC], s.sg[:, c % 2, :], ALU.mult).then_inc(hidden.sem, 1)
                    turn_in(b + 1)
        n = BLOCKS
        used.close(MOE_SLABS * n)
        gathered.close(16 * (n + 1))
        numbered.close(n + 1)
        flipped.close(n + 1)
        ready.close(n + 1)
        for signal in (lit, hidden, turned, moved):
            signal.close(STEPS * n)
        kept.close(n)
        stored.close(16 * n)
        for signal in landed:
            signal.close(16 * n * (MOE_SLABS // MOE_SLOTS))

    def gather_experts(self, s):
        rows = [self.sig(f"row_landed{j}") for j in range(TOP2 * TT)]
        summed, scaled = self.sig("moe_summed"), self.sig("x_scaled")
        with self.nc.Block() as block:
            @block.gpsimd
            def _(pool):
                for t in range(TT):
                    for c in range(TOP2):
                        pool.indirect_dma_start(
                            out=s.rows[:, c * TT + t, :], out_offset=None, in_=s.slots_y,
                            in_offset=bass.IndirectOffsetOnAxis(ap=s.slot[:, c * TT + t:c * TT + t + 1], axis=0)).then_inc(rows[c * TT + t].sem, 16)

            @block.vector
            def _(dve):
                for t in range(TT):
                    dve.wait_ge(rows[t].sem, rows[t].at(16))
                    dve.tensor_scalar(s.y[:, t, :], s.rows[:, t, :], s.w[:, 0, t:t + 1], None, ALU.mult).then_inc(summed.sem, 1)
                    dve.wait_ge(rows[TT + t].sem, rows[TT + t].at(16))
                    dve.wait_ge(summed.sem, summed.at(2 * t + 1))
                    dve.scalar_tensor_tensor(s.y[:, t, :], s.rows[:, TT + t, :], s.w[:, 1, t:t + 1], s.y[:, t, :], ALU.mult, ALU.add).then_inc(summed.sem, 1)

            @block.scalar
            def _(act):
                act.activation(self.x[:], self.x[:], ACT.Copy, scale=ALPHA).then_inc(scaled.sem, 1)
        for signal in rows:
            signal.close(16)
        summed.close(2 * TT)
        scaled.close(1)

    def store(self, tile):
        done = self.sig("out_stored")
        with self.nc.Block() as block:
            @block.sync
            def _(sp):
                sp.dma_start(self.d["out"].rearrange("(t p) n -> p t n", p=P), tile[:]).then_inc(done.sem, 16)
                sp.wait_ge(done.sem, done.at(16))

    def build(self):
        nc, d = self.nc, self.d
        with self.ctx:
            self.stream = [d[n] for n in ("w_mod", "ada_0", "ada_1", "w_in", "w_conv_o", "w_attn_o", "w_out", "peer_wq",
                                          "w_in2_0", "w_out2_0", "ffn_up", "ffn_down", "w_in2_1", "w_out2_1")]
            self.slab_used = self.ctx.enter_context(nc.semaphore("slab_used"))
            self.taken = self.ctx.enter_context(nc.semaphore("bank_taken"))
            self.landed = [self.ctx.enter_context(nc.semaphore(f"slab_landed{j}")) for j in range(SLOTS)]
            psum = self.ps("psum", [P, 8, T])
            self.bank, self.side = psum[:, 0:4, :], psum[:, 4:8, :]
            self.x = self.sb("x", [P, KT, T])
            self.h = self.sb("h", [P, KT, T])
            self.squares = self.sb("squares", [P, KT, T])
            self.stat = self.sb("stat", [P, 2, T])
            self.ring = [self.sb(f"slab{j}", [P, HALF_FT * P]) for j in range(SLOTS)]
            self.consts = self.sb("consts_sb", [P, NCONST])
            self.vectors = self.sb("vectors_sb", [P, NVEC])
            self.small = self.sb("small_sb", [P, d["small"].shape[1]])
            self.mod = self.sb("mod", [P, NMOD, 2])
            self.mod2 = self.sb("mod2", [P, 2 * NMOD])
            self.cooked = self.sb("cooked", [P, 11, KT])
            self.cond = self.sb("cond_sb", [P, KT, 3])
            self.cond_s = self.sb("cond_s", [P, KT, 3])
            eps = self.sb("eps", [P, 3])
            self.one = eps[:, 2:3]
            self.eps = {EPS: eps[:, 0:1], LN_EPS: eps[:, 1:2]}
            with nc.Block() as block:
                @block.vector
                def _(dve):
                    dve.memset(eps[:, 0:1], EPS)
                    dve.memset(eps[:, 1:2], LN_EPS)
                    dve.memset(eps[:, 2:3], 1.0)

            def column(tile, *at):
                return lambda k: tile[(slice(None), *at, slice(k, k + 1))]

            def vec(name, layer=0):
                return lambda k: self.vectors[:, VECTORS[name][0] + layer * KT + k:VECTORS[name][0] + layer * KT + k + 1]

            def mod(part, who):
                return lambda k: self.mod[:, part * KT + k:part * KT + k + 1, who]

            def mod2(part, layer):
                return lambda k: self.mod2[:, layer * NMOD + part * KT + k:layer * NMOD + part * KT + k + 1]

            with ExitStack() as first:
                class s:
                    pass
                s.v = self.sb("v", [P, ST, KV_HEADS * P], scope=first)
                s.kc = self.sb("kc", [P, KV_HEADS, CTX], scope=first)
                s.qk = self.sb("qk", [P, HEADS + KV_HEADS, T], scope=first)
                s.gates = self.sb("gates", [P, 2 * KT, T], scope=first)
                s.conv = self.sb("conv", [P, KT, T], scope=first)
                with ExitStack() as inner:
                    self.ctx_in = self.sb("ctx_in", [P, KT, CTX], scope=inner)
                    self.hc = self.sb("hc", [P, KT, CTX], scope=inner)
                    s.ab = self.sb("ab", [P, 4, T], scope=inner)
                    s.gpad = self.sb("gpad", [P, 2, T + 2 * PAD], scope=inner)
                    self.load_and_modulate()
                    if self.stop == "mod":
                        return self.dump(self.mod2[:])
                    self.normalise(self.ctx_in, CTX, EPS, [(self.hc, ACT.Identity, column(self.cooked, 1), mod(0, 1))])
                    self.normalise(self.x, T, EPS, [(self.h, ACT.Identity, column(self.cooked, 0), mod(0, 0))])
                    if self.stop == "norm1":
                        return self.dump(self.h[:])
                    self.project(s)
                if self.stop == "conv":
                    return self.dump(s.conv[:])
                self.normalise(s.conv, T, EPS, [(self.h, ACT.Silu, vec("cln_g"), vec("cln_b"))], centre=True)
                self.conv_out(s)
                if self.stop == "conv_out":
                    return self.dump(s.gates[:])
                with ExitStack() as inner:
                    s.sq = self.sb("rot_sq", [P, 2, T], scope=inner)
                    s.root = self.sb("rot_root", [P, 2, T], scope=inner)
                    s.inv = self.sb("rot_inv", [P, 2, T], scope=inner)
                    s.nrm = self.sb("rot_nrm", [P, 2, T], scope=inner)
                    s.cosx = self.sb("rot_cosx", [P, 2, T], scope=inner)
                    s.sinx = self.sb("rot_sinx", [P, 2, T], scope=inner)
                    self.rotate(s)
                if self.stop == "rotate":
                    return self.dump(s.qk[:])
                with ExitStack() as inner:
                    s.o = s.conv
                    s.q = self.sb("q", [P, 2, T], scope=inner)
                    s.p = self.sb("p", [P, 2, SKV], scope=inner)
                    s.pt = self.sb("pt", [P, 2, ST, T], scope=inner)
                    s.top = self.sb("att_top", [P, 2 * TT], scope=inner)
                    s.bias = self.sb("att_bias", [P, 2 * TT], scope=inner)
                    s.total = self.sb("att_total", [P, 2 * TT], scope=inner)
                    s.recip = self.sb("att_recip", [P, 2 * TT], scope=inner)
                    self.attend(s)
                if self.stop == "attend":
                    return self.dump(s.o[:])
                self.mix_out(s)
                if self.stop == "mixed":
                    return self.dump(self.x[:])

            self.normalise(self.x, T, EPS, [(self.h, ACT.Identity, column(self.cooked, 2), mod(3, 0))])
            if self.stop == "h2":
                return self.dump(self.h[:])
            with ExitStack() as peer:
                class s:
                    pass
                s.expert = self.sb("expert", [P, TT, PSEL], U32, scope=peer)
                s.weight = self.sb("weight", [P, TT, PSEL], scope=peer)
                s.hn = self.sb("hn", [P, TT, D], scope=peer)
                s.y = self.sb("peer_y", [P, TT, D], scope=peer)
                with ExitStack() as inner:
                    s.keys = self.sb("keys", [P, 2 * PH, PKEYS], scope=inner)
                    s.pq = self.sb("pq", [P, 2, T], scope=inner)
                    s.sk = self.sb("sk", [P, 2, T], scope=inner)
                    s.val = self.sb("val", [P, TT, PTOP], scope=inner)
                    s.pos = self.sb("pos", [P, TT, PTOP], U32, scope=inner)
                    s.best = self.sb("best", [P, TT, 2 * PH, PTOP], scope=inner)
                    s.at = self.sb("at", [P, TT, 2 * PH, PTOP], U32, scope=inner)
                    s.cand = self.sb("cand", [P, PH * NCAND], scope=inner)
                    s.spare = self.sb("spare", [P, NCAND], scope=inner)
                    s.top = self.sb("top", [P, PH, PTOP], scope=inner)
                    s.place = self.sb("place", [P, PH, PTOP], U32, scope=inner)
                    s.which = self.sb("which", [P, PSEL], U32, scope=inner)
                    s.whichf = self.sb("whichf", [P, PSEL], scope=inner)
                    s.atf = self.sb("atf", [P, PH, PTOP], scope=inner)
                    s.key = self.sb("key", [P, 2, PSEL], scope=inner)
                    s.power = self.sb("power", [P, PH, PTOP], scope=inner)
                    s.wsum = self.sb("wsum", [P, PH], scope=inner)
                    s.mark = self.sb("mark", [P, 1], scope=inner)
                    self.flip_tiles(self.h, s.hn, True)
                    self.score_keys(s)
                    self.combine(s)
                if self.stop == "expert":
                    return self.dump(s.weight[:])
                with ExitStack() as inner:
                    s.row = self.sb("row", [P, 16, D], scope=inner)
                    s.index = self.sb("index", [P, 16], U32, scope=inner)
                    s.dot = self.sb("dot", [P, 16], scope=inner)
                    s.hcur = self.sb("hcur", [P, D], scope=inner)
                    s.acc = self.squares[:, 4:8, :].rearrange("p (a b) n -> p a (b n)", a=2)
                    s.act = self.sb("acts", [P, PSEL], scope=inner)
                    s.gelu = self.sb("gelu", [P, PSEL], scope=inner)
                    s.coef = self.sb("coef", [P, PSEL], scope=inner)
                    self.experts(s)
                if self.stop == "peer":
                    return self.dump(s.y[:])
                self.flip_tiles(s.y, None, False, after=lambda dve, k, t, at: dve.scalar_tensor_tensor(
                    self.x[:, k, t * P:(t + 1) * P], at, mod(5, 0)(k), self.x[:, k, t * P:(t + 1) * P], ALU.mult, ALU.add))
            self.normalise(self.x, T, EPS, [(self.x, ACT.Copy, vec("final"), None), (self.h, ACT.Identity, column(self.cooked, 3), mod2(0, 0))])
            if self.stop == "x1":
                return self.dump(self.x[:])
            if self.stop == "u0":
                return self.dump(self.h[:])

            for layer in range(2):
                with ExitStack() as scope:
                    class s:
                        pass
                    s.y = self.sb(f"y{layer}", [P, KT, T], scope=scope)
                    s.cch = self.sb(f"cch{layer}", [P, 2 * CONV2, T], scope=scope)
                    s.qk = self.sb(f"gqk{layer}", [P, 4, T], scope=scope)
                    s.v = self.sb(f"gv{layer}", [P, TT, GH, GDV], scope=scope)
                    s.gate = self.sb(f"ggate{layer}", [P, GH, T], scope=scope)
                    s.eb = self.sb(f"eb{layer}", [P, 2, T], scope=scope)
                    s.enb = self.sb(f"enb{layer}", [P, 2, T], scope=scope)
                    s.kout = self.sb(f"kout{layer}", [P, 2, T], scope=scope)
                    with ExitStack() as inner:
                        s.zpad = self.sb(f"zpad{layer}", [P, CONV2, T + 2], scope=inner)
                        s.cb = self.sb(f"cb{layer}", [P, CONV2, T], scope=inner)
                        s.low = self.sb(f"low{layer}", [16, T], scope=inner)
                        s.z = self.sb(f"z{layer}", [P, 2, T], scope=inner)
                        s.b = self.sb(f"b{layer}", [P, 2, T], scope=inner)
                        self.mix_in(s, layer)
                    with ExitStack() as inner:
                        s.kmask = s.cch[:, 0:4, :]
                        s.sq = s.cch[:, 4:8, :]
                        s.a = self.sb(f"a{layer}", [P, GH, T], scope=inner)
                        s.kon = self.squares[:, 0:4, :].rearrange("p (r a) n -> p r a n", r=2)
                        s.state = self.sb(f"state{layer}", [P, 2, NCH, 2 * GDV], scope=inner)
                        s.root = s.kmask
                        s.inv = self.stat[:, 0, :]
                        self.linear_attention(s, layer)
                    self.residual(s.y, lambda i: self.cooked[:, 4 + 4 * layer, ds(i, 1)])
                self.normalise(self.x, T, LN_EPS, [(self.x, ACT.Identity, vec("ln1_g", layer), vec("ln1_b", layer)),
                                                   (self.h, ACT.Identity, column(self.cooked, 5 + 4 * layer), mod2(3, layer))], centre=True)
                if self.stop == f"xa{layer}":
                    return self.dump(self.x[:])
                if self.stop == f"v{layer}":
                    return self.dump(self.h[:])
                gain = lambda i: self.cooked[:, 6 + 4 * layer, ds(i, 1)]
                if layer == 0:
                    with ExitStack() as scope:
                        class s:
                            pass
                        s.hidden = self.sb("hidden", [P, FT, T], scope=scope)
                        s.ab = self.sb("ffn_ab", [P, 4, T], scope=scope)
                        self.dense_up(s)
                        self.dense_down(s, gain)
                    self.normalise(self.x, T, LN_EPS, [(self.x, ACT.Identity, vec("ln2_g"), vec("ln2_b")),
                                                       (self.h, ACT.Identity, column(self.cooked, 7), mod2(0, 1))], centre=True)
                    if self.stop == "x2":
                        return self.dump(self.x[:])
                    if self.stop == "u1":
                        return self.dump(self.h[:])

            with ExitStack() as scope:
                class s:
                    pass
                s.owner = self.sb("moe_owner", [P, BLOCKS], I32, scope=scope)
                s.slot = self.sb("moe_slot", [P, TOP2 * TT], U32, scope=scope)
                s.w = self.sb("moe_w", [P, TOP2, TT], F32, scope=scope)
                s.slot_token = self.sb("moe_slot_token", [P, BLOCKS + 1], U32, scope=scope)
                s.tokens = nc.dram_tensor("token_rows", (T, D), F32, kind="Internal").ap()
                s.table = nc.dram_tensor("slot_table", ((BLOCKS + 1) * P, 1), U32, kind="Internal").ap()
                s.slots_y = nc.dram_tensor("slot_rows", (BLOCKS * P, D), F32, kind="Internal").ap()
                with ExitStack() as inner:
                    s.hn = self.sb("route_hn", [P, TT, D], F32, scope=inner)
                    s.logit = self.sb("route_logit", [P, TT, NE], F32, scope=inner)
                    s.best = self.sb("route_best", [P, TT, NE], F32, scope=inner)
                    s.place = self.sb("route_place", [P, TT, NE], U32, scope=inner)
                    s.choice = self.sb("route_choice", [P, TOP2, TT], F32, scope=inner)
                    s.hot = self.sb("route_hot", [P, TOP2, TT, NE], F32, scope=inner)
                    s.member = self.sb("route_member", [P, TT, NE], F32, scope=inner)
                    s.blocks = self.sb("route_blocks", [P, NE], F32, scope=inner)
                    s.end = self.sb("route_end", [P, NE], F32, scope=inner)
                    s.start = self.sb("route_start", [P, NE], F32, scope=inner)
                    s.where = self.sb("route_where", [P, TT, NE], F32, scope=inner)
                    s.slotf = self.sb("route_slotf", [P, TOP2 * TT], F32, scope=inner)
                    s.before = self.sb("route_before", [P, BLOCKS, NE], F32, scope=inner)
                    s.ownerf = self.sb("route_ownerf", [P, BLOCKS], F32, scope=inner)
                    s.zero = self.sb("route_zero", [P, BLOCKS + 1], U32, scope=inner)
                    s.token = self.sb("route_token", [P, TT], U32, scope=inner)
                    s.mark = self.sb("route_mark", [P, 1], F32, scope=inner)
                    s.mark2 = self.sb("route_mark2", [P, 1], F32, scope=inner)
                    self.flip_tiles(self.h, s.hn, True)
                    self.route(s)
                with ExitStack() as inner:
                    s.wring = self.sb("exp_wring", [P, MOE_SLOTS, KT * FC], F32, scope=inner)
                    s.xs = self.sb("exp_xs", [P, D], F32, scope=inner)
                    s.xt = self.sb("exp_xt", [P, KT, P], F32, scope=inner)
                    s.number = self.sb("exp_number", [P, 1], U32, scope=inner)
                    s.sg = self.sb("exp_sg", [P, 2, FC], F32, scope=inner)
                    s.hidden = self.sb("exp_hidden", [P, 2, FC], F32, scope=inner)
                    s.ht = self.sb("exp_ht", [P, 2, FC], F32, scope=inner)
                    s.ys = self.sb("exp_ys", [P, D], F32, scope=inner)
                    self.run_experts(s)
                s.rows = self.sb("expert_rows", [P, TOP2 * TT, D], scope=scope)
                s.y = self.sb("expert_y", [P, TT, D], scope=scope)
                self.gather_experts(s)
                self.flip_tiles(s.y, None, False, after=lambda dve, k, t, at: dve.scalar_tensor_tensor(
                    self.x[:, k, t * P:(t + 1) * P], at, self.cooked[:, 10, k:k + 1], self.x[:, k, t * P:(t + 1) * P], ALU.mult, ALU.add))
                self.normalise(self.x, T, LN_EPS, [(self.x, ACT.Identity, vec("ln2_g", 1), vec("ln2_b", 1))], centre=True)
                if self.stop == "x3":
                    return self.dump(self.x[:])
                self.flip_tiles(self.x, s.y, True)
                self.store(s.y)

    def dump(self, ap):
        nc = self.nc
        shape = list(ap.shape)
        out = nc.dram_tensor("dump", tuple(shape), F32, kind="ExternalOutput").ap()
        sem = self.ctx.enter_context(nc.semaphore("dumped"))
        with nc.Block() as block:
            @block.sync
            def _(sp):
                sp.dma_start(out, ap).then_inc(sem, 16)
                sp.wait_ge(sem, 16)


def _slabs(w, order=None):
    k, n = w.shape
    w = w.reshape(k // P, P, n // P, P).transpose(2, 1, 0, 3)
    if order is not None:
        w = w[order]
    return np.ascontiguousarray(w).reshape(-1, P, k)


def _tiles(v):
    return np.ascontiguousarray(v.reshape(-1, P).T)


def _channels(x):
    t, c = x.shape
    return np.ascontiguousarray(x.T.reshape(c // P, P, t).transpose(1, 0, 2))


def _consts():
    out = np.zeros((P, NCONST), np.float32)

    def put(name, value):
        at, w = CONSTS[name]
        out[:, at:at + w] = value
    i = np.arange(P)
    put("ident", np.eye(P))
    put("ones", 1.0)
    perm = np.zeros((P, P), np.float32)
    for m in range(P):
        if m % 64 < 32:
            perm[m + 32, m] = -1.0
        else:
            perm[m - 32, m] = 1.0
    put("perm", perm)
    put("causal", (i[:, None] <= i[None, :]) & (i[:, None] // GCH == i[None, :] // GCH))
    put("before", i[:, None] < i[None, :])
    put("pair", (i[:, None] // GDK) == (np.arange(2 * P)[None, :] // P))
    put("iota", i[None, :])
    t = np.arange(T)
    row, col = (t // 64).astype(np.float32), (t % 64).astype(np.float32)
    inv = (np.float32(10000.0) ** (-np.arange(0, 64, 2, dtype=np.float32) / np.float32(64))).astype(np.float32)
    angle = np.where((i < 64)[:, None], row[None, :], col[None, :]) * inv[i % 32][:, None]
    put("cos", np.cos(angle.astype(np.float32)))
    put("sin", np.sin(angle.astype(np.float32)))
    put("carry", np.broadcast_to(t % GCH != 0, (P, T)))
    put("half", (i[:, None] // GCH) == np.arange(2)[None, :])
    return out


def _inputs(a):
    x, ctx = a["x"][0], a["ctx"][0]
    vectors = {
        "b_mod": _tiles(a["b_mod"][0]), "norm1": _tiles(a["norm1_g"][0]), "norm2": _tiles(a["norm2_g"][0]),
        "final": _tiles(a["final_norm_g"]),
        "qk_gain": np.concatenate([np.repeat(_tiles(a["q_norm_g"][0]), HEADS, 1), np.repeat(_tiles(a["k_norm_g"][0]), KV_HEADS, 1)], 1),
        "k_gain": _tiles(a["k_norm_g"][0]),
        "conv_w": a["conv_dw"][0].reshape(TAPS, KT, P).transpose(2, 1, 0).reshape(P, -1),
        "conv_b": _tiles(a["conv_b"][0]), "cln_g": _tiles(a["conv_ln_g"][0]), "cln_b": _tiles(a["conv_ln_b"][0]),
        "ada_b": _tiles(a["ada_b_2"].reshape(-1)), "gk_b": _tiles(a["gk_b_2"].reshape(-1)),
        "ln1_g": _tiles(a["ln1_g_2"].reshape(-1)), "ln1_b": _tiles(a["ln1_b_2"].reshape(-1)),
        "ln2_g": _tiles(a["ln2_g_2"].reshape(-1)), "ln2_b": _tiles(a["ln2_b_2"].reshape(-1)),
        "gla_g": _tiles(a["gla_norm_w_2"].reshape(-1)),
        "conv2_w": a["conv_w_2"].reshape(2, TAPS2, CONV2, P).transpose(3, 0, 2, 1).reshape(P, -1),
    }
    packed = np.concatenate([np.asarray(vectors[n]).reshape(P, VECTORS[n][1]) for n in VECTORS], 1)
    low = a["w_in_2"][:, :, 24 * P:].reshape(2, KT, P, 16).transpose(2, 0, 1, 3).reshape(P, -1)
    router = a["router_w_2"][0].reshape(KT, P, NE).transpose(1, 0, 2).reshape(P, -1)
    gk = np.zeros((P, 2 * 2 * P), np.float32)
    gk[0:16] = a["gk_w2_2"].transpose(1, 0, 2).reshape(16, -1)
    gate = a["ffn_w_gate_2"][0].reshape(D, FT, 1, P)
    up = a["ffn_w_up_2"][0].reshape(D, FT, 1, P)
    down = a["ffn_w_down_2"][0].reshape(2, HALF_FT, P, KT, P).transpose(3, 0, 2, 1, 4)
    parts = [w.reshape(NE, KT, P, STEPS, FC).transpose(3, 0, 2, 1, 4).reshape(STEPS, NE, P, KT * FC)
             for w in (a["moe_w_gate_2"][0], a["moe_w_up_2"][0])]
    parts.append(a["moe_w_down_2"][0].reshape(NE, STEPS, 2, P, D).transpose(1, 0, 3, 2, 4).reshape(STEPS, NE, P, 2 * D))
    moe = np.stack([parts[part][c] for part, c in MOE_ORDER], 1)
    return {
        "x": _channels(x), "ctx": _channels(ctx), "consts": _consts(),
        "cond": np.stack([_tiles(a["c"][0]), _tiles(a["c_ctx"]), _tiles(a["c_2"][0])], 2),
        "vectors": packed, "small": np.concatenate([low, router, gk], 1),
        "w_mod": _slabs(a["w_mod"][0]), "ada_0": _slabs(a["ada_w_2"][0]), "ada_1": _slabs(a["ada_w_2"][1]),
        "w_in": _slabs(a["w_in"][0], W_IN_ORDER), "w_conv_o": _slabs(a["w_conv_o"][0]),
        "w_attn_o": _slabs(a["w_attn_o"][0]), "w_out": _slabs(a["w_out"][0]), "peer_wq": _slabs(a["peer_wq"][0]),
        "w_in2_0": _slabs(a["w_in_2"][0][:, 0:24 * P], W_IN2_ORDER), "w_in2_1": _slabs(a["w_in_2"][1][:, 0:24 * P], W_IN2_ORDER),
        "w_out2_0": _slabs(a["w_out_2"][0]), "w_out2_1": _slabs(a["w_out_2"][1]),
        "ffn_up": _slabs(np.concatenate([gate, up], 2).reshape(D, 2 * FF)),
        "ffn_down": np.ascontiguousarray(down).reshape(2 * KT, P, HALF_FT * P),
        "keys": np.ascontiguousarray(a["peer_keys"][0].reshape(2 * PH, PKEYS, P).transpose(2, 0, 1)),
        "peer_u": a["peer_u"][0], "peer_v": a["peer_v"][0],
        "moe": moe,
    }


def kernel(stop=None, **inputs):
    import concourse.bacc as bacc
    from concourse.bass_utils import run_bass_kernel_spmd as run

    arrays = {f"in_{k}": np.ascontiguousarray(v) for k, v in _inputs({k: np.asarray(v) for k, v in inputs.items()}).items()}
    nc = bacc.Bacc("TRN2", target_bir_lowering=False, num_devices=1)
    d = {k[3:]: nc.dram_tensor(k, v.shape, F32, kind="ExternalInput").ap() for k, v in arrays.items()}
    if stop is None:
        d["out"] = nc.dram_tensor("out", (T, D), F32, kind="ExternalOutput").ap()
    Program(nc, d, stop).build()
    r = run(nc, [arrays], core_ids=[0])
    return r.results[0]["out"].reshape(1, T, D)
```

```python
from contextlib import ExitStack, contextmanager

import numpy as np

import concourse.bass as bass
from concourse import mybir

F32 = mybir.dt.float32
U32 = mybir.dt.uint32
I32 = mybir.dt.int32
F32R = mybir.dt.float32r
ACT = mybir.ActivationFunctionType
ALU = mybir.AluOpType
AX = mybir.AxisListType
ds = bass.ds

P = 128
D = 1024
KT = D // P
T = 512
TT = T // P
CTX = 256
SKV = T + CTX
ST = SKV // P
HEADS, KV_HEADS = 8, 2
GROUP = HEADS // KV_HEADS
NMOD = 6 * KT
TAPS = 31
PAD = TAPS // 2
PH, PTOP, PKEYS = 8, 16, 128
NCAND = PTOP * PTOP
PSEL = PH * PTOP
GH, GDK, GDV, GCH = 4, 64, 128, 64
NCH = T // GCH
CONV2 = 4
TAPS2 = 3
FF = 2816
FT = FF // P
NE = 8
EPS, LN_EPS = 1e-6, 1e-5
ALPHA = 4.0 ** 0.25
SLOTS = 4
TOP2 = 2
BLOCKS = (TOP2 * T) // P + NE - 1
FC = 2 * P
STEPS = FF // FC
HALF_FT = FT // 2
LOW = -3.0e38
ROWS = 16
GROUPS = PSEL // ROWS
DIAGS = 4
SELECT = 25

W_IN_ORDER = [8, 9, 10, 11] + [t for c in range(8) for t in (20 + c, 12 + c)] + list(range(8)) + list(range(28, 44))
W_IN2_ORDER = [t for c in range(4) for t in (4 + c, 8 + c)] + list(range(4)) + list(range(12, 24))
MOE_ORDER = [(0, 0), (1, 0)] + [x for c in range(1, STEPS) for x in ((0, c), (1, c), (2, c - 1))] + [(2, STEPS - 1)]
MOE_SLABS = len(MOE_ORDER)
ROUNDED = 3
AHEAD = 2
MOE_SLOTS = STEPS

VECTORS = {}


def _vector_columns():
    at = 0
    for name, width in (
        ("b_mod", NMOD), ("norm1", KT), ("norm2", KT), ("final", KT), ("qk_gain", HEADS + KV_HEADS),
        ("k_gain", 1), ("conv_w", KT * TAPS), ("conv_b", KT), ("cln_g", KT), ("cln_b", KT),
        ("ada_b", 2 * NMOD), ("ln1_g", 2 * KT), ("ln1_b", 2 * KT), ("ln2_g", 2 * KT), ("ln2_b", 2 * KT),
        ("gk_b", 2 * 2), ("gla_g", 2), ("conv2_w", 2 * CONV2 * TAPS2),
    ):
        VECTORS[name] = (at, width)
        at += width
    return at


NVEC = _vector_columns()

CONSTS = {}


def _const_columns():
    at = 0
    for name, width in (("ident", P), ("ones", P), ("perm", P), ("causal", P), ("before", P),
                        ("pair", 2 * P), ("iota", P), ("cos", T), ("sin", T), ("carry", T), ("half", 2)):
        CONSTS[name] = (at, width)
        at += width
    return at


NCONST = _const_columns()


class Signal:

    def __init__(self, sem):
        self.sem, self.base = sem, 0

    def at(self, n):
        return self.base + n

    def close(self, n):
        self.base += n


@contextmanager
def repeat(eng, n):
    if n == 1:
        yield 0
    else:
        with eng.Fori(0, n) as i:
            yield i


class Program:
    def __init__(self, nc, d, stop=None):
        self.nc, self.d, self.stop = nc, d, stop
        self.ctx = ExitStack()
        self.signals = {}
        self.issued = 0
        self.used = 0

    def sb(self, name, shape, dt=F32, scope=None):
        return (scope or self.ctx).enter_context(self.nc.sbuf_tensor(name, shape, dt))

    def ps(self, name, shape, dt=F32):
        return self.ctx.enter_context(self.nc.psum_tensor(name, shape, dt))

    def sig(self, name):
        if name not in self.signals:
            self.signals[name] = Signal(self.ctx.enter_context(self.nc.semaphore(name)))
        return self.signals[name]

    def vec(self, name, i=0, n=1):
        at, _ = VECTORS[name]
        return self.vectors[:, ds(at + i, n)]

    def const(self, name, rows=P, a=0, b=None):
        at, w = CONSTS[name]
        return self.consts[0:rows, at + a:at + (w if b is None else b)]

    def issue(self, sp, upto):
        upto = min(upto, sum(ap.shape[0] for ap in self.stream))
        while self.issued < upto:
            at = 0
            for ap in self.stream:
                if self.issued < at + ap.shape[0]:
                    break
                at += ap.shape[0]
            n = min(upto, at + ap.shape[0]) - self.issued
            first, index = self.issued, self.issued - at
            width = ap.shape[2]

            def group(turn):
                for j in range(SLOTS):
                    free = first + SLOTS * turn + j - SLOTS + 1
                    if not (isinstance(free, int) and free <= 0):
                        sp.wait_ge(self.slab_used, free)
                    sp.dma_start(self.ring[j][:, 0:width], ap[ds(index + SLOTS * turn + j, 1)].rearrange("a p n -> (a p) n")
                                 ).then_inc(self.landed[j], 16)

            turns = n // SLOTS
            assert turns * SLOTS == n
            done = 0
            if first == 0:
                group(0)
                done = 1
            if turns - done > 1:
                with sp.Fori(done, turns) as turn:
                    group(turn)
            elif turns - done == 1:
                group(done)
            self.issued += n

    def slabs(self, pe, first, n, product, every=1):
        first += self.used

        def group(turn):
            for j in range(SLOTS):
                pe.wait_ge(self.landed[j], 16 * (first // SLOTS + 1) + 16 * turn)
                taken = first + SLOTS * turn + j - SLOTS + 1
                if not (isinstance(taken, int) and taken <= 0):
                    pe.wait_ge(self.taken, taken)
                product(j, SLOTS * turn + j).then_inc(self.slab_used, 1)

        turns = n // SLOTS
        assert first % SLOTS == 0 and turns * SLOTS == n
        done = 0
        if first == 0:
            group(0)
            done = 1
        if turns - done > 1:
            with pe.Fori(done, turns) as turn:
                group(turn)
        elif turns - done == 1:
            group(done)

    def take(self, eng, first, n, out_of_bank, width=SLOTS):
        first += self.used
        with repeat(eng, n // width) as turn:
            for j in range(width):
                eng.wait_ge(self.slab_used, first + width * turn + j + 1)
                out_of_bank(self.bank[:, (first + j) % SLOTS, :], width * turn + j).then_inc(self.taken, 1)

    def wslab(self, slot, k):
        return self.ring[slot][:, k * P:(k + 1) * P]

    def linear(self, pe, src):
        def product(slot, index):
            for k in range(KT):
                mm = pe.matmul(self.bank[:, slot, :], self.wslab(slot, k), src[:, k, :], start=k == 0, stop=k == KT - 1)
            return mm
        return product

    def natural(self, pe, src, slot, out, tiles):
        for t in range(tiles):
            for k in range(KT):
                mm = pe.matmul(out[:, t * P:(t + 1) * P], src[:, k, t * P:(t + 1) * P], self.wslab(slot, k),
                               start=k == 0, stop=k == KT - 1)
        return mm

    def normalise(self, src, width, eps, outs, centre=False, also=None):
        nc, squares = self.nc, self.squares
        squared, summed, rooted, inverted = (self.sig(n) for n in ("squared", "summed", "rooted", "inverted"))
        centred, averaged, scaled, normed = (self.sig(n) for n in ("centred", "averaged", "scaled", "normed"))
        total = self.side[:, 0, 0:width]
        mean = self.side[:, 1, 0:width]
        root, inv = self.stat[:, 0, 0:width], self.stat[:, 1, 0:width]
        ones = self.const("ones")
        with nc.Block() as block:
            if also is not None:
                block.sync(also[0])

            @block.scalar
            def _(act):
                for k in range(KT):
                    if centre:
                        act.wait_ge(centred.sem, centred.at(k + 1))
                    act.activation(squares[:, k, 0:width], src[:, k, 0:width], ACT.Square).then_inc(squared.sem, 1)
                act.wait_ge(summed.sem, summed.at(1))
                act.activation(root, total, ACT.Sqrt, bias=self.eps[eps], scale=1.0 / D).then_inc(rooted.sem, 1)
                for k in range(KT):
                    act.wait_ge(scaled.sem, scaled.at(k + 1))
                    for n, (dst, func, scale, bias) in enumerate(outs):
                        at = squares[:, k, 0:width]
                        if n == 1:
                            act.wait_ge(normed.sem, normed.at(2 * k + 1))
                            at = outs[0][0][:, k, 0:width]
                        if bias is None:
                            act.activation(dst[:, k, 0:width], at, ACT.Copy, scale=scale(k)).then_inc(normed.sem, 1)
                        else:
                            act.activation(dst[:, k, 0:width], at, func, scale=scale(k), bias=bias(k)).then_inc(normed.sem, 1)

            @block.vector
            def _(dve):
                if centre:
                    dve.wait_ge(averaged.sem, averaged.at(1))
                    for k in range(KT):
                        dve.scalar_tensor_tensor(src[:, k, 0:width], mean, -1.0 / D, src[:, k, 0:width],
                                                            ALU.mult, ALU.add).then_inc(centred.sem, 1)
                dve.wait_ge(rooted.sem, rooted.at(1))
                dve.reciprocal(inv, root).then_inc(inverted.sem, 1)
                dve.wait_ge(inverted.sem, inverted.at(1))
                for k in range(KT):
                    dve.tensor_tensor(squares[:, k, 0:width], src[:, k, 0:width], inv, ALU.mult).then_inc(scaled.sem, 1)
                if also is not None:
                    also[2](dve)

            @block.tensor
            def _(pe):
                if centre:
                    for k in range(KT):
                        mm = pe.matmul(mean, ones, src[:, k, 0:width], start=k == 0, stop=k == KT - 1)
                    mm.then_inc(averaged.sem, 1)
                if also is not None:
                    also[1](pe)
                for k in range(KT):
                    pe.wait_ge(squared.sem, squared.at(k + 1))
                    mm = pe.matmul(total, ones, squares[:, k, 0:width], start=k == 0, stop=k == KT - 1)
                mm.then_inc(summed.sem, 1)
        squared.close(KT)
        summed.close(1)
        rooted.close(1)
        inverted.close(1)
        scaled.close(KT)
        normed.close(KT * len(outs))
        if centre:
            centred.close(KT)
            averaged.close(1)

    def modulate_slabs(self, pe, first, n, column, who):
        first += self.used
        a, b = who

        def product(j, at, turn):
            pe.wait_ge(self.landed[j], 16 * (first // SLOTS + 1) + 16 * turn)
            for k in range(KT):
                mm = pe.matmul(self.side[:, 2, at], self.wslab(j, k), self.cond_s[:, k, a:b], start=k == 0, stop=k == KT - 1)
            mm.then_inc(self.slab_used, 1)
        assert first % SLOTS == 0 and n % SLOTS == 0
        for i in range(n):
            at = column + (b - a) * i
            product(i % SLOTS, slice(at, at + b - a), i // SLOTS)

    def modulation(self, dve, first, n, column):
        out = self.mod[:, column:column + n, :]
        dve.wait_ge(self.slab_used, self.used + first + n)
        dve.tensor_tensor(out, self.side[:, 2, 2 * column:2 * (column + n)].rearrange("p (a c) -> p a c", c=2),
                          self.vec("b_mod", column, n).unsqueeze(2).to_broadcast([P, n, 2]), ALU.add).then_inc(self.taken, n)

    def gain_of(self, dve, row, at, name):
        cooked = self.sig("cooked")
        dve.scalar_tensor_tensor(self.cooked[:, row, :], at, 1.0, self.vec(name, 0, KT), ALU.add, ALU.mult).then_inc(cooked.sem, 1)

    def load_and_modulate(self):
        nc, d = self.nc, self.d
        loaded, ready, cooked = self.sig("loaded"), self.sig("cond_ready"), self.sig("cooked")
        with nc.Block() as block:
            @block.sync
            def _(sp):
                sp.dma_start(self.cond[:], d["cond"]).then_inc(self.sig("cond_loaded").sem, 16)
                self.issue(sp, 2 * KT + SLOTS)

            @block.scalar
            def _(act):
                act.wait_ge(self.sig("cond_loaded").sem, self.sig("cond_loaded").at(16))
                act.activation(self.cond_s[:], self.cond[:], ACT.Silu).then_inc(ready.sem, 1)
                for dst, src in ((self.vectors, d["vectors"]), (self.consts, d["consts"]), (self.small, d["small"])):
                    act.dma_start(dst[:], src).then_inc(loaded.sem, 16)
                act.dma_start(self.ctx_in[:], d["ctx"]).then_inc(self.sig("x_loaded").sem, 16)
                act.dma_start(self.x[:], d["x"]).then_inc(self.sig("x_loaded").sem, 16)
                act.wait_ge(self.sig("x_loaded").sem, self.sig("x_loaded").at(32))

            @block.tensor
            def _(pe):
                pe.wait_ge(ready.sem, ready.at(1))
                self.modulate_slabs(pe, 0, 2 * KT, 0, (0, 2))

            @block.vector
            def _(dve):
                dve.wait_ge(loaded.sem, loaded.at(48))
                self.modulation(dve, 0, 2 * KT, 0)
                dve.wait_ge(self.taken, 2 * KT)
                self.gain_of(dve, 0, self.mod[:, KT:2 * KT, 0], "norm1")
                self.gain_of(dve, 1, self.mod[:, KT:2 * KT, 1], "norm1")
        cooked.close(2)
        self.used += 2 * KT

    def conv_norm(self, s, gain, bias):
        self.normalise(s.conv, T, EPS, [(self.h, ACT.Silu, gain, bias)], centre=True, also=(
            lambda sp, upto=self.used + KT + SLOTS: self.issue(sp, upto),
            lambda pe: self.modulate_slabs(pe, 0, KT, 4 * KT, (0, 2)),
            lambda dve: self.modulation(dve, 0, KT, 2 * KT)))
        self.used += KT

    def project(self, s):
        nc = self.nc
        free, tapped = self.sig("gate_slot_free"), self.sig("tapped")
        side_ready, side_taken = self.sig("side_ready"), self.sig("side_taken")
        base = self.used
        with nc.Block() as block:
            @block.sync
            def _(sp):
                self.issue(sp, base + 44 + SLOTS)

            @block.tensor
            def _(pe):
                def kv(slot, index):
                    side = self.side[:, slot, :]
                    if slot < 2:
                        for k in range(KT):
                            mm = pe.matmul(side[:, 0:CTX], self.wslab(slot, k), self.hc[:, k, :], start=k == 0, stop=k == KT - 1)
                        mm.then_inc(side_ready.sem, 1)
                        return self.linear(pe, self.h)(slot, index)
                    self.natural(pe, self.hc, slot, side, CTX // P).then_inc(side_ready.sem, 1)
                    return self.natural(pe, self.h, slot, self.bank[:, slot, :], TT)
                self.slabs(pe, 0, 4, kv)
                self.slabs(pe, 4, 40, self.linear(pe, self.h))

            @block.scalar
            def _(act):
                def kv(bank, i):
                    act.wait_ge(side_ready.sem, side_ready.at(i + 1))
                    if i < 2:
                        act.activation(s.kc[:, i, :], self.side[:, i, 0:CTX], ACT.Copy)
                        return act.activation(s.qk[:, HEADS + i, :], bank, ACT.Copy)
                    g = slice((i - 2) * P, (i - 1) * P)
                    act.activation(s.v[:, TT:ST, g], self.side[:, i, 0:CTX].rearrange("p (a c) -> p a c", c=P), ACT.Copy)
                    return act.activation(s.v[:, 0:TT, g], bank.rearrange("p (a c) -> p a c", c=P), ACT.Copy)
                self.take(act, 0, 4, kv)
                with act.Fori(0, KT // 2) as turn:
                    for j in range(2):
                        for half in range(2):
                            act.wait_ge(self.slab_used, base + 5 + 4 * turn + 2 * j + half)
                            n = 2 * j + half
                            if half == 0:
                                act.wait_ge(free.sem, free.at(2 * turn + j + 1))
                            act.activation(s.ab[:, n, :], self.bank[:, n, :], ACT.Sigmoid if half == 0 else ACT.Copy
                                           ).then_inc(self.taken, 1)
                self.take(act, 20, HEADS, lambda bank, i: act.activation(s.qk[:, ds(i, 1), :].rearrange("p a t -> p (a t)"), bank, ACT.Copy))
                self.take(act, 28, 16, lambda bank, i: act.activation(s.gates[:, ds(i, 1), :].rearrange("p a t -> p (a t)"), bank, ACT.Sigmoid))

            @block.vector
            def _(dve):
                dve.memset(s.gpad[:], 0.0).then_inc(free.sem, 2)
                dve.wait_ge(free.sem, free.at(2))
                with dve.Fori(0, KT // 2) as turn:
                    for j in range(2):
                        c = 2 * turn + j
                        dve.wait_ge(self.taken, base + 4 + 2 * c + 2)
                        gp = s.gpad[:, j, :]
                        dve.tensor_tensor(gp[:, PAD:PAD + T], s.ab[:, 2 * j, :], s.ab[:, 2 * j + 1, :], ALU.mult).then_inc(free.sem, 1)
                        dve.wait_ge(free.sem, free.at(c + 3))
                        out = s.conv[:, ds(c, 1), :].rearrange("p a t -> p (a t)")
                        dve.tensor_scalar(out, gp[:, 0:T], self.vec("conv_w", TAPS * c), self.vec("conv_b", c), ALU.mult, ALU.add).then_inc(tapped.sem, 1)
                        for tap in range(1, TAPS):
                            dve.wait_ge(tapped.sem, tapped.at(TAPS * c + tap))
                            dve.scalar_tensor_tensor(out, gp[:, tap:tap + T], self.vec("conv_w", TAPS * c + tap), out,
                                                               ALU.mult, ALU.add).then_inc(tapped.sem, 1)
        side_ready.close(4)
        free.close(KT + 2)
        tapped.close(TAPS * KT)
        self.used += 44

    def conv_out(self, s):
        base = self.used
        with self.nc.Block() as block:
            @block.sync
            def _(sp):
                self.issue(sp, base + KT + SLOTS)

            @block.tensor
            def _(pe):
                self.slabs(pe, 0, KT, self.linear(pe, self.h))

            @block.vector
            def _(dve):
                def gate(bank, i):
                    at = s.gates[:, ds(KT + i, 1), :].rearrange("p a t -> p (a t)")
                    return dve.tensor_tensor(at, bank, at, ALU.mult)
                self.take(dve, 0, KT, gate)
        self.used += KT

    def rotate(self, s):
        sig = self.sig
        squared, summed, rooted, inverted = sig("h_squared"), sig("h_summed"), sig("h_rooted"), sig("h_inverted")
        normed, turned, products, rotated = sig("h_normed"), sig("h_turned"), sig("h_products"), sig("h_rotated")
        units = HEADS + KV_HEADS

        def unit_src(u):
            return s.kc[:].rearrange("p a t -> p (a t)") if u is None else s.qk[:, ds(u, 1), :].rearrange("p a t -> p (a t)")

        base = self.used
        slabs = 3 * KT
        turns = units // 2
        assert slabs == SLOTS * (turns + 1)

        with self.nc.Block() as block:
            @block.sync
            def _(sp):
                self.issue(sp, base + slabs + SLOTS)

            @block.scalar
            def _(act):
                def unit(u, j, n):
                    act.activation(s.sq[:, j, :], unit_src(u), ACT.Square).then_inc(squared.sem, 1)
                    act.wait_ge(summed.sem, summed.at(n + 1))
                    act.activation(s.root[:, j, :], self.bank[:, j, :], ACT.Sqrt, bias=self.eps[EPS], scale=1.0 / P).then_inc(rooted.sem, 1)
                with act.Fori(0, units // 2) as turn:
                    for j in range(2):
                        unit(2 * turn + j, j, 2 * turn + j)
                unit(None, 0, units)

            @block.tensor
            def _(pe):
                def total(j, n):
                    pe.wait_ge(squared.sem, squared.at(n + 1))
                    pe.matmul(self.bank[:, j, :], self.const("ones"), s.sq[:, j, :], start=True, stop=True).then_inc(summed.sem, 1)

                def modulate(turn, j):
                    pe.wait_ge(self.landed[j], 16 * (base // SLOTS + 1) + 16 * turn)
                    for k in range(KT):
                        mm = pe.matmul(self.side[:, 2, ds(6 * KT + 2 * SLOTS * turn + 2 * j, 2)], self.wslab(j, k), self.cond_s[:, k, 0:2],
                                       start=k == 0, stop=k == KT - 1)
                    mm.then_inc(self.slab_used, 1)
                total(0, 0)
                with pe.Fori(0, turns) as turn:
                    for j in range(2):
                        n = 2 * turn + j
                        total(1 - j, n + 1)
                        modulate(turn, 2 * j)
                        pe.wait_ge(normed.sem, normed.at(n + 1))
                        pe.matmul(self.side[:, j, :], self.const("perm"), s.nrm[:, j, :], start=True, stop=True).then_inc(turned.sem, 1)
                        modulate(turn, 2 * j + 1)
                for j in range(SLOTS):
                    modulate(turns, j)

            @block.vector
            def _(dve):
                def unit(u, j, n, gain, out):
                    dve.wait_ge(rooted.sem, rooted.at(n + 1))
                    dve.reciprocal(s.inv[:, j, :], s.root[:, j, :]).then_inc(inverted.sem, 1)
                    dve.wait_ge(inverted.sem, inverted.at(n + 1))
                    dve.scalar_tensor_tensor(out, unit_src(u), gain, s.inv[:, j, :], ALU.mult, ALU.mult).then_inc(normed.sem, 1)
                with dve.Fori(0, units // 2) as turn:
                    for j in range(2):
                        n = 2 * turn + j
                        unit(n, j, n, self.vec("qk_gain", n), s.nrm[:, j, :])
                        dve.wait_ge(normed.sem, normed.at(n + 1))
                        dve.tensor_tensor(s.cosx[:, j, :], s.nrm[:, j, :], self.const("cos"), ALU.mult).then_inc(products.sem, 1)
                        dve.wait_ge(turned.sem, turned.at(n + 1))
                        dve.tensor_tensor(s.sinx[:, j, :], self.side[:, j, :], self.const("sin"), ALU.mult).then_inc(products.sem, 1)
                        dve.wait_ge(products.sem, products.at(2 * n + 2))
                        dve.tensor_tensor(unit_src(n), s.cosx[:, j, :], s.sinx[:, j, :], ALU.add).then_inc(rotated.sem, 1)
                unit(None, 0, units, self.vec("k_gain"), unit_src(None))
                self.modulation(dve, 0, slabs, 3 * KT)
                dve.wait_ge(self.taken, base + slabs)
                self.gain_of(dve, 2, self.mod[:, 4 * KT:5 * KT, 0], "norm2")
        squared.close(units + 1)
        summed.close(units + 1)
        rooted.close(units + 1)
        inverted.close(units + 1)
        normed.close(units + 1)
        turned.close(units)
        products.close(2 * units)
        rotated.close(units)
        sig("cooked").close(1)
        self.used += slabs

    def attend(self, s):
        sig = self.sig
        staged, scored, topped, biased = sig("q_staged"), sig("scored"), sig("topped"), sig("biased")
        powered, inverse, probable = sig("powered"), sig("inverse"), sig("probable")
        flipped, moved_a, moved_b = sig("flipped"), sig("moved_a"), sig("moved_b")
        weighted, kept = sig("weighted"), sig("kept")
        scale = float(P) ** -0.5
        PAIRS = HEADS // 2
        TILES = 2 * TT

        def scores(i):
            return self.bank[:, 2 * (i % 2):2 * (i % 2) + 2, :].rearrange("p a n -> p (a n)")[:, 0:SKV]

        def flips(half):
            return self.side[:, half, :].rearrange("p (a n) -> p a n", n=P)

        with self.nc.Block() as block:
            @block.gpsimd
            def _(pool):
                def stage(pair, j):
                    pool.tensor_copy(s.q[:, j, :], s.qk[:, ds(2 * pair + j, 1), :].rearrange("p a t -> p (a t)")).then_inc(staged.sem, 1)
                for j in range(2):
                    stage(0, j)
                with pool.Fori(1, PAIRS) as pair:
                    for j in range(2):
                        pool.wait_ge(scored.sem, scored.at(TT * (2 * pair + j - 1)))
                        stage(pair, j)

            @block.tensor
            def _(pe):
                for g in range(KV_HEADS):
                    with pe.Fori(0, PAIRS // KV_HEADS) as p:
                        pair = p + g * (PAIRS // KV_HEADS)

                        def score(i):
                            j, qt = divmod(i, TT)
                            if qt == 0:
                                pe.wait_ge(staged.sem, staged.at(2 * pair + j + 1))
                            if i >= 2:
                                pe.wait_ge(powered.sem, powered.at(TILES * pair + i - 1))
                            at, q = scores(i), s.q[:, j, qt * P:(qt + 1) * P]
                            pe.matmul(at[:, 0:T], q, s.qk[:, HEADS + g, :], start=True, stop=True)
                            pe.matmul(at[:, T:SKV], q, s.kc[:, g, :], start=True, stop=True).then_inc(scored.sem, 1)

                        def flip(i):
                            pe.wait_ge(probable.sem, probable.at(TILES * pair + i + 1))
                            if i >= 1:
                                pe.wait_ge(moved_a.sem, moved_a.at(TILES * pair + i))
                                pe.wait_ge(moved_b.sem, moved_b.at(TILES * pair + i))
                            for st in range(ST):
                                mm = pe.transpose(flips(st // 4)[:, st % 4, :], s.p[:, i % 2, st * P:(st + 1) * P], self.const("ident"))
                            mm.then_inc(flipped.sem, 1)

                        def weigh(j):
                            pe.wait_ge(moved_a.sem, moved_a.at(TILES * pair + TT * (j + 1)))
                            pe.wait_ge(moved_b.sem, moved_b.at(TILES * pair + TT * (j + 1)))
                            for st in range(ST):
                                mm = pe.matmul(self.side[:, 2 + j, :], s.v[:, st, g * P:(g + 1) * P], s.pt[:, j, st, :],
                                               start=st == 0, stop=st == ST - 1)
                            mm.then_inc(weighted.sem, 1)
                        score(0)
                        for i in range(TILES):
                            if i + 1 < TILES:
                                score(i + 1)
                            flip(i)
                            if i == TT:
                                weigh(0)
                        weigh(1)
                        pe.wait_ge(kept.sem, kept.at(2 * pair + 2))

            @block.scalar
            def _(act):
                with act.Fori(0, PAIRS) as pair:
                    def exponentials(i):
                        act.wait_ge(biased.sem, biased.at(TILES * pair + i + 1))
                        act.activation(s.p[:, i % 2, :], scores(i), ACT.Exp, bias=s.bias[:, i:i + 1], scale=scale,
                                                  accum_out=s.total[:, i:i + 1]).then_inc(powered.sem, 1)

                    def move(i):
                        act.wait_ge(flipped.sem, flipped.at(TILES * pair + i + 1))
                        j, qt = divmod(i, TT)
                        act.activation(s.pt[:, j, 0:4, qt * P:(qt + 1) * P], flips(0), ACT.Copy).then_inc(moved_a.sem, 1)
                    for i in range(TILES):
                        exponentials(i)
                        if i >= 1:
                            move(i - 1)
                        if i == TT + 2:
                            act.wait_ge(weighted.sem, weighted.at(2 * pair + 1))
                            act.activation(s.o[:, ds(2 * pair, 1), :].rearrange("p a t -> p (a t)"), self.side[:, 2, :], ACT.Copy).then_inc(kept.sem, 1)
                    move(TILES - 1)
                    act.wait_ge(weighted.sem, weighted.at(2 * pair + 2))
                    act.activation(s.o[:, ds(2 * pair + 1, 1), :].rearrange("p a t -> p (a t)"), self.side[:, 3, :], ACT.Copy).then_inc(kept.sem, 1)

            @block.vector
            def _(dve):
                with dve.Fori(0, PAIRS) as pair:
                    def top(i):
                        dve.wait_ge(scored.sem, scored.at(TILES * pair + i + 1))
                        instruction = dve.tensor_reduce(s.top[:, i:i + 1], scores(i), AX.X, ALU.max)
                        instruction.then_inc(topped.sem, 1)
                        dve.wait_ge(topped.sem, topped.at(TILES * pair + i + 1))
                        dve.tensor_scalar(s.bias[:, i:i + 1], s.top[:, i:i + 1], -scale, None, ALU.mult).then_inc(biased.sem, 1)

                    def normal(i):
                        dve.wait_ge(powered.sem, powered.at(TILES * pair + i + 1))
                        dve.reciprocal(s.recip[:, i:i + 1], s.total[:, i:i + 1]).then_inc(inverse.sem, 1)
                        dve.wait_ge(inverse.sem, inverse.at(TILES * pair + i + 1))
                        dve.tensor_scalar(s.p[:, i % 2, :], s.p[:, i % 2, :], s.recip[:, i:i + 1], None, ALU.mult).then_inc(probable.sem, 1)

                    def move(i):
                        dve.wait_ge(flipped.sem, flipped.at(TILES * pair + i + 1))
                        j, qt = divmod(i, TT)
                        dve.tensor_copy(s.pt[:, j, 4:ST, qt * P:(qt + 1) * P], flips(1)[:, 0:ST - 4, :]).then_inc(moved_b.sem, 1)
                    top(0)
                    for i in range(TILES):
                        if i + 1 < TILES:
                            top(i + 1)
                        normal(i)
                        if i >= 1:
                            move(i - 1)
                    move(TILES - 1)
        n = HEADS * TT
        for signal in (scored, topped, biased, powered, inverse, probable, flipped, moved_a, moved_b):
            signal.close(n)
        staged.close(HEADS)
        weighted.close(HEADS)
        kept.close(HEADS)

    def mix_out(self, s):
        base = self.used
        part, merged = self.sig("part"), self.sig("merged")
        with self.nc.Block() as block:
            @block.sync
            def _(sp):
                self.issue(sp, base + 2 * KT + SLOTS)

            @block.tensor
            def _(pe):
                self.slabs(pe, 0, KT, self.linear(pe, s.o))
                pe.wait_ge(merged.sem, merged.at(KT))
                self.slabs(pe, KT, KT, self.linear(pe, s.gates[:, KT:2 * KT, :]))

            @block.vector
            def _(dve):
                def flat(tile, i):
                    return tile[:, ds(i, 1), :].rearrange("p a t -> p (a t)")
                with dve.Fori(0, KT // SLOTS) as turn:
                    for j in range(SLOTS):
                        i = SLOTS * turn + j
                        dve.wait_ge(self.slab_used, base + i + 1)
                        dve.tensor_tensor(flat(s.gates, i), self.bank[:, j, :], flat(s.gates, i), ALU.mult).then_inc(self.taken, 1)
                        dve.wait_ge(self.taken, base + i + 1)
                        dve.tensor_tensor(flat(s.gates, KT + i), flat(s.gates, i), flat(s.gates, KT + i), ALU.add).then_inc(merged.sem, 1)
                self.take(dve, KT, KT, lambda bank, i: dve.scalar_tensor_tensor(
                    flat(self.x, i), bank, self.mod[:, ds(2 * KT + i, 1), 0], flat(self.x, i), ALU.mult, ALU.add))
        merged.close(KT)
        self.used += 2 * KT

    def flip_tiles(self, src, dst, to_natural, after=None):
        flipped, copied = self.sig("tiles_flipped"), self.sig("tiles_copied")
        n = TT * KT // 4

        def where(i):
            t, quarter = divmod(i, KT // 4)
            return t, quarter * 4
        with self.nc.Block() as block:
            @block.tensor
            def _(pe):
                for i in range(n):
                    t, k0 = where(i)
                    if i >= 4:
                        pe.wait_ge(copied.sem, copied.at(i - 3))
                    for j in range(4):
                        at = self.side[:, i % 4, j * P:(j + 1) * P]
                        k = k0 + j
                        tile = src[:, k, t * P:(t + 1) * P] if to_natural else src[:, t, k * P:(k + 1) * P]
                        mm = pe.transpose(at, tile, self.const("ident"))
                    mm.then_inc(flipped.sem, 1)

            @block.vector
            def _(dve):
                for i in range(n):
                    t, k0 = where(i)
                    dve.wait_ge(flipped.sem, flipped.at(i + 1))
                    if to_natural:
                        last = dve.tensor_copy(dst[:, t, k0 * P:(k0 + 4) * P], self.side[:, i % 4, :])
                    elif after is None:
                        last = dve.tensor_copy(dst[:, k0:k0 + 4, t * P:(t + 1) * P],
                                               self.side[:, i % 4, :].rearrange("p (a c) -> p a c", c=P))
                    else:
                        for j in range(4):
                            last = after(dve, k0 + j, t, self.side[:, i % 4, j * P:(j + 1) * P])
                    last.then_inc(copied.sem, 1)
        flipped.close(n)
        copied.close(n)

    def select(self, dve, s, tile, g, n):
        chain = self.sig("pick_chain")
        start = n

        def after(n):
            dve.wait_ge(chain.sem, chain.at(n))
            dve.nop(nofuse=True)

        def grid(ap):
            return ap.rearrange("p (a b) -> p a b", b=PTOP)

        def grids(ap):
            return ap.rearrange("p (c a b) -> p c a b", c=2, b=PTOP)
        dve.tensor_copy(s.two[:], s.sk[:, ds(2 * g, 2), ds(tile * P, P)]).then_inc(chain.sem, 1)
        after(start + 1)
        for half in range(2):
            dve.max(s.val[:, half, 0:8], s.two[:, half, :]).then_inc(chain.sem, 1)
        after(start + 3)
        for half in range(2):
            dve.max_index(s.pos[:, half, 0:8], s.val[:, half, 0:8], s.two[:, half, :]).then_inc(chain.sem, 1)
        for half in range(2):
            dve.match_replace(s.spare[:, half * P:(half + 1) * P], s.val[:, half, 0:8], s.two[:, half, :], LOW).then_inc(chain.sem, 1)
        after(start + 7)
        for half in range(2):
            dve.max(s.val[:, half, 8:16], s.spare[:, half * P:(half + 1) * P]).then_inc(chain.sem, 1)
        after(start + 9)
        for half in range(2):
            dve.max_index(s.pos[:, half, 8:16], s.val[:, half, 8:16], s.spare[:, half * P:(half + 1) * P]).then_inc(chain.sem, 1)
        dve.tensor_tensor(grid(s.cand[:, 0:NCAND]), s.val[:, 0, :].unsqueeze(2).to_broadcast([P, PTOP, PTOP]),
                          s.val[:, 1, :].unsqueeze(1).to_broadcast([P, PTOP, PTOP]), ALU.add).then_inc(chain.sem, 1)
        after(start + 12)
        cand = s.cand[:, 0:NCAND]
        dve.max(s.best[:, 0:8], cand).then_inc(chain.sem, 1)
        dve.tensor_copy(s.posf[:], s.pos[:]).then_inc(chain.sem, 1)
        after(start + 14)
        dve.max_index(s.place[:, 0:8], s.best[:, 0:8], cand).then_inc(chain.sem, 1)
        dve.match_replace(s.spare[:], s.best[:, 0:8], cand, LOW).then_inc(chain.sem, 1)
        after(start + 16)
        dve.max(s.best[:, 8:16], s.spare[:]).then_inc(chain.sem, 1)
        after(start + 17)
        dve.max_index(s.place[:, 8:16], s.best[:, 8:16], s.spare[:]).then_inc(chain.sem, 1)
        dve.wait_ge(chain.sem, chain.at(start + 18))
        dve.tensor_copy(s.top[:, ds(g, 1), :].rearrange("p a k -> p (a k)"), s.best[:]).then_inc(chain.sem, 1)
        dve.tensor_scalar(s.which[:, 0, :], s.place[:], 4, None, ALU.logical_shift_right).then_inc(chain.sem, 1)
        dve.tensor_scalar(s.which[:, 1, :], s.place[:], PTOP - 1, None, ALU.bitwise_and).then_inc(chain.sem, 1)
        dve.wait_ge(chain.sem, chain.at(start + 21))
        dve.tensor_tensor(grids(s.cand[:]), s.which[:].unsqueeze(3).to_broadcast([P, 2, PTOP, PTOP]),
                          self.const("iota", b=PTOP).unsqueeze(1).unsqueeze(1).to_broadcast([P, 2, PTOP, PTOP]), ALU.is_equal).then_inc(chain.sem, 1)
        dve.wait_ge(chain.sem, chain.at(start + 22))
        dve.tensor_tensor(grids(s.cand[:]), grids(s.cand[:]), s.posf[:].unsqueeze(2).to_broadcast([P, 2, PTOP, PTOP]), ALU.mult).then_inc(chain.sem, 1)
        dve.wait_ge(chain.sem, chain.at(start + 23))
        dve.tensor_reduce(s.key[:], grids(s.cand[:]), AX.X, ALU.add).then_inc(chain.sem, 1)
        dve.wait_ge(chain.sem, chain.at(start + 24))
        dve.scalar_tensor_tensor(s.expert[:, ds(tile, 1), ds(PTOP * g, PTOP)].rearrange("p a k -> p (a k)"),
                                 s.key[:, 0, :], float(PKEYS), s.key[:, 1, :], ALU.mult, ALU.add).then_inc(chain.sem, 1)
        dve.wait_ge(chain.sem, chain.at(start + SELECT))

    def weigh_experts(self, dve, s, tile):
        soft, powered = self.sig("soft_chain"), self.sig("w_powered")
        dve.tensor_tensor(s.power[:], s.top[:], s.top[:, :, 0:1].to_broadcast([P, PH, PTOP]), ALU.subtract).then_inc(soft.sem, 1)
        dve.wait_ge(powered.sem, powered.at(tile + 1))
        dve.tensor_reduce(s.wsum[:], s.power[:], AX.X, ALU.add).then_inc(soft.sem, 1)
        dve.wait_ge(soft.sem, soft.at(4 * tile + 2))
        dve.reciprocal(s.wsum[:], s.wsum[:]).then_inc(soft.sem, 1)
        dve.wait_ge(soft.sem, soft.at(4 * tile + 3))
        dve.tensor_tensor(s.weight[:].rearrange("p (h k) -> p h k", k=PTOP), s.power[:], s.wsum[:].unsqueeze(2).to_broadcast([P, PH, PTOP]),
                          ALU.mult).then_inc(soft.sem, 1)
        dve.wait_ge(soft.sem, soft.at(4 * tile + 4))

    def exponentials(self, act, s, tile):
        soft, powered = self.sig("soft_chain"), self.sig("w_powered")
        act.wait_ge(soft.sem, soft.at(4 * tile + 1))
        act.activation(s.power[:], s.power[:], ACT.Exp).then_inc(powered.sem, 1)

    def score_keys(self, s):
        base, n = self.used, 2 * PH
        sig = self.sig
        keyed, copied, scored, staged = sig("keys_loaded"), sig("pq_copied"), sig("key_scored"), sig("key_staged")
        chain = sig("pick_chain")
        with self.nc.Block() as block:
            @block.sync
            def _(sp):
                sp.dma_start(s.keys[:], self.d["keys"]).then_inc(keyed.sem, 16)
                self.issue(sp, base + n + SLOTS)

            @block.tensor
            def _(pe):
                pe.wait_ge(keyed.sem, keyed.at(16))

                def against_keys(i, j):
                    pe.wait_ge(copied.sem, copied.at(i + 1))
                    if i >= 2:
                        pe.wait_ge(staged.sem, staged.at(i - 1))
                    for t in range(TT):
                        mm = pe.matmul(self.side[:, j, t * P:(t + 1) * P], s.pq[:, j, t * P:(t + 1) * P],
                                       s.keys[:, ds(i, 1), :].rearrange("p a n -> p (a n)"), start=True, stop=True)
                    mm.then_inc(scored.sem, 1)
                for i in range(n):
                    pos = base + i
                    pe.wait_ge(self.landed[i % SLOTS], 16 * (pos // SLOTS + 1))
                    pe.wait_ge(self.taken, pos - SLOTS + 1)
                    self.linear(pe, self.h)(i % SLOTS, i).then_inc(self.slab_used, 1)
                    if i:
                        against_keys(i - 1, (i - 1) % 2)
                against_keys(n - 1, (n - 1) % 2)

            @block.scalar
            def _(act):
                def stage(i):
                    act.wait_ge(scored.sem, scored.at(i + 1))
                    act.activation(s.sk[:, i, :], self.side[:, i % 2, :], ACT.Copy).then_inc(staged.sem, 1)
                for i in range(n):
                    if i >= 2:
                        act.wait_ge(scored.sem, scored.at(i - 1))
                    act.wait_ge(self.slab_used, base + i + 1)
                    act.activation(s.pq[:, i % 2, :], self.bank[:, i % SLOTS, :], ACT.Copy).then_inc(self.taken, 1)
                    act.wait_ge(self.taken, base + i + 1)
                    act.activation(s.mark[:], self.eps[EPS], ACT.Copy).then_inc(copied.sem, 1)
                    if i:
                        stage(i - 1)
                stage(n - 1)
                self.exponentials(act, s, 0)

            @block.vector
            def _(dve):
                with dve.Fori(0, PH) as g:
                    dve.wait_ge(staged.sem, staged.at(2 * g + 2))
                    self.select(dve, s, 0, g, SELECT * g)
                self.weigh_experts(dve, s, 0)
        copied.close(n)
        scored.close(n)
        staged.close(n)
        chain.close(SELECT * PH)
        sig("soft_chain").close(4)
        sig("w_powered").close(1)
        keyed.close(16)
        self.used += n

    def experts(self, s):
        sig, d = self.sig, self.d
        HALF = ROWS // 2
        indexed, dotted, row_used, coefficient = sig("indexed"), sig("dotted"), sig("row_used"), sig("coefficient")
        pe_used, lined, summed, zeroed = sig("pe_row_used"), sig("diagonal"), sig("pe_summed"), sig("peer_zeroed")
        gelued, added, hready, selected = sig("gelued"), sig("row_added"), sig("h_ready"), sig("tile_selected")
        chain, cooked = sig("pick_chain"), sig("cooked")
        landed = [sig(f"row_landed{j}") for j in range(ROWS)]
        U, V = ROWS * GROUPS, HALF * GROUPS
        base = self.used
        slabs = 2 * NMOD
        assert slabs == SLOTS * GROUPS * (TT - 1)

        with self.nc.Block() as block:
            @block.sync
            def _(sp):
                self.issue(sp, base + slabs + SLOTS)

            @block.gpsimd
            def _(pool):
                def gathers(table, t, group, number, free, free_pe=None):
                    for half in range(2):
                        if free is not None:
                            dve_rows, step = free
                            pool.wait_ge(row_used.sem, row_used.at(dve_rows + step * (half + 1)))
                            if free_pe is not None:
                                pool.wait_ge(pe_used.sem, pe_used.at(DIAGS + free_pe + HALF // 2 * (half + 1)))
                            pool.nop(nofuse=True)
                        at = slice(HALF * half, HALF * (half + 1))
                        pool.tensor_copy(s.index[:, at], s.expert[:, ds(t, 1), ds(ROWS * group + HALF * half, HALF)].rearrange("p a n -> p (a n)")
                                         ).then_inc(indexed.sem, 1)
                        pool.wait_ge(indexed.sem, indexed.at(2 * number + half + 1))
                        pool.nop(nofuse=True)
                        for j in range(HALF * half, HALF * (half + 1)):
                            pool.indirect_dma_start(
                                out=s.row[j], out_offset=None, in_=table,
                                in_offset=bass.IndirectOffsetOnAxis(ap=s.index[:, j:j + 1], axis=0)).then_inc(landed[j].sem, 16)

                def tile(t, first):
                    done, done_pe, number = (U + V) * t, V * t, 2 * GROUPS * t
                    if first:
                        gathers(d["peer_u"], t, 0, number, None)
                    else:
                        pool.wait_ge(selected.sem, selected.at(t))
                        gathers(d["peer_u"], t, 0, number, (done - HALF, HALF // 2), done_pe - HALF)
                    with pool.Fori(1, GROUPS) as group:
                        gathers(d["peer_u"], t, group, number + group, (done + ROWS * (group - 1), HALF))
                    gathers(d["peer_v"], t, 0, number + GROUPS, (done + U - ROWS, HALF))
                    with pool.Fori(1, GROUPS) as group:
                        gathers(d["peer_v"], t, group, number + GROUPS + group, (done + U + HALF * (group - 1), HALF // 2),
                                done_pe + HALF * (group - 1))
                tile(0, True)
                with pool.Fori(1, TT) as t:
                    tile(t, False)

            @block.vector
            def _(dve):
                dve.memset(s.zero[:], 0.0).then_inc(zeroed.sem, 1)

                def tile(t, pick):
                    dve.tensor_copy(s.hcur, s.hn[:, ds(t, 1), :].rearrange("p a n -> p (a n)")).then_inc(hready.sem, 1)
                    dve.wait_ge(hready.sem, hready.at(t + 1))
                    dve.nop(nofuse=True)
                    done = (U + V) * t
                    with dve.Fori(0, GROUPS) as group:
                        number = 2 * GROUPS * t + group
                        for j in range(ROWS):
                            dve.wait_ge(landed[j].sem, landed[j].at(16 * (number + 1)))
                            dve.tensor_tensor_reduce(s.row[j], s.row[j], s.hcur, 1.0, 0.0, ALU.mult, ALU.add,
                                                     s.dot[:, j:j + 1]).then_inc(row_used.sem, 1)
                        dve.wait_ge(row_used.sem, row_used.at(done + ROWS * (group + 1)))
                        dve.tensor_copy(s.act[:, ds(ROWS * group, ROWS)], s.dot[:]).then_inc(dotted.sem, 1)
                        dve.wait_ge(dotted.sem, dotted.at(GROUPS * t + group + 1))
                    dve.wait_ge(gelued.sem, gelued.at(t + 1))
                    dve.tensor_tensor(s.coef[:], s.act[:], s.weight[:], ALU.mult).then_inc(coefficient.sem, 1)
                    dve.memset(s.acc, 0.0).then_inc(coefficient.sem, 1)
                    dve.wait_ge(coefficient.sem, coefficient.at(2 * t + 2))
                    dve.nop(nofuse=True)
                    with dve.Fori(0, GROUPS) as group:
                        number = 2 * GROUPS * t + GROUPS + group
                        if pick:
                            self.select(dve, s, t + 1, group, SELECT * (PH * t + group))
                        for i in range(HALF):
                            j = 2 * i
                            dve.wait_ge(landed[j].sem, landed[j].at(16 * (number + 1)))
                            if i >= 2:
                                dve.wait_ge(row_used.sem, row_used.at(done + U + HALF * group + i - 1))
                            dve.scalar_tensor_tensor(s.acc[:, i % 2, :], s.row[j], s.coef[:, ds(ROWS * group + j, 1)],
                                                     s.acc[:, i % 2, :], ALU.mult, ALU.add).then_inc(row_used.sem, 1)
                        dve.wait_ge(row_used.sem, row_used.at(done + U + HALF * (group + 1)))
                    if pick:
                        dve.memset(s.wsum[:], 0.0).then_inc(selected.sem, 1)
                    y = s.y[:, ds(t, 1), :].rearrange("p a n -> p (a n)")
                    dve.tensor_tensor(y, s.acc[:, 0, :], s.acc[:, 1, :], ALU.add).then_inc(added.sem, 1)
                    dve.wait_ge(added.sem, added.at(2 * t + 1))
                    dve.wait_ge(summed.sem, summed.at(t + 1))
                    dve.tensor_tensor(y, self.side[:, 0:2, :].rearrange("p a n -> p (a n)"), y, ALU.add).then_inc(added.sem, 1)
                    dve.wait_ge(added.sem, added.at(2 * t + 2))
                    if pick:
                        dve.wait_ge(selected.sem, selected.at(t + 1))
                        self.weigh_experts(dve, s, t)
                with dve.Fori(0, TT - 1) as t:
                    tile(t, True)
                tile(TT - 1, False)
                dve.wait_ge(self.slab_used, base + slabs)
                dve.tensor_tensor(self.mod2[:], self.side[:, 2, 0:slabs], self.vec("ada_b", 0, slabs), ALU.add).then_inc(self.taken, slabs)
                dve.wait_ge(self.taken, base + slabs)
                for layer in range(2):
                    for n, at in enumerate((1, 2, 4, 5)):
                        dve.tensor_scalar(self.cooked[:, 3 + 4 * layer + n, :],
                                          self.mod2[:, layer * NMOD + at * KT:layer * NMOD + (at + 1) * KT],
                                          1.0, None, ALU.add).then_inc(cooked.sem, 1)

            @block.scalar
            def _(act):
                act.activation(s.mark[:], self.eps[EPS], ACT.Copy).then_inc(pe_used.sem, DIAGS)

                def tile(t, pick):
                    act.wait_ge(dotted.sem, dotted.at(GROUPS * (t + 1)))
                    act.activation(s.act[:], s.act[:], ACT.Gelu).then_inc(gelued.sem, 1)
                    act.wait_ge(coefficient.sem, coefficient.at(2 * t + 1))
                    with act.Fori(0, GROUPS) as group:
                        for i in range(HALF):
                            act.wait_ge(pe_used.sem, pe_used.at(V * t + HALF * group + i + 1))
                            act.activation(s.diag[:, i % DIAGS, :], self.const("ident"), ACT.Copy,
                                           scale=s.coef[:, ds(ROWS * group + 2 * i + 1, 1)]).then_inc(lined.sem, 1)
                    if pick:
                        self.exponentials(act, s, t)
                with act.Fori(0, TT - 1) as t:
                    tile(t, True)
                tile(TT - 1, False)

            @block.tensor
            def _(pe):
                pe.wait_ge(zeroed.sem, zeroed.at(1))
                sums = self.side[:, 0:2, :]

                def modulate(turn, j):
                    pe.wait_ge(self.landed[j], 16 * (base // SLOTS + 1) + 16 * turn)
                    for k in range(KT):
                        mm = pe.matmul(self.side[:, 2, ds(SLOTS * turn + j, 1)], self.wslab(j, k), self.cond_s[:, k, 2:3],
                                       start=k == 0, stop=k == KT - 1)
                    mm.then_inc(self.slab_used, 1)

                def tile(t, slabs_too, first=False):
                    if slabs_too:
                        with pe.Fori(0, GROUPS) as group:
                            for j in range(SLOTS):
                                modulate(GROUPS * t + group, j)
                    if not first:
                        pe.wait_ge(added.sem, added.at(2 * t))
                    for half in range(2):
                        pe.matmul(sums[:, half, :], s.zero[:], self.const("cos"), start=True, stop=False, skip_group_check=True)
                    with pe.Fori(0, GROUPS) as group:
                        number = 2 * GROUPS * t + GROUPS + group
                        for i in range(HALF):
                            j = 2 * i + 1
                            pe.wait_ge(landed[j].sem, landed[j].at(16 * (number + 1)))
                            pe.wait_ge(lined.sem, lined.at(V * t + HALF * group + i + 1))
                            for half in range(2):
                                mm = pe.matmul(sums[:, half, :], s.diag[:, i % DIAGS, :], s.row[j][:, half * T:(half + 1) * T],
                                               start=False, stop=False, skip_group_check=True)
                            mm.then_inc(pe_used.sem, 1)
                    for half in range(2):
                        mm = pe.matmul(sums[:, half, :], s.zero[:], self.const("cos"), start=False, stop=True, skip_group_check=True)
                    mm.then_inc(summed.sem, 1)
                tile(0, True, first=True)
                with pe.Fori(1, TT - 1) as t:
                    tile(t, True)
                tile(TT - 1, False)
        groups = 2 * GROUPS * TT
        indexed.close(2 * groups)
        for signal in landed:
            signal.close(16 * groups)
        row_used.close((U + V) * TT)
        pe_used.close(V * TT + DIAGS)
        lined.close(V * TT)
        summed.close(TT)
        zeroed.close(1)
        dotted.close(GROUPS * TT)
        gelued.close(TT)
        coefficient.close(2 * TT)
        added.close(2 * TT)
        hready.close(TT)
        selected.close(TT - 1)
        chain.close(SELECT * PH * (TT - 1))
        sig("soft_chain").close(4 * (TT - 1))
        sig("w_powered").close(TT - 1)
        cooked.close(8)
        self.used += slabs

    def mix_in(self, s, layer):
        base = self.used
        sig = self.sig
        chain, low, gate = sig("mix_chain"), sig("low"), sig("decay")
        with self.nc.Block() as block:
            @block.sync
            def _(sp):
                self.issue(sp, base + 24 + SLOTS)

            @block.tensor
            def _(pe):
                self.slabs(pe, 0, 16, self.linear(pe, self.h))
                for k in range(KT):
                    at = (layer * KT + k) * 16
                    mm = pe.matmul(self.side[0:16, 0, :], self.small[:, at:at + 16], self.h[:, k, :], start=k == 0, stop=k == KT - 1)
                mm.then_inc(low.sem, 1)
                pe.wait_ge(low.sem, low.at(2))
                for p in range(2):
                    at = 2 * KT * 16 + KT * NE + layer * 2 * P + p * P
                    mm = pe.matmul(self.side[:, 1 + p, :], self.small[0:16, at:at + P], s.low[0:16, :], start=True, stop=True)
                mm.then_inc(low.sem, 1)
                self.slabs(pe, 16, 4, lambda slot, i: self.natural(pe, self.h, slot, self.bank[:, slot, :], TT))
                self.slabs(pe, 20, 4, self.linear(pe, self.h))

            @block.scalar
            def _(act):
                def flat(tile):
                    return lambda bank, i: act.activation(tile[:, ds(i, 1), :].rearrange("p a t -> p (a t)"), bank, ACT.Copy)
                self.take(act, 0, 8, flat(s.cch))
                self.take(act, 8, 4, flat(s.cb))
                self.take(act, 12, 4, flat(s.qk))
                act.wait_ge(low.sem, low.at(1))
                act.activation(s.low[0:16, :], self.side[0:16, 0, :], ACT.Copy).then_inc(low.sem, 1)
                act.wait_ge(low.sem, low.at(3))
                for p in range(2):
                    act.activation(s.z[:, p, :], self.side[:, 1 + p, :], ACT.Identity, bias=self.vectors[
                        :, VECTORS["gk_b"][0] + 2 * layer + p:VECTORS["gk_b"][0] + 2 * layer + p + 1]).then_inc(gate.sem, 1)
                act.wait_ge(gate.sem, gate.at(3))
                act.activation(s.b[:], s.b[:], ACT.Exp, scale=-1.0).then_inc(gate.sem, 1)
                act.wait_ge(gate.sem, gate.at(4))
                act.activation(s.b[:], s.b[:], ACT.Ln, bias=self.one).then_inc(gate.sem, 1)
                act.wait_ge(gate.sem, gate.at(6))
                act.activation(s.eb[:], s.b[:], ACT.Exp).then_inc(gate.sem, 1)
                act.activation(s.enb[:], s.b[:], ACT.Exp, scale=-1.0).then_inc(gate.sem, 1)
                act.activation(s.z[:], s.z[:], ACT.Exp).then_inc(gate.sem, 1)
                self.take(act, 16, 4, lambda bank, i: act.activation(
                    s.v[:, :, ds(i, 1), :].rearrange("p t a n -> p t (a n)"), bank.rearrange("p (t n) -> p t n", n=P), ACT.Copy))
                self.take(act, 20, 4, lambda bank, i: act.activation(
                    s.gate[:, ds(i, 1), :].rearrange("p a t -> p (a t)"), bank, ACT.Silu))

            @block.vector
            def _(dve):
                n = [0]

                def step(instruction):
                    instruction.then_inc(chain.sem, 1)
                    n[0] += 1
                    dve.wait_ge(chain.sem, chain.at(n[0]))

                def tap(c, j):
                    at = VECTORS["conv2_w"][0] + (layer * CONV2 + c) * TAPS2 + j
                    return self.vectors[:, at:at + 1]
                step(dve.memset(s.zpad[:, :, 0:2], 0.0))
                for c in range(CONV2):
                    dve.wait_ge(self.taken, base + 2 * c + 2)
                    step(dve.tensor_tensor(s.zpad[:, c, 2:2 + T], s.cch[:, 2 * c, :], s.cch[:, 2 * c + 1, :], ALU.mult))
                    step(dve.tensor_scalar(s.y[:, c, :], s.zpad[:, c, 0:T], tap(c, 0), None, ALU.mult))
                    for j in range(1, TAPS2):
                        step(dve.scalar_tensor_tensor(s.y[:, c, :], s.zpad[:, c, j:j + T], tap(c, j), s.y[:, c, :], ALU.mult, ALU.add))
                for c in range(CONV2):
                    dve.wait_ge(self.taken, base + 9 + c)
                    step(dve.tensor_tensor(s.y[:, c, :], s.y[:, c, :], s.cb[:, c, :], ALU.mult))
                dve.wait_ge(gate.sem, gate.at(2))
                dve.scalar_tensor_tensor(s.b[:], s.z[:], -1.0, s.z[:], ALU.mult, ALU.max).then_inc(gate.sem, 1)
                dve.wait_ge(gate.sem, gate.at(5))
                step(dve.scalar_tensor_tensor(s.z[:], s.z[:], 0.0, s.b[:], ALU.min, ALU.subtract))
                step(dve.tensor_scalar(s.z[:], s.z[:], 1.0 / 16.0, -1.0, ALU.mult, ALU.max))
                for p in range(2):
                    step(dve.tensor_tensor_scan(s.b[:, p, :], self.const("carry"), s.z[:, p, :], 0.0, ALU.mult, ALU.add))
                chunks = s.b[:].rearrange("p a (n c) -> p (a n) c", c=GCH)
                dve.tensor_tensor(s.z[:].rearrange("p a (n c) -> p (a n) c", c=GCH),
                                          chunks[:, :, GCH - 1:GCH].to_broadcast([P, 2 * NCH, GCH]), chunks, ALU.subtract).then_inc(gate.sem, 1)
                dve.wait_ge(self.taken, base + 16)
                dve.wait_ge(gate.sem, gate.at(9))
                step(dve.scalar_tensor_tensor(s.qk[:, 0:2, :], s.qk[:, 0:2, :], float(GDK) ** -0.5, s.eb[:], ALU.mult, ALU.mult))
                step(dve.tensor_tensor(s.enb[:], s.enb[:], s.qk[:, 2:4, :], ALU.mult))
                step(dve.tensor_tensor(s.kout[:], s.z[:], s.qk[:, 2:4, :], ALU.mult))
                s.steps = n[0]
        chain.close(s.steps)
        low.close(3)
        gate.close(9)
        self.used += 24

    def linear_attention(self, s, layer):
        sig = self.sig
        masked, scored, weighed = sig("k_masked"), sig("gla_scored"), sig("gla_weighed")
        flipped, parted, added, chain = sig("kout_flipped"), sig("kout_parted"), sig("kv_made"), sig("state_chain")
        made, squared, summed, rooted = sig("o_made"), sig("o_squared"), sig("o_summed"), sig("o_rooted")
        oc = sig("o_chain")
        half = self.const("half")
        qin = s.qk[:, 0:2, :]
        PAIRS = GH // 2

        with self.nc.Block() as block:
            @block.tensor
            def _(pe):
                for p in range(PAIRS):
                    for t in range(TT):
                        mm = pe.transpose(self.side[:, p, t * P:(t + 1) * P], s.kout[:, p, t * P:(t + 1) * P], self.const("ident"))
                    mm.then_inc(flipped.sem, 1)
                for h in range(GH):
                    pe.wait_ge(masked.sem, masked.at(h + 1))
                    for t in range(TT):
                        at = slice(t * P, (t + 1) * P)
                        mm = pe.matmul(self.bank[:, h, at], s.kmask[:, h, at], qin[:, h // 2, at], start=True, stop=True)
                    mm.then_inc(scored.sem, 1)
                for p in range(PAIRS):
                    after = weighed if p == 0 else parted
                    pe.wait_ge(after.sem, after.at(GH))
                    if p == 0:
                        pe.wait_ge(parted.sem, parted.at(2))
                    for n in range(NCH):
                        place = (self.bank if p == 0 else self.side)[:, n // 2, (n % 2) * 2 * P:(n % 2 + 1) * 2 * P]
                        mm = pe.matmul(place, s.kon[:, n % 2, p, (n // 2) * P:(n // 2 + 1) * P],
                                       s.v[:, n // 2, 2 * p:2 * p + 2, :].rearrange("p a n -> p (a n)"), start=True, stop=True)
                        if n % 2:
                            mm.then_inc(added.sem, 1)
                for h in range(GH):
                    p = h // 2
                    pe.wait_ge(chain.sem, chain.at((p + 1) * (NCH // 2 + NCH - 2)))
                    if p == 0 and h == 0:
                        pass
                    for t in range(TT):
                        pe.matmul(self.bank[:, h, t * P:(t + 1) * P], s.v[:, t, h, :], s.a[:, h, t * P:(t + 1) * P],
                                  start=True, stop=False, skip_group_check=True)
                        for r in range(2):
                            n = 2 * t + r
                            if n:
                                mm = pe.matmul(self.bank[:, h, n * GCH:(n + 1) * GCH],
                                               s.state[:, p, n - 1, (h % 2) * P:(h % 2 + 1) * P],
                                               qin[:, p, n * GCH:(n + 1) * GCH], start=False, stop=r == 1, skip_group_check=True)
                    mm.then_inc(made.sem, 1)
                for h in range(GH):
                    pe.wait_ge(squared.sem, squared.at(h + 1))
                    if h == 0:
                        pe.wait_ge(chain.sem, chain.at(PAIRS * (NCH // 2 + NCH - 2)))
                    pe.matmul(self.side[:, h, :], self.const("ones"), s.sq[:, h, :], start=True, stop=True).then_inc(summed.sem, 1)

            @block.vector
            def _(dve):
                for h in range(GH):
                    dve.tensor_scalar(s.kmask[:, h, :], s.enb[:, h // 2, :], half[:, h % 2:h % 2 + 1], None, ALU.mult).then_inc(masked.sem, 1)
                for p in range(PAIRS):
                    dve.wait_ge(flipped.sem, flipped.at(p + 1))
                    for r in range(2):
                        dve.tensor_scalar(s.kon[:, r, p, :], self.side[:, p, :], half[:, r:r + 1], None, ALU.mult).then_inc(parted.sem, 1)
                for h in range(GH):
                    dve.wait_ge(scored.sem, scored.at(h + 1))
                    dve.tensor_tensor(s.a[:, h, :].rearrange("p (t n) -> p t n", n=P),
                                                 self.bank[:, h, :].rearrange("p (t n) -> p t n", n=P),
                                                 self.const("causal").unsqueeze(1).to_broadcast([P, TT, P]), ALU.mult).then_inc(weighed.sem, 1)
                k = 0
                for p in range(PAIRS):
                    source = self.bank if p == 0 else self.side
                    for n in range(NCH // 2):
                        dve.wait_ge(added.sem, added.at(p * (NCH // 2) + n + 1))
                        dve.tensor_tensor(s.state[:, p, 2 * n:2 * n + 2, :], source[:, n, :].rearrange("p (a m) -> p a m", a=2),
                                                   self.const("pair").unsqueeze(1).to_broadcast([P, 2, 2 * P]), ALU.mult).then_inc(chain.sem, 1)
                        k += 1
                    for n in range(1, NCH - 1):
                        dve.wait_ge(chain.sem, chain.at(k))
                        dve.scalar_tensor_tensor(s.state[:, p, n, :], s.state[:, p, n - 1, :],
                                                          s.eb[:, p, (n + 1) * GCH - 1:(n + 1) * GCH], s.state[:, p, n, :],
                                                          ALU.mult, ALU.add).then_inc(chain.sem, 1)
                        k += 1
                assert k == PAIRS * (NCH // 2 + NCH - 2)
                for h in range(GH):
                    dve.wait_ge(rooted.sem, rooted.at(h + 1))
                    dve.reciprocal(s.inv[:], s.root[:, h, :]).then_inc(oc.sem, 1)
                    dve.wait_ge(oc.sem, oc.at(3 * h + 1))
                    dve.tensor_tensor(s.inv[:], self.bank[:, h, :], s.inv[:], ALU.mult).then_inc(oc.sem, 1)
                    dve.wait_ge(oc.sem, oc.at(3 * h + 2))
                    dve.scalar_tensor_tensor(s.y[:, CONV2 + h, :], s.inv[:],
                                                   self.vectors[:, VECTORS["gla_g"][0] + layer:VECTORS["gla_g"][0] + layer + 1],
                                                   s.gate[:, h, :], ALU.mult, ALU.mult).then_inc(oc.sem, 1)
                    dve.wait_ge(oc.sem, oc.at(3 * h + 3))

            @block.scalar
            def _(act):
                for h in range(GH):
                    act.wait_ge(made.sem, made.at(h + 1))
                    act.activation(s.sq[:, h, :], self.bank[:, h, :], ACT.Square).then_inc(squared.sem, 1)
                for h in range(GH):
                    act.wait_ge(summed.sem, summed.at(h + 1))
                    act.activation(s.root[:, h, :], self.side[:, h, :], ACT.Sqrt, bias=self.eps[EPS], scale=1.0 / GDV).then_inc(rooted.sem, 1)
        for signal in (masked, scored, weighed, parted, made, squared, summed, rooted):
            signal.close(GH)
        flipped.close(2)
        added.close(NCH)
        chain.close(PAIRS * (NCH // 2 + NCH - 2))
        oc.close(3 * GH)

    def residual(self, src, gain):
        base = self.used
        chain = self.sig("residual_chain")
        with self.nc.Block() as block:
            @block.sync
            def _(sp):
                self.issue(sp, base + KT + SLOTS)

            @block.tensor
            def _(pe):
                self.slabs(pe, 0, KT, self.linear(pe, src))

            @block.vector
            def _(dve):
                with dve.Fori(0, KT // SLOTS) as turn:
                    for j in range(SLOTS):
                        i = SLOTS * turn + j
                        dve.wait_ge(self.slab_used, base + i + 1)
                        dve.tensor_scalar(self.stat[:, j % 2, :], self.bank[:, j, :], gain(i), None, ALU.mult).then_inc(self.taken, 1)
                        dve.wait_ge(self.taken, base + i + 1)
                        flat = self.x[:, ds(i, 1), :].rearrange("p a t -> p (a t)")
                        dve.scalar_tensor_tensor(flat, flat, ALPHA, self.stat[:, j % 2, :], ALU.mult, ALU.add).then_inc(chain.sem, 1)
                        dve.wait_ge(chain.sem, chain.at(i + 1))
        chain.close(KT)
        self.used += KT

    def dense_up(self, s):
        base = self.used
        sig = self.sig
        made, rounded, split = sig("hidden_made"), sig("slab_rounded"), sig("slab_split")
        h_rounded, h_split = sig("h_rounded"), sig("h_split")
        PLACES = 2
        N = 2 * FT
        assert base % SLOTS == 0 and N % SLOTS == 0 and SLOTS % PLACES == 0
        with self.nc.Block() as block:
            @block.sync
            def _(sp):
                self.issue(sp, base + N + SLOTS)

            @block.tensor
            def _(pe):
                pe.wait_ge(h_split.sem, h_split.at(KT))

                def turn(turn):
                    for j in range(SLOTS):
                        i = SLOTS * turn + j
                        pe.wait_ge(split.sem, split.at(i + 1))
                        pe.wait_ge(self.taken, base + i - SLOTS + 1)
                        for k in range(KT):
                            at = slice(k * P, (k + 1) * P)
                            for n, (w, x) in enumerate(((s.high, s.hhigh), (s.high, s.hlow), (s.low, s.hhigh))):
                                mm = pe.matmul(self.bank[:, j, :], w[:, j % PLACES, at], x[:, k, :],
                                               start=k == 0 and n == 0, stop=k == KT - 1 and n == 2)
                        mm.then_inc(self.slab_used, 1)
                with pe.Fori(0, N // SLOTS) as t:
                    turn(t)

            @block.gpsimd
            def _(pool):
                with pool.Fori(0, N // SLOTS) as turn:
                    for j in range(SLOTS):
                        pool.wait_ge(rounded.sem, rounded.at(SLOTS * turn + j + 1))
                        pool.tensor_tensor(s.low[:, j % PLACES, :], self.ring[j][:, 0:D], s.high[:, j % PLACES, :].bitcast(F32),
                                           ALU.subtract).then_inc(split.sem, 1)

            @block.scalar
            def _(act):
                def round_slab(turn, j):
                    act.wait_ge(self.landed[j % SLOTS], 16 * (base // SLOTS + j // SLOTS + 1) + 16 * turn)
                    act.activation(s.high[:, j % PLACES, :], self.ring[j % SLOTS][:, 0:D], ACT.Copy).then_inc(rounded.sem, 1)

                def turn(turn, first=False, last=False):
                    for j in range(SLOTS):
                        act.wait_ge(self.slab_used, base + SLOTS * turn + j + 1)
                        if not (last and j + PLACES >= SLOTS):
                            round_slab(turn, j + PLACES)
                        if j % 2 == 0 and not first:
                            act.wait_ge(made.sem, made.at(2 * turn + j // 2 - 1))
                        act.activation(s.ab[:, j, :], self.bank[:, j, :], ACT.Copy if j % 2 else ACT.Silu).then_inc(self.taken, 1)
                for j in range(PLACES):
                    round_slab(0, j)
                for k in range(KT):
                    act.activation(s.hhigh[:, k, :], self.h[:, k, :], ACT.Copy).then_inc(h_rounded.sem, 1)
                turn(0, first=True)
                with act.Fori(1, N // SLOTS - 1) as t:
                    turn(t)
                turn(N // SLOTS - 1, last=True)

            @block.vector
            def _(dve):
                for k in range(KT):
                    dve.wait_ge(h_rounded.sem, h_rounded.at(k + 1))
                    dve.tensor_tensor(s.hlow[:, k, :], self.h[:, k, :], s.hhigh[:, k, :].bitcast(F32), ALU.subtract).then_inc(h_split.sem, 1)
                with dve.Fori(0, FT // 2) as turn:
                    for j in range(2):
                        f = 2 * turn + j
                        dve.wait_ge(self.taken, base + 2 * f + 2)
                        dve.tensor_tensor(s.hidden[:, ds(f, 1), :].rearrange("p a t -> p (a t)"),
                                                  s.ab[:, 2 * j, :], s.ab[:, 2 * j + 1, :], ALU.mult).then_inc(made.sem, 1)
        made.close(FT)
        rounded.close(N)
        split.close(N)
        h_rounded.close(KT)
        h_split.close(KT)
        self.used += N

    def dense_down(self, s, gain):
        base = self.used
        chain = self.sig("residual_chain")
        with self.nc.Block() as block:
            @block.sync
            def _(sp):
                self.issue(sp, base + 2 * KT + SLOTS)

            @block.tensor
            def _(pe):
                def product(slot, index):
                    half = slot % 2
                    for k in range(HALF_FT):
                        mm = pe.matmul(self.bank[:, slot - half, :], self.wslab(slot, k), s.hidden[:, half * HALF_FT + k, :],
                                       start=half == 0 and k == 0, stop=half == 1 and k == HALF_FT - 1)
                    return mm
                self.slabs(pe, 0, 2 * KT, product)

            @block.vector
            def _(dve):
                with dve.Fori(0, KT // 2) as turn:
                    for j in range(2):
                        i = 2 * turn + j
                        dve.wait_ge(self.slab_used, base + 2 * i + 2)
                        dve.tensor_scalar(self.stat[:, j, :], self.bank[:, 2 * j, :], gain(i), None, ALU.mult).then_inc(self.taken, 2)
                        dve.wait_ge(self.taken, base + 2 * i + 2)
                        flat = self.x[:, ds(i, 1), :].rearrange("p a t -> p (a t)")
                        dve.scalar_tensor_tensor(flat, flat, ALPHA, self.stat[:, j, :], ALU.mult, ALU.add).then_inc(chain.sem, 1)
                        dve.wait_ge(chain.sem, chain.at(i + 1))
        chain.close(KT)
        self.used += 2 * KT

    def route(self, s):
        sig, d = self.sig, self.d
        stored, routed, picked, member = sig("tokens_stored"), sig("routed"), sig("expert_picked"), sig("member")
        ranked, chain, weights = sig("ranked"), sig("route_chain"), sig("route_exp")
        cleared, spread, numbered, read = sig("table_cleared"), sig("table_filled"), sig("numbered"), sig("table_read")
        at = 2 * KT * 16
        with self.nc.Block() as block:
            @block.sync
            def _(sp):
                sp.dma_start(s.tokens.rearrange("(t p) n -> p t n", p=P), s.hn[:]).then_inc(stored.sem, 16)
                sp.wait_ge(stored.sem, stored.at(16))
                sp.wait_ge(spread.sem, spread.at(16 * 2 * TT))
                with self.nc.allow_non_contiguous_dma(reason="2048 slot numbers"):
                    sp.dma_start(s.slot_token[:], s.table.rearrange("(b p) o -> p (b o)", p=P)).then_inc(read.sem, 16)
                sp.wait_ge(read.sem, read.at(16))

            @block.tensor
            def _(pe):
                for t in range(TT):
                    for k in range(KT):
                        mm = pe.matmul(self.side[:, 0, t * NE:(t + 1) * NE], self.h[:, k, t * P:(t + 1) * P],
                                       self.small[:, at + k * NE:at + (k + 1) * NE], start=k == 0, stop=k == KT - 1)
                mm.then_inc(routed.sem, 1)
                pe.wait_ge(member.sem, member.at(1))
                for t in range(TT):
                    pe.matmul(self.side[:, 1, t * NE:(t + 1) * NE], self.const("before"), s.member[:, t, :], start=True, stop=t == 0)
                    for u in range(t):
                        pe.matmul(self.side[:, 1, t * NE:(t + 1) * NE], self.const("ones"), s.member[:, u, :], start=False, stop=u == t - 1)
                for t in range(TT):
                    mm = pe.matmul(self.side[:, 2, 0:NE], self.const("ones"), s.member[:, t, :], start=t == 0, stop=t == TT - 1)
                mm.then_inc(ranked.sem, 1)

            @block.scalar
            def _(act):
                act.wait_ge(weights.sem, weights.at(1))
                act.activation(s.w[:, 1, :], s.w[:, 1, :], ACT.Exp).then_inc(weights.sem, 1)
                act.wait_ge(chain.sem, chain.at(1))
                act.dma_start(s.table.rearrange("(p b) o -> p (b o)", p=P), s.zero[:]).then_inc(self.sig("act_stored").sem, 16)
                act.wait_ge(self.sig("act_stored").sem, self.sig("act_stored").at(16))
                act.activation(s.mark[:], self.eps[EPS], ACT.Copy).then_inc(cleared.sem, 1)

            @block.vector
            def _(dve):
                n = [0]

                def step(instruction):
                    instruction.then_inc(chain.sem, 1)
                    n[0] += 1
                    dve.wait_ge(chain.sem, chain.at(n[0]))
                step(dve.memset(s.zero[:], 0))
                dve.wait_ge(routed.sem, routed.at(1))
                step(dve.tensor_copy(s.logit[:].rearrange("p t e -> p (t e)"), self.side[:, 0, 0:TT * NE]))
                for t in range(TT):
                    step(dve.max(s.best[:, t, :], s.logit[:, t, :]))
                    step(dve.max_index(s.place[:, t, :], s.best[:, t, :], s.logit[:, t, :]))
                dve.tensor_tensor(s.w[:, 1, :], s.best[:, :, 1], s.best[:, :, 0], ALU.subtract).then_inc(weights.sem, 1)
                step(dve.tensor_copy(s.choice[:].rearrange("p c t -> p t c"), s.place[:, :, 0:2]))
                iota = self.const("iota", b=NE).unsqueeze(1).to_broadcast([P, TOP2 * TT, NE])
                step(dve.tensor_tensor(s.hot[:].rearrange("p c t e -> p (c t) e"),
                                       s.choice[:].rearrange("p c t -> p (c t)").unsqueeze(2).to_broadcast([P, TOP2 * TT, NE]), iota, ALU.is_equal))
                dve.tensor_tensor(s.member[:], s.hot[:, 0, :, :], s.hot[:, 1, :, :], ALU.add).then_inc(member.sem, 1)
                dve.wait_ge(weights.sem, weights.at(2))
                step(dve.tensor_scalar(s.w[:, 0, :], s.w[:, 1, :], 1.0, None, ALU.add))
                step(dve.reciprocal(s.w[:, 0, :], s.w[:, 0, :]))
                step(dve.tensor_tensor(s.w[:, 1, :], s.w[:, 1, :], s.w[:, 0, :], ALU.mult))
                dve.wait_ge(ranked.sem, ranked.at(1))
                total = self.side[:, 2, 0:NE]
                step(dve.tensor_scalar(s.blocks[:], total, 0.0, None, ALU.is_gt))
                for j in range(1, TT):
                    step(dve.scalar_tensor_tensor(s.blocks[:], total, float(j * P), s.blocks[:], ALU.is_gt, ALU.add))
                step(dve.tensor_tensor_scan(s.end[:], self.const("ones", b=NE), s.blocks[:], 0.0, ALU.mult, ALU.add))
                step(dve.tensor_tensor(s.start[:], s.end[:], s.blocks[:], ALU.subtract))
                step(dve.tensor_scalar(s.start[:], s.start[:], float(P), None, ALU.mult))
                step(dve.tensor_tensor(s.where[:], self.side[:, 1, 0:TT * NE].rearrange("p (t e) -> p t e", e=NE),
                                       s.start[:].unsqueeze(1).to_broadcast([P, TT, NE]), ALU.add))
                for c in range(TOP2):
                    step(dve.tensor_tensor(s.hot[:, c, :, :], s.hot[:, c, :, :], s.where[:], ALU.mult))
                step(dve.tensor_reduce(s.slotf[:], s.hot[:].rearrange("p c t e -> p (c t) e"), AX.X, ALU.add))
                step(dve.tensor_copy(s.slot[:], s.slotf[:]))
                step(dve.tensor_tensor(s.before[:], s.end[:].unsqueeze(1).to_broadcast([P, BLOCKS, NE]),
                                       self.const("iota", b=BLOCKS).unsqueeze(2).to_broadcast([P, BLOCKS, NE]), ALU.is_le))
                step(dve.tensor_reduce(s.ownerf[:], s.before[:], AX.X, ALU.add))
                step(dve.tensor_scalar(s.ownerf[:], s.ownerf[:], float(NE - 1), None, ALU.min))
                step(dve.tensor_copy(s.owner[:], s.ownerf[:]))
                dve.memset(s.mark2[:], 0.0).then_inc(picked.sem, 1)
                s.steps = n[0]

            @block.gpsimd
            def _(pool):
                pool.iota(s.token[:], pattern=[[P, TT]], base=0, channel_multiplier=1).then_inc(numbered.sem, 1)
                pool.wait_ge(numbered.sem, numbered.at(1))
                pool.wait_ge(cleared.sem, cleared.at(1))
                pool.wait_ge(picked.sem, picked.at(1))
                for c in range(TOP2):
                    for t in range(TT):
                        j = c * TT + t
                        pool.indirect_dma_start(
                            out=s.table, out_offset=bass.IndirectOffsetOnAxis(ap=s.slot[:, j:j + 1], axis=0),
                            in_=s.token[:, t:t + 1], in_offset=None).then_inc(spread.sem, 16)
                pool.wait_ge(spread.sem, spread.at(16 * TOP2 * TT))
        stored.close(16)
        routed.close(1)
        picked.close(1)
        member.close(1)
        ranked.close(1)
        chain.close(s.steps)
        weights.close(2)
        cleared.close(1)
        spread.close(16 * TOP2 * TT)
        numbered.close(1)
        read.close(16)
        self.sig("act_stored").close(16)

    def run_experts(self, s):
        sig, d = self.sig, self.d
        used, gathered, numbered = sig("moe_used"), sig("slots_gathered"), sig("slots_numbered")
        flipped, ready = sig("x_flipped"), sig("x_ready")
        lit, hidden, turned, moved = sig("pair_silu"), sig("pair_hidden"), sig("hidden_turned"), sig("hidden_moved")
        kept, stored = sig("kept"), sig("act_stored")
        landed = [sig(f"expert_slab_landed{j}") for j in range(MOE_SLOTS)]
        assert MOE_SLABS % MOE_SLOTS == 0
        weights = d["moe"].rearrange("e s p n -> (e s) p n")
        rounded, split = sig("slab_rounded"), sig("slab_split")
        x_rounded, ht_rounded = sig("x_rounded"), sig("hidden_rounded")
        used.close(ROUNDED)

        with self.nc.Block() as block:
            @block.sync
            def _(sp):
                def slab(b, e, i, first=False):
                    if not first:
                        sp.wait_ge(split.sem, split.at(MOE_SLABS * b + i - MOE_SLOTS + 1))
                    sp.dma_start(
                        s.wring[i % MOE_SLOTS], weights[ds(e * MOE_SLABS + i, 1)].rearrange("a p n -> (a p) n")).then_inc(landed[i % MOE_SLOTS].sem, 16)
                e = sp.value_load(s.owner[0:1, 0:1], min_val=0, max_val=NE - 1)
                for i in range(MOE_SLABS):
                    slab(0, e, i, first=i < MOE_SLOTS)
                with sp.Fori(1, BLOCKS) as b:
                    e = sp.value_load(s.owner[0:1, ds(b, 1)], min_val=0, max_val=NE - 1)
                    for i in range(MOE_SLABS):
                        slab(b, e, i)
                for i in range(AHEAD):
                    slab(BLOCKS, 0, i)

            @block.gpsimd
            def _(pool):
                def gather(b):
                    pool.tensor_copy(s.number[:], s.slot_token[:, ds(b, 1)]).then_inc(numbered.sem, 1)
                    pool.wait_ge(numbered.sem, numbered.at(b + 1))
                    pool.nop(nofuse=True)
                    pool.indirect_dma_start(out=s.xs[:], out_offset=None, in_=s.tokens,
                                                        in_offset=bass.IndirectOffsetOnAxis(ap=s.number[:], axis=0)).then_inc(gathered.sem, 16)
                gather(0)
                with pool.Fori(1, BLOCKS + 1) as b:
                    pool.wait_ge(flipped.sem, flipped.at(b))
                    pool.nop(nofuse=True)
                    gather(b)

            @block.tensor
            def _(pe):
                def flip(b):
                    pe.wait_ge(gathered.sem, gathered.at(16 * (b + 1)))
                    for k in range(KT):
                        mm = pe.transpose(self.side[:, 2 + k // 4, (k % 4) * P:(k % 4 + 1) * P], s.xs[:, k * P:(k + 1) * P], self.const("ident"))
                    mm.then_inc(flipped.sem, 1)

                flip(0)
                with pe.Fori(0, BLOCKS) as b:
                    def slab(i):
                        pe.wait_ge(split.sem, split.at(MOE_SLABS * b + i + 1))
                        return s.high[:, i % ROUNDED, :], s.low[:, i % ROUNDED, :]

                    def turn(c):
                        pe.wait_ge(hidden.sem, hidden.at(STEPS * b + c + 1))
                        for kk in range(2):
                            mm = pe.transpose(self.bank[:, 2 + c % 2, kk * P:(kk + 1) * P], s.hidden[:, c % 2, kk * P:(kk + 1) * P],
                                              self.const("ident"))
                        mm.then_inc(turned.sem, 1)

                    def down(c):
                        high, low = slab(MOE_ORDER.index((2, c)))
                        pe.wait_ge(moved.sem, moved.at(STEPS * b + c + 1))
                        if c == 0:
                            pe.wait_ge(kept.sem, kept.at(b))
                        for kk in range(2):
                            for half in range(2):
                                at = slice(kk * D + half * T, kk * D + (half + 1) * T)
                                for n, (x, w) in enumerate(((s.ht, high), (s.ht, low), (s.htlow, high))):
                                    mm = pe.matmul(self.side[:, half, :], x[:, c % 2, kk * P:(kk + 1) * P], w[:, at],
                                                   start=c == 0 and kk == 0 and n == 0, stop=c == STEPS - 1 and kk == 1 and n == 2)
                        mm.then_inc(used.sem, 1)
                        return mm
                    pe.wait_ge(ready.sem, ready.at(b + 1))
                    for c in range(STEPS):
                        if c >= 2:
                            pe.wait_ge(hidden.sem, hidden.at(STEPS * b + c - 1))
                        for part in range(2):
                            high, low = slab(MOE_ORDER.index((part, c)))
                            for k in range(KT):
                                at = slice(k * FC, (k + 1) * FC)
                                for n, (x, w) in enumerate(((s.xt, high), (s.xt, low), (s.xlow, high))):
                                    mm = pe.matmul(self.bank[:, c % 2, part * FC:(part + 1) * FC], x[:, k, :], w[:, at],
                                                   start=k == 0 and n == 0, stop=k == KT - 1 and n == 2)
                            mm.then_inc(used.sem, 1)
                            if c and part == 0:
                                turn(c - 1)
                        if c:
                            down(c - 1)
                    turn(STEPS - 1)
                    flip(b + 1)
                    down(STEPS - 1)

            @block.scalar
            def _(act):
                act.activation(s.mark[:], self.eps[EPS], ACT.Copy).then_inc(used.sem, ROUNDED)

                def round_slab(b, i):
                    act.wait_ge(landed[i % MOE_SLOTS].sem, landed[i % MOE_SLOTS].at(16 * (MOE_SLABS // MOE_SLOTS) * b + 16 * (i // MOE_SLOTS + 1)))
                    act.wait_ge(used.sem, used.at(MOE_SLABS * b + i - ROUNDED + 1))
                    act.activation(s.high[:, i % ROUNDED, :], s.wring[i % MOE_SLOTS], ACT.Copy).then_inc(rounded.sem, 1)
                for i in range(AHEAD):
                    round_slab(0, i)
                with act.Fori(0, BLOCKS) as b:
                    def move(c):
                        act.wait_ge(turned.sem, turned.at(STEPS * b + c + 1))
                        act.activation(s.ht[:, c % 2, :], self.bank[:, 2 + c % 2, 0:FC], ACT.Copy).then_inc(ht_rounded.sem, 1)
                    for c in range(STEPS):
                        if c:
                            round_slab(b, 3 * c + 1)
                            move(c - 1)
                        round_slab(b, 3 * c + 2)
                        act.wait_ge(used.sem, used.at(MOE_SLABS * b + MOE_ORDER.index((1, c)) + 1))
                        act.activation(s.sg[:, c % 2, :], self.bank[:, c % 2, 0:FC], ACT.Silu).then_inc(lit.sem, 1)
                        if c < STEPS - 1:
                            round_slab(b, 3 * c + 3)
                    move(STEPS - 1)
                    for i in range(AHEAD):
                        round_slab(b, MOE_SLABS + i)
                    act.wait_ge(used.sem, used.at(MOE_SLABS * (b + 1)))
                    act.wait_ge(stored.sem, stored.at(16 * b))
                    act.activation(s.ys[:, 0:T], self.side[:, 0, :], ACT.Copy)
                    act.activation(s.ys[:, T:D], self.side[:, 1, :], ACT.Copy).then_inc(kept.sem, 1)
                    act.wait_ge(kept.sem, kept.at(b + 1))
                    act.dma_start(s.slots_y.rearrange("(b p) n -> b p n", p=P)[ds(b, 1)].rearrange("a p n -> (a p) n"), s.ys).then_inc(stored.sem, 16)
                act.wait_ge(stored.sem, stored.at(16 * BLOCKS))

            @block.vector
            def _(dve):
                def turn_in(b):
                    turned_x = self.side[:, 2:4, :].rearrange("p a n -> p (a n)")
                    dve.wait_ge(flipped.sem, flipped.at(b + 1))
                    dve.tensor_copy(s.xt[:].rearrange("p k n -> p (k n)"), turned_x).then_inc(x_rounded.sem, 1)
                    dve.wait_ge(x_rounded.sem, x_rounded.at(b + 1))
                    dve.tensor_tensor(s.xlow[:].rearrange("p k n -> p (k n)"), turned_x,
                                      s.xt[:].rearrange("p k n -> p (k n)").bitcast(F32), ALU.subtract).then_inc(ready.sem, 1)
                def split_slab(b, i):
                    dve.wait_ge(rounded.sem, rounded.at(MOE_SLABS * b + i + 1))
                    dve.tensor_tensor(s.low[:, i % ROUNDED, :], s.wring[i % MOE_SLOTS], s.high[:, i % ROUNDED, :].bitcast(F32), ALU.subtract
                                      ).then_inc(split.sem, 1)
                turn_in(0)
                for i in range(AHEAD):
                    split_slab(0, i)
                with dve.Fori(0, BLOCKS) as b:
                    def move(c):
                        dve.wait_ge(ht_rounded.sem, ht_rounded.at(STEPS * b + c + 1))
                        dve.tensor_tensor(s.htlow[:, c % 2, :], self.bank[:, 2 + c % 2, 0:FC], s.ht[:, c % 2, :].bitcast(F32), ALU.subtract
                                          ).then_inc(moved.sem, 1)
                    for c in range(STEPS):
                        if c:
                            split_slab(b, 3 * c + 1)
                            move(c - 1)
                        split_slab(b, 3 * c + 2)
                        dve.wait_ge(lit.sem, lit.at(STEPS * b + c + 1))
                        dve.tensor_tensor(s.hidden[:, c % 2, :], self.bank[:, c % 2, FC:2 * FC], s.sg[:, c % 2, :], ALU.mult).then_inc(hidden.sem, 1)
                        if c < STEPS - 1:
                            split_slab(b, 3 * c + 3)
                    move(STEPS - 1)
                    split_slab(b, MOE_SLABS)
                    turn_in(b + 1)
                    for i in range(1, AHEAD):
                        split_slab(b, MOE_SLABS + i)
        for signal in (rounded, split):
            signal.close(MOE_SLABS * BLOCKS + AHEAD)
        x_rounded.close(BLOCKS + 1)
        ht_rounded.close(STEPS * BLOCKS)
        n = BLOCKS
        used.close(MOE_SLABS * n)
        gathered.close(16 * (n + 1))
        numbered.close(n + 1)
        flipped.close(n + 1)
        ready.close(n + 1)
        for signal in (lit, hidden, turned, moved):
            signal.close(STEPS * n)
        kept.close(n)
        stored.close(16 * n)
        for j, signal in enumerate(landed):
            signal.close(16 * n * (MOE_SLABS // MOE_SLOTS) + (16 if j < AHEAD else 0))

    def gather_experts(self, s):
        rows = [self.sig(f"row_landed{j}") for j in range(TOP2 * TT)]
        summed, scaled = self.sig("moe_summed"), self.sig("x_scaled")
        with self.nc.Block() as block:
            @block.gpsimd
            def _(pool):
                for t in range(TT):
                    for c in range(TOP2):
                        pool.indirect_dma_start(
                            out=s.rows[:, c * TT + t, :], out_offset=None, in_=s.slots_y,
                            in_offset=bass.IndirectOffsetOnAxis(ap=s.slot[:, c * TT + t:c * TT + t + 1], axis=0)).then_inc(rows[c * TT + t].sem, 16)

            @block.vector
            def _(dve):
                for t in range(TT):
                    dve.wait_ge(rows[t].sem, rows[t].at(16))
                    dve.tensor_scalar(s.y[:, t, :], s.rows[:, t, :], s.w[:, 0, t:t + 1], None, ALU.mult).then_inc(summed.sem, 1)
                    dve.wait_ge(rows[TT + t].sem, rows[TT + t].at(16))
                    dve.wait_ge(summed.sem, summed.at(2 * t + 1))
                    dve.scalar_tensor_tensor(s.y[:, t, :], s.rows[:, TT + t, :], s.w[:, 1, t:t + 1], s.y[:, t, :], ALU.mult, ALU.add).then_inc(summed.sem, 1)

            @block.scalar
            def _(act):
                act.activation(self.x[:], self.x[:], ACT.Copy, scale=ALPHA).then_inc(scaled.sem, 1)
        for signal in rows:
            signal.close(16)
        summed.close(2 * TT)
        scaled.close(1)

    def store(self, tile):
        done = self.sig("out_stored")
        with self.nc.Block() as block:
            @block.sync
            def _(sp):
                sp.dma_start(self.d["out"].rearrange("(t p) n -> p t n", p=P), tile[:]).then_inc(done.sem, 16)
                sp.wait_ge(done.sem, done.at(16))

    def build(self):
        nc, d = self.nc, self.d
        with self.ctx:
            w_mod = d["w_mod"]
            self.stream = [w_mod[0:2 * KT], d["w_in"], w_mod[2 * KT:3 * KT], d["w_conv_o"], w_mod[3 * KT:NMOD]]
            self.stream += [d[n] for n in ("w_attn_o", "w_out", "peer_wq", "ada", "w_in2_0", "w_out2_0", "ffn_up", "ffn_down", "w_in2_1", "w_out2_1")]
            self.slab_used = self.ctx.enter_context(nc.semaphore("slab_used"))
            self.taken = self.ctx.enter_context(nc.semaphore("bank_taken"))
            self.landed = [self.ctx.enter_context(nc.semaphore(f"slab_landed{j}")) for j in range(SLOTS)]
            psum = self.ps("psum", [P, 8, T])
            self.bank, self.side = psum[:, 0:4, :], psum[:, 4:8, :]
            self.x = self.sb("x", [P, KT, T])
            self.h = self.sb("h", [P, KT, T])
            self.squares = self.sb("squares", [P, KT, T])
            self.stat = self.sb("stat", [P, 2, T])
            self.slab_ring = self.sb("slab_ring", [P, SLOTS * HALF_FT * P])
            self.ring = [self.slab_ring[:, j * HALF_FT * P:(j + 1) * HALF_FT * P] for j in range(SLOTS)]
            self.consts = self.sb("consts_sb", [P, NCONST])
            self.vectors = self.sb("vectors_sb", [P, NVEC])
            self.small = self.sb("small_sb", [P, d["small"].shape[1]])
            self.mod = self.sb("mod", [P, NMOD, 2])
            self.mod2 = self.sb("mod2", [P, 2 * NMOD])
            self.cooked = self.sb("cooked", [P, 11, KT])
            self.cond = self.sb("cond_sb", [P, KT, 3])
            self.cond_s = self.sb("cond_s", [P, KT, 3])
            eps = self.sb("eps", [P, 3])
            self.one = eps[:, 2:3]
            self.eps = {EPS: eps[:, 0:1], LN_EPS: eps[:, 1:2]}
            with nc.Block() as block:
                @block.vector
                def _(dve):
                    dve.memset(eps[:, 0:1], EPS)
                    dve.memset(eps[:, 1:2], LN_EPS)
                    dve.memset(eps[:, 2:3], 1.0)

            def column(tile, *at):
                return lambda k: tile[(slice(None), *at, slice(k, k + 1))]

            def vec(name, layer=0):
                return lambda k: self.vectors[:, VECTORS[name][0] + layer * KT + k:VECTORS[name][0] + layer * KT + k + 1]

            def mod(part, who):
                return lambda k: self.mod[:, part * KT + k:part * KT + k + 1, who]

            def mod2(part, layer):
                return lambda k: self.mod2[:, layer * NMOD + part * KT + k:layer * NMOD + part * KT + k + 1]

            with ExitStack() as first:
                class s:
                    pass
                s.v = self.sb("v", [P, ST, KV_HEADS * P], scope=first)
                s.kc = self.sb("kc", [P, KV_HEADS, CTX], scope=first)
                s.qk = self.sb("qk", [P, HEADS + KV_HEADS, T], scope=first)
                s.gates = self.sb("gates", [P, 2 * KT, T], scope=first)
                s.conv = self.sb("conv", [P, KT, T], scope=first)
                with ExitStack() as inner:
                    self.ctx_in = self.sb("ctx_in", [P, KT, CTX], scope=inner)
                    self.hc = self.sb("hc", [P, KT, CTX], scope=inner)
                    s.ab = self.sb("ab", [P, 4, T], scope=inner)
                    s.gpad = self.sb("gpad", [P, 2, T + 2 * PAD], scope=inner)
                    self.load_and_modulate()
                    if self.stop == "mod":
                        return self.dump(self.mod2[:])
                    self.normalise(self.ctx_in, CTX, EPS, [(self.hc, ACT.Identity, column(self.cooked, 1), mod(0, 1))])
                    self.normalise(self.x, T, EPS, [(self.h, ACT.Identity, column(self.cooked, 0), mod(0, 0))])
                    if self.stop == "norm1":
                        return self.dump(self.h[:])
                    self.project(s)
                if self.stop == "conv":
                    return self.dump(s.conv[:])
                self.conv_norm(s, vec("cln_g"), vec("cln_b"))
                self.conv_out(s)
                if self.stop == "conv_out":
                    return self.dump(s.gates[:])
                with ExitStack() as inner:
                    s.sq = self.sb("rot_sq", [P, 2, T], scope=inner)
                    s.root = self.sb("rot_root", [P, 2, T], scope=inner)
                    s.inv = self.sb("rot_inv", [P, 2, T], scope=inner)
                    s.nrm = self.sb("rot_nrm", [P, 2, T], scope=inner)
                    s.cosx = self.sb("rot_cosx", [P, 2, T], scope=inner)
                    s.sinx = self.sb("rot_sinx", [P, 2, T], scope=inner)
                    self.rotate(s)
                if self.stop == "rotate":
                    return self.dump(s.qk[:])
                with ExitStack() as inner:
                    s.o = s.conv
                    s.q = self.sb("q", [P, 2, T], scope=inner)
                    s.p = self.sb("p", [P, 2, SKV], scope=inner)
                    s.pt = self.sb("pt", [P, 2, ST, T], scope=inner)
                    s.top = self.sb("att_top", [P, 2 * TT], scope=inner)
                    s.bias = self.sb("att_bias", [P, 2 * TT], scope=inner)
                    s.total = self.sb("att_total", [P, 2 * TT], scope=inner)
                    s.recip = self.sb("att_recip", [P, 2 * TT], scope=inner)
                    self.attend(s)
                if self.stop == "attend":
                    return self.dump(s.o[:])
                self.mix_out(s)
                if self.stop == "mixed":
                    return self.dump(self.x[:])

            self.normalise(self.x, T, EPS, [(self.h, ACT.Identity, column(self.cooked, 2), mod(3, 0))])
            if self.stop == "h2":
                return self.dump(self.h[:])
            with ExitStack() as peer:
                class s:
                    pass
                s.expert = self.sb("expert", [P, TT, PSEL], U32, scope=peer)
                s.weight = self.sb("weight", [P, PSEL], scope=peer)
                s.hn = self.sb("hn", [P, TT, D], scope=peer)
                s.y = self.h[:].rearrange("p (t a) n -> p t (a n)", t=TT)
                s.sk = self.sb("sk", [P, 2 * PH, T], scope=peer)
                s.two = self.sb("two", [P, 2, PKEYS], scope=peer)
                s.spare = self.sb("spare", [P, NCAND], scope=peer)
                s.val = self.sb("val", [P, 2, PTOP], scope=peer)
                s.pos = self.sb("pos", [P, 2, PTOP], U32, scope=peer)
                s.posf = self.sb("posf", [P, 2, PTOP], scope=peer)
                s.cand = self.sb("cand", [P, 2 * NCAND], scope=peer)
                s.best = self.sb("best", [P, PTOP], scope=peer)
                s.place = self.sb("place", [P, PTOP], U32, scope=peer)
                s.which = self.sb("which", [P, 2, PTOP], U32, scope=peer)
                s.whichf = self.sb("whichf", [P, 2, PTOP], scope=peer)
                s.key = self.sb("key", [P, 2, PTOP], scope=peer)
                s.top = self.sb("top", [P, PH, PTOP], scope=peer)
                s.power = self.sb("power", [P, PH, PTOP], scope=peer)
                s.wsum = self.sb("wsum", [P, PH], scope=peer)
                s.mark = self.sb("mark", [P, 1], scope=peer)
                with ExitStack() as inner:
                    s.keys = self.sb("keys", [P, 2 * PH, PKEYS], scope=inner)
                    s.pq = self.sb("pq", [P, 2, T], scope=inner)
                    self.flip_tiles(self.h, s.hn, True)
                    self.score_keys(s)
                if self.stop == "expert":
                    return self.dump(s.weight[:])
                with ExitStack() as inner:
                    own = self.sb("row", [P, ROWS - 2, D], scope=inner)
                    s.row = [own[:, j, :] for j in range(ROWS - 2)] + [
                        self.squares[:, 0:2, :].rearrange("p a n -> p (a n)"), self.stat[:].rearrange("p a n -> p (a n)")]
                    s.hcur = self.squares[:, 2:4, :].rearrange("p a n -> p (a n)")
                    s.acc = self.squares[:, 4:8, :].rearrange("p (a b) n -> p a (b n)", a=2)
                    s.index = self.sb("index", [P, ROWS], U32, scope=inner)
                    s.dot = self.sb("dot", [P, ROWS], scope=inner)
                    s.act = self.sb("acts", [P, PSEL], scope=inner)
                    s.coef = self.sb("coef", [P, PSEL], scope=inner)
                    s.diag = self.sb("diag", [P, DIAGS, P], scope=inner)
                    s.zero = self.sb("peer_zero", [P, P], scope=inner)
                    self.experts(s)
                if self.stop == "peer":
                    return self.dump(s.y)
                self.flip_tiles(s.y, None, False, after=lambda dve, k, t, at: dve.scalar_tensor_tensor(
                    self.x[:, k, t * P:(t + 1) * P], at, mod(5, 0)(k), self.x[:, k, t * P:(t + 1) * P], ALU.mult, ALU.add))
            self.normalise(self.x, T, EPS, [(self.x, ACT.Copy, vec("final"), None), (self.h, ACT.Identity, column(self.cooked, 3), mod2(0, 0))])
            if self.stop == "x1":
                return self.dump(self.x[:])
            if self.stop == "u0":
                return self.dump(self.h[:])

            for layer in range(2):
                with ExitStack() as scope:
                    class s:
                        pass
                    s.y = self.sb(f"y{layer}", [P, KT, T], scope=scope)
                    s.cch = self.sb(f"cch{layer}", [P, 2 * CONV2, T], scope=scope)
                    s.qk = self.sb(f"gqk{layer}", [P, 4, T], scope=scope)
                    s.v = self.sb(f"gv{layer}", [P, TT, GH, GDV], scope=scope)
                    s.gate = self.sb(f"ggate{layer}", [P, GH, T], scope=scope)
                    s.eb = self.sb(f"eb{layer}", [P, 2, T], scope=scope)
                    s.enb = self.sb(f"enb{layer}", [P, 2, T], scope=scope)
                    s.kout = self.sb(f"kout{layer}", [P, 2, T], scope=scope)
                    with ExitStack() as inner:
                        s.zpad = self.sb(f"zpad{layer}", [P, CONV2, T + 2], scope=inner)
                        s.cb = self.sb(f"cb{layer}", [P, CONV2, T], scope=inner)
                        s.low = self.sb(f"low{layer}", [16, T], scope=inner)
                        s.z = self.sb(f"z{layer}", [P, 2, T], scope=inner)
                        s.b = self.sb(f"b{layer}", [P, 2, T], scope=inner)
                        self.mix_in(s, layer)
                    with ExitStack() as inner:
                        s.kmask = s.cch[:, 0:4, :]
                        s.sq = s.cch[:, 4:8, :]
                        s.a = self.sb(f"a{layer}", [P, GH, T], scope=inner)
                        s.kon = self.squares[:, 0:4, :].rearrange("p (r a) n -> p r a n", r=2)
                        s.state = self.sb(f"state{layer}", [P, 2, NCH, 2 * GDV], scope=inner)
                        s.root = s.kmask
                        s.inv = self.stat[:, 0, :]
                        self.linear_attention(s, layer)
                    self.residual(s.y, lambda i: self.cooked[:, 4 + 4 * layer, ds(i, 1)])
                self.normalise(self.x, T, LN_EPS, [(self.x, ACT.Identity, vec("ln1_g", layer), vec("ln1_b", layer)),
                                                   (self.h, ACT.Identity, column(self.cooked, 5 + 4 * layer), mod2(3, layer))], centre=True)
                if self.stop == f"xa{layer}":
                    return self.dump(self.x[:])
                if self.stop == f"v{layer}":
                    return self.dump(self.h[:])
                gain = lambda i: self.cooked[:, 6 + 4 * layer, ds(i, 1)]
                if layer == 0:
                    with ExitStack() as scope:
                        class s:
                            pass
                        s.hidden = self.sb("hidden", [P, FT, T], scope=scope)
                        with ExitStack() as inner:
                            s.ab = self.sb("ffn_ab", [P, 4, T], scope=inner)
                            s.high = self.sb("ffn_high", [P, 2, D], F32R, scope=inner)
                            s.low = self.sb("ffn_low", [P, 2, D], F32R, scope=inner)
                            s.hhigh = self.sb("ffn_hhigh", [P, KT, T], F32R, scope=inner)
                            s.hlow = self.sb("ffn_hlow", [P, KT, T], F32R, scope=inner)
                            self.dense_up(s)
                        self.dense_down(s, gain)
                    self.normalise(self.x, T, LN_EPS, [(self.x, ACT.Identity, vec("ln2_g"), vec("ln2_b")),
                                                       (self.h, ACT.Identity, column(self.cooked, 7), mod2(0, 1))], centre=True)
                    if self.stop == "x2":
                        return self.dump(self.x[:])
                    if self.stop == "u1":
                        return self.dump(self.h[:])

            with ExitStack() as scope:
                class s:
                    pass
                s.owner = self.sb("moe_owner", [P, BLOCKS], I32, scope=scope)
                s.slot = self.sb("moe_slot", [P, TOP2 * TT], U32, scope=scope)
                s.w = self.sb("moe_w", [P, TOP2, TT], F32, scope=scope)
                s.slot_token = self.sb("moe_slot_token", [P, BLOCKS + 1], U32, scope=scope)
                s.tokens = nc.dram_tensor("token_rows", (T, D), F32, kind="Internal").ap()
                s.table = nc.dram_tensor("slot_table", ((BLOCKS + 1) * P, 1), U32, kind="Internal").ap()
                s.slots_y = nc.dram_tensor("slot_rows", (BLOCKS * P, D), F32, kind="Internal").ap()
                with ExitStack() as inner:
                    s.hn = self.sb("route_hn", [P, TT, D], F32, scope=inner)
                    s.logit = self.sb("route_logit", [P, TT, NE], F32, scope=inner)
                    s.best = self.sb("route_best", [P, TT, NE], F32, scope=inner)
                    s.place = self.sb("route_place", [P, TT, NE], U32, scope=inner)
                    s.choice = self.sb("route_choice", [P, TOP2, TT], F32, scope=inner)
                    s.hot = self.sb("route_hot", [P, TOP2, TT, NE], F32, scope=inner)
                    s.member = self.sb("route_member", [P, TT, NE], F32, scope=inner)
                    s.blocks = self.sb("route_blocks", [P, NE], F32, scope=inner)
                    s.end = self.sb("route_end", [P, NE], F32, scope=inner)
                    s.start = self.sb("route_start", [P, NE], F32, scope=inner)
                    s.where = self.sb("route_where", [P, TT, NE], F32, scope=inner)
                    s.slotf = self.sb("route_slotf", [P, TOP2 * TT], F32, scope=inner)
                    s.before = self.sb("route_before", [P, BLOCKS, NE], F32, scope=inner)
                    s.ownerf = self.sb("route_ownerf", [P, BLOCKS], F32, scope=inner)
                    s.zero = self.sb("route_zero", [P, BLOCKS + 1], U32, scope=inner)
                    s.token = self.sb("route_token", [P, TT], U32, scope=inner)
                    s.mark = self.sb("route_mark", [P, 1], F32, scope=inner)
                    s.mark2 = self.sb("route_mark2", [P, 1], F32, scope=inner)
                    self.flip_tiles(self.h, s.hn, True)
                    self.route(s)
                with ExitStack() as inner:
                    flat = lambda tile: tile.rearrange("p a n -> p (a n)")
                    own = self.sb("exp_wring", [P, MOE_SLOTS - 6, KT * FC], F32, scope=inner)
                    s.wring = [own[:, j, :] for j in range(MOE_SLOTS - 6)]
                    s.wring += [flat(tile[:, 4 * j:4 * j + 4, :]) for tile in (self.h, self.squares) for j in range(2)]
                    s.wring += [self.slab_ring[:, j * KT * FC:(j + 1) * KT * FC] for j in range(2)]
                    s.high = self.sb("exp_high", [P, ROUNDED, KT * FC], F32R, scope=inner)
                    s.low = self.sb("exp_low", [P, ROUNDED, KT * FC], F32R, scope=inner)
                    s.xs = self.sb("exp_xs", [P, D], F32, scope=inner)
                    s.xt = self.sb("exp_xt", [P, KT, P], F32R, scope=inner)
                    s.number = self.sb("exp_number", [P, 1], U32, scope=inner)
                    s.sg = self.sb("exp_sg", [P, 2, FC], F32, scope=inner)
                    s.hidden = self.sb("exp_hidden", [P, 2, FC], F32, scope=inner)
                    s.ht = self.sb("exp_ht", [P, 2, FC], F32R, scope=inner)
                    s.htlow = self.sb("exp_htlow", [P, 2, FC], F32R, scope=inner)
                    s.xlow = self.sb("exp_xlow", [P, KT, P], F32R, scope=inner)
                    s.mark = self.sb("exp_mark", [P, 1], F32, scope=inner)
                    s.ys = flat(self.stat[:])
                    self.run_experts(s)
                s.rows = self.sb("expert_rows", [P, TOP2 * TT, D], scope=scope)
                s.y = self.sb("expert_y", [P, TT, D], scope=scope)
                self.gather_experts(s)
                self.flip_tiles(s.y, None, False, after=lambda dve, k, t, at: dve.scalar_tensor_tensor(
                    self.x[:, k, t * P:(t + 1) * P], at, self.cooked[:, 10, k:k + 1], self.x[:, k, t * P:(t + 1) * P], ALU.mult, ALU.add))
                self.normalise(self.x, T, LN_EPS, [(self.x, ACT.Identity, vec("ln2_g", 1), vec("ln2_b", 1))], centre=True)
                if self.stop == "x3":
                    return self.dump(self.x[:])
                self.flip_tiles(self.x, s.y, True)
                self.store(s.y)

    def dump(self, ap):
        nc = self.nc
        shape = list(ap.shape)
        out = nc.dram_tensor("dump", tuple(shape), F32, kind="ExternalOutput").ap()
        sem = self.ctx.enter_context(nc.semaphore("dumped"))
        with nc.Block() as block:
            @block.sync
            def _(sp):
                sp.dma_start(out, ap).then_inc(sem, 16)
                sp.wait_ge(sem, 16)


def _slabs(w, order=None):
    k, n = w.shape
    w = w.reshape(k // P, P, n // P, P).transpose(2, 1, 0, 3)
    if order is not None:
        w = w[order]
    return np.ascontiguousarray(w).reshape(-1, P, k)


def _tiles(v):
    return np.ascontiguousarray(v.reshape(-1, P).T)


def _channels(x):
    t, c = x.shape
    return np.ascontiguousarray(x.T.reshape(c // P, P, t).transpose(1, 0, 2))


def _consts():
    out = np.zeros((P, NCONST), np.float32)

    def put(name, value):
        at, w = CONSTS[name]
        out[:, at:at + w] = value
    i = np.arange(P)
    put("ident", np.eye(P))
    put("ones", 1.0)
    perm = np.zeros((P, P), np.float32)
    for m in range(P):
        if m % 64 < 32:
            perm[m + 32, m] = -1.0
        else:
            perm[m - 32, m] = 1.0
    put("perm", perm)
    put("causal", (i[:, None] <= i[None, :]) & (i[:, None] // GCH == i[None, :] // GCH))
    put("before", i[:, None] < i[None, :])
    put("pair", (i[:, None] // GDK) == (np.arange(2 * P)[None, :] // P))
    put("iota", i[None, :])
    t = np.arange(T)
    row, col = (t // 64).astype(np.float32), (t % 64).astype(np.float32)
    inv = (np.float32(10000.0) ** (-np.arange(0, 64, 2, dtype=np.float32) / np.float32(64))).astype(np.float32)
    angle = np.where((i < 64)[:, None], row[None, :], col[None, :]) * inv[i % 32][:, None]
    put("cos", np.cos(angle.astype(np.float32)))
    put("sin", np.sin(angle.astype(np.float32)))
    put("carry", np.broadcast_to(t % GCH != 0, (P, T)))
    put("half", (i[:, None] // GCH) == np.arange(2)[None, :])
    return out


def _inputs(a):
    x, ctx = a["x"][0], a["ctx"][0]
    vectors = {
        "b_mod": _tiles(a["b_mod"][0]), "norm1": _tiles(a["norm1_g"][0]), "norm2": _tiles(a["norm2_g"][0]),
        "final": _tiles(a["final_norm_g"]),
        "qk_gain": np.concatenate([np.repeat(_tiles(a["q_norm_g"][0]), HEADS, 1), np.repeat(_tiles(a["k_norm_g"][0]), KV_HEADS, 1)], 1),
        "k_gain": _tiles(a["k_norm_g"][0]),
        "conv_w": a["conv_dw"][0].reshape(TAPS, KT, P).transpose(2, 1, 0).reshape(P, -1),
        "conv_b": _tiles(a["conv_b"][0]), "cln_g": _tiles(a["conv_ln_g"][0]), "cln_b": _tiles(a["conv_ln_b"][0]),
        "ada_b": _tiles(a["ada_b_2"].reshape(-1)), "gk_b": _tiles(a["gk_b_2"].reshape(-1)),
        "ln1_g": _tiles(a["ln1_g_2"].reshape(-1)), "ln1_b": _tiles(a["ln1_b_2"].reshape(-1)),
        "ln2_g": _tiles(a["ln2_g_2"].reshape(-1)), "ln2_b": _tiles(a["ln2_b_2"].reshape(-1)),
        "gla_g": _tiles(a["gla_norm_w_2"].reshape(-1)),
        "conv2_w": a["conv_w_2"].reshape(2, TAPS2, CONV2, P).transpose(3, 0, 2, 1).reshape(P, -1),
    }
    packed = np.concatenate([np.asarray(vectors[n]).reshape(P, VECTORS[n][1]) for n in VECTORS], 1)
    low = a["w_in_2"][:, :, 24 * P:].reshape(2, KT, P, 16).transpose(2, 0, 1, 3).reshape(P, -1)
    router = a["router_w_2"][0].reshape(KT, P, NE).transpose(1, 0, 2).reshape(P, -1)
    gk = np.zeros((P, 2 * 2 * P), np.float32)
    gk[0:16] = a["gk_w2_2"].transpose(1, 0, 2).reshape(16, -1)
    gate = a["ffn_w_gate_2"][0].reshape(D, FT, 1, P)
    up = a["ffn_w_up_2"][0].reshape(D, FT, 1, P)
    down = a["ffn_w_down_2"][0].reshape(2, HALF_FT, P, KT, P).transpose(3, 0, 2, 1, 4)
    parts = [w.reshape(NE, KT, P, STEPS, FC).transpose(3, 0, 2, 1, 4).reshape(STEPS, NE, P, KT * FC)
             for w in (a["moe_w_gate_2"][0], a["moe_w_up_2"][0])]
    parts.append(a["moe_w_down_2"][0].reshape(NE, STEPS, 2, P, D).transpose(1, 0, 3, 2, 4).reshape(STEPS, NE, P, 2 * D))
    moe = np.stack([parts[part][c] for part, c in MOE_ORDER], 1)
    return {
        "x": _channels(x), "ctx": _channels(ctx), "consts": _consts(),
        "cond": np.stack([_tiles(a["c"][0]), _tiles(a["c_ctx"]), _tiles(a["c_2"][0])], 2),
        "vectors": packed, "small": np.concatenate([low, router, gk], 1),
        "w_mod": _slabs(a["w_mod"][0]), "ada": np.concatenate([_slabs(a["ada_w_2"][0]), _slabs(a["ada_w_2"][1])]),
        "w_in": _slabs(a["w_in"][0], W_IN_ORDER), "w_conv_o": _slabs(a["w_conv_o"][0]),
        "w_attn_o": _slabs(a["w_attn_o"][0]), "w_out": _slabs(a["w_out"][0]), "peer_wq": _slabs(a["peer_wq"][0]),
        "w_in2_0": _slabs(a["w_in_2"][0][:, 0:24 * P], W_IN2_ORDER), "w_in2_1": _slabs(a["w_in_2"][1][:, 0:24 * P], W_IN2_ORDER),
        "w_out2_0": _slabs(a["w_out_2"][0]), "w_out2_1": _slabs(a["w_out_2"][1]),
        "ffn_up": _slabs(np.concatenate([gate, up], 2).reshape(D, 2 * FF)),
        "ffn_down": np.ascontiguousarray(down).reshape(2 * KT, P, HALF_FT * P),
        "keys": np.ascontiguousarray(a["peer_keys"][0].reshape(2 * PH, PKEYS, P).transpose(2, 0, 1)),
        "peer_u": a["peer_u"][0], "peer_v": a["peer_v"][0],
        "moe": moe,
    }


def kernel(stop=None, **inputs):
    import concourse.bacc as bacc
    from concourse.bass_utils import run_bass_kernel_spmd as run

    arrays = {f"in_{k}": np.ascontiguousarray(v) for k, v in _inputs({k: np.asarray(v) for k, v in inputs.items()}).items()}
    nc = bacc.Bacc("TRN2", target_bir_lowering=False, num_devices=1)
    d = {k[3:]: nc.dram_tensor(k, v.shape, F32, kind="ExternalInput").ap() for k, v in arrays.items()}
    if stop is None:
        d["out"] = nc.dram_tensor("out", (T, D), F32, kind="ExternalOutput").ap()
    Program(nc, d, stop).build()
    r = run(nc, [arrays], core_ids=[0])
    return r.results[0]["out"].reshape(1, T, D)
```
